# Optimizing a Trainium2 kernel written in Bass

```python
import math
import jax, jax.numpy as jnp
from jax import lax
import numpy as np

D_MODEL = 1024
BATCH = 1
SEQ = 512
DEPTH = 1

N_HEADS = 8
HEAD_DIM = 64
V_DIM = 2 * HEAD_DIM
ROPE_THETA = 10000.0
Q_BLOCK = 128
SSM_GROUP = 16
SSM_GROUPS = 32
SSM_WIDTH = SSM_GROUP * SSM_GROUPS
SSM_STATE = 64
DT_MIN = 0.001
DT_MAX = 0.1
D_FF = 2816
CONV_WIDTH = 3
EPS = 1e-6
QK_COLS = N_HEADS * 2 * HEAD_DIM
V_COLS = N_HEADS * V_DIM
GATE_COLS = 2 * D_MODEL
IN_COLS = 2 * QK_COLS + V_COLS + SSM_WIDTH + GATE_COLS


def rmsnorm(x, g):
    xf = x.astype(jnp.float32)
    xf = xf * lax.rsqrt(jnp.mean(xf * xf, axis=-1, keepdims=True) + EPS)
    return (xf * g.astype(jnp.float32)).astype(x.dtype)

def rope(t, cos, sin):
    tf = t.astype(jnp.float32)
    t1, t2 = jnp.split(tf, 2, axis=-1)
    out = jnp.concatenate([t1 * cos - t2 * sin, t2 * cos + t1 * sin], axis=-1)
    return out.astype(t.dtype)

def diff_attention(q, k, v, lam):
    bsz, seq = q.shape[0], q.shape[1]
    nb = seq // Q_BLOCK
    scale = 1.0 / math.sqrt(HEAD_DIM)
    qb = q.reshape(bsz, nb, Q_BLOCK, N_HEADS, 2, HEAD_DIM).transpose(1, 0, 2, 3, 4, 5)
    kpos = jnp.arange(seq)
    neg = jnp.finfo(jnp.float32).min

    def one_block(args):
        qblk, bi = args
        s = jnp.einsum('bqhcd,bkhcd->bhcqk', qblk, k).astype(jnp.float32) * scale
        qpos = bi * Q_BLOCK + jnp.arange(Q_BLOCK)
        mask = kpos[None, :] <= qpos[:, None]
        s = jnp.where(mask, s, neg)
        p = jax.nn.softmax(s, axis=-1)
        a = p[:, :, 0] - lam * p[:, :, 1]
        return jnp.einsum('bhqk,bkhe->bqhe', a.astype(v.dtype), v)

    o = lax.map(one_block, (qb, jnp.arange(nb)))
    return o.transpose(1, 0, 2, 3, 4).reshape(bsz, seq, N_HEADS, V_DIM)

def _complex_affine_combine(e1, e2):
    a1r, a1i, b1r, b1i = e1
    a2r, a2i, b2r, b2i = e2
    ar = a2r * a1r - a2i * a1i
    ai = a2r * a1i + a2i * a1r
    br = a2r * b1r - a2i * b1i + b2r
    bi = a2r * b1i + a2i * b1r + b2i
    return ar, ai, br, bi

def s5_layer(u, a_re, a_im, log_dt, b_re, b_im, c_re, c_im, d_skip, w_glu, b_glu):
    dtype = u.dtype
    bsz, seq = u.shape[0], u.shape[1]
    f32 = jnp.float32
    uf = u.astype(f32).reshape(bsz, seq, SSM_GROUPS, SSM_GROUP)
    a_re = a_re.astype(f32); a_im = a_im.astype(f32)
    dt = jnp.exp(log_dt.astype(f32))[:, None]
    mag = jnp.exp(a_re * dt)
    lb_re = mag * jnp.cos(a_im * dt)
    lb_im = mag * jnp.sin(a_im * dt)
    nr, ni = lb_re - 1.0, lb_im
    den = a_re * a_re + a_im * a_im
    cr = (nr * a_re + ni * a_im) / den
    ci = (ni * a_re - nr * a_im) / den
    b_re = b_re.astype(f32); b_im = b_im.astype(f32)
    bb_re = cr[..., None] * b_re - ci[..., None] * b_im
    bb_im = cr[..., None] * b_im + ci[..., None] * b_re
    bu_re = jnp.einsum('blgc,gpc->blgp', uf, bb_re)
    bu_im = jnp.einsum('blgc,gpc->blgp', uf, bb_im)
    ar = jnp.broadcast_to(lb_re, bu_re.shape)
    ai = jnp.broadcast_to(lb_im, bu_im.shape)
    _, _, xr, xi = lax.associative_scan(_complex_affine_combine, (ar, ai, bu_re, bu_im), axis=1)
    y = (jnp.einsum('gcp,blgp->blgc', c_re.astype(f32), xr)
         - jnp.einsum('gcp,blgp->blgc', c_im.astype(f32), xi)
         + d_skip.astype(f32) * uf)
    y = y.reshape(bsz, seq, SSM_WIDTH)
    g = jax.nn.gelu(y)
    out = g * jax.nn.sigmoid(g @ w_glu.astype(f32) + b_glu.astype(f32))
    return out.astype(dtype)

def causal_dwconv(u, w, b):
    c = u.shape[-1]
    out = lax.conv_general_dilated(
        u, w.astype(u.dtype)[:, None, :], window_strides=(1,),
        padding=[(CONV_WIDTH - 1, 0)], dimension_numbers=('NWC', 'WIO', 'NWC'),
        feature_group_count=c)
    return out + b.astype(u.dtype)

def first_inputs(seed: int = 0) -> dict:
    key = jax.random.key(seed)
    ks = iter(jax.random.split(key, 40))

    def nrm(shape, scale):
        return jax.random.normal(next(ks), shape, jnp.float32) * scale

    def gain(shape):
        return 1.0 + nrm(shape, 0.02)

    L = DEPTH
    x = nrm((BATCH, SEQ, D_MODEL), 1.0)
    norm1_gain = gain((L, D_MODEL))
    w_in = nrm((L, D_MODEL, IN_COLS), D_MODEL ** -0.5)
    q_norm_gain = gain((L, HEAD_DIM))
    k_norm_gain = gain((L, HEAD_DIM))
    lambda_q1 = nrm((L, HEAD_DIM), 0.1)
    lambda_k1 = nrm((L, HEAD_DIM), 0.1)
    lambda_q2 = nrm((L, HEAD_DIM), 0.1)
    lambda_k2 = nrm((L, HEAD_DIM), 0.1)
    subln_gain = gain((L, V_DIM))
    w_attn_proj = nrm((L, V_COLS, D_MODEL), V_COLS ** -0.5)
    ssm_a_re = -0.5 * (1.0 + nrm((L, SSM_GROUPS, SSM_STATE), 0.02))
    ssm_a_im = (math.pi * jnp.arange(SSM_STATE, dtype=jnp.float32))[None, None, :] + nrm((L, SSM_GROUPS, SSM_STATE), 0.02)
    ssm_log_dt = jax.random.uniform(next(ks), (L, SSM_GROUPS), jnp.float32,
                                    math.log(DT_MIN), math.log(DT_MAX))
    ssm_b_re = nrm((L, SSM_GROUPS, SSM_STATE, SSM_GROUP), (2 * SSM_GROUP) ** -0.5)
    ssm_b_im = nrm((L, SSM_GROUPS, SSM_STATE, SSM_GROUP), (2 * SSM_GROUP) ** -0.5)
    ssm_c_re = nrm((L, SSM_GROUPS, SSM_GROUP, SSM_STATE), (2 * SSM_STATE) ** -0.5)
    ssm_c_im = nrm((L, SSM_GROUPS, SSM_GROUP, SSM_STATE), (2 * SSM_STATE) ** -0.5)
    ssm_d = nrm((L, SSM_GROUPS, SSM_GROUP), 1.0)
    w_glu = nrm((L, SSM_WIDTH, SSM_WIDTH), SSM_WIDTH ** -0.5)
    b_glu = nrm((L, SSM_WIDTH), 0.02)
    w_ssm_proj = nrm((L, SSM_WIDTH, D_MODEL), SSM_WIDTH ** -0.5)
    w_out = nrm((L, D_MODEL, D_MODEL), D_MODEL ** -0.5)
    norm2_gain = gain((L, D_MODEL))
    w_up = nrm((L, D_MODEL, 2 * D_FF), D_MODEL ** -0.5)
    conv_w = nrm((L, CONV_WIDTH, 2 * D_FF), CONV_WIDTH ** -0.5)
    conv_b = nrm((L, 2 * D_FF), 0.02)
    w_down = nrm((L, D_FF, D_MODEL), D_FF ** -0.5)
    return {"x": x, "norm1_gain": norm1_gain, "w_in": w_in,
            "q_norm_gain": q_norm_gain, "k_norm_gain": k_norm_gain,
            "lambda_q1": lambda_q1, "lambda_k1": lambda_k1,
            "lambda_q2": lambda_q2, "lambda_k2": lambda_k2,
            "subln_gain": subln_gain, "w_attn_proj": w_attn_proj,
            "ssm_a_re": ssm_a_re, "ssm_a_im": ssm_a_im, "ssm_log_dt": ssm_log_dt,
            "ssm_b_re": ssm_b_re, "ssm_b_im": ssm_b_im,
            "ssm_c_re": ssm_c_re, "ssm_c_im": ssm_c_im, "ssm_d": ssm_d,
            "w_glu": w_glu, "b_glu": b_glu, "w_ssm_proj": w_ssm_proj,
            "w_out": w_out, "norm2_gain": norm2_gain, "w_up": w_up,
            "conv_w": conv_w, "conv_b": conv_b, "w_down": w_down}

def first_block(x, norm1_gain, w_in, q_norm_gain, k_norm_gain, lambda_q1, lambda_k1,
              lambda_q2, lambda_k2, subln_gain, w_attn_proj, ssm_a_re, ssm_a_im,
              ssm_log_dt, ssm_b_re, ssm_b_im, ssm_c_re, ssm_c_im, ssm_d, w_glu, b_glu,
              w_ssm_proj, w_out, norm2_gain, w_up, conv_w, conv_b, w_down):
    bsz, seq, _ = x.shape
    f32 = jnp.float32
    pos = jnp.arange(seq, dtype=f32)
    inv_freq = 1.0 / (ROPE_THETA ** (jnp.arange(0, HEAD_DIM, 2, dtype=f32) / HEAD_DIM))
    ang = pos[:, None] * inv_freq[None, :]
    cos = jnp.cos(ang)[None, :, None, None, :]
    sin = jnp.sin(ang)[None, :, None, None, :]
    splits = [QK_COLS, 2 * QK_COLS, 2 * QK_COLS + V_COLS, 2 * QK_COLS + V_COLS + SSM_WIDTH]

    h = x
    for i in range(DEPTH):
        lam_init = 0.8 - 0.6 * math.exp(-0.3 * i)
        xn = rmsnorm(h, norm1_gain[i])
        proj = xn @ w_in[i]
        q, k, v, u, gates = jnp.split(proj, splits, axis=-1)
        q = q.reshape(bsz, seq, N_HEADS, 2, HEAD_DIM)
        k = k.reshape(bsz, seq, N_HEADS, 2, HEAD_DIM)
        v = v.reshape(bsz, seq, N_HEADS, V_DIM)
        q = rope(rmsnorm(q, q_norm_gain[i]), cos, sin)
        k = rope(rmsnorm(k, k_norm_gain[i]), cos, sin)
        lam = (jnp.exp(jnp.sum(lambda_q1[i].astype(f32) * lambda_k1[i].astype(f32)))
               - jnp.exp(jnp.sum(lambda_q2[i].astype(f32) * lambda_k2[i].astype(f32)))
               + lam_init)
        o = diff_attention(q, k, v, lam)
        o = rmsnorm(o, subln_gain[i]) * (1.0 - lam_init)
        attn_branch = o.reshape(bsz, seq, V_COLS) @ w_attn_proj[i]
        s = s5_layer(u, ssm_a_re[i], ssm_a_im[i], ssm_log_dt[i], ssm_b_re[i], ssm_b_im[i],
                     ssm_c_re[i], ssm_c_im[i], ssm_d[i], w_glu[i], b_glu[i])
        ssm_branch = s @ w_ssm_proj[i]
        g_attn, g_ssm = jnp.split(jax.nn.sigmoid(gates), 2, axis=-1)
        h = h + (g_attn * attn_branch + g_ssm * ssm_branch) @ w_out[i]
        hn = rmsnorm(h, norm2_gain[i])
        up = causal_dwconv(hn @ w_up[i], conv_w[i], conv_b[i])
        gate, val = jnp.split(up, 2, axis=-1)
        h = h + (jax.nn.silu(gate) * val) @ w_down[i]
    return h


N_ATTN_HEADS = 8
ATTN_WIDTH = N_ATTN_HEADS * HEAD_DIM
DILATED_PATTERNS = ((128, 1), (512, 4), (2048, 16))
SPAN = 128
MAX_DILATION = 16
PAD_MULT = MAX_DILATION * SPAN
LRU_WIDTH = D_MODEL // 2
N_LRU_BLOCKS = 8
LRU_BLOCK = LRU_WIDTH // N_LRU_BLOCKS
CONV_WIDTH_2 = 4
LRU_C = 8.0
MIX_WIDTH = ATTN_WIDTH + LRU_WIDTH
IN_WIDTH = 3 * ATTN_WIDTH + 2 * LRU_WIDTH
D_FF_2 = 4 * D_MODEL
NORM_EPS = 1e-6


def rms_norm(x, g):
    xf = x.astype(jnp.float32)
    y = xf * lax.rsqrt(jnp.mean(xf * xf, axis=-1, keepdims=True) + NORM_EPS)
    return (y * g.astype(jnp.float32)).astype(x.dtype)

def dilated_branch(q, k, v, window, dilation):
    b, sp, h, dh = q.shape
    span = window // dilation
    nb = sp // (dilation * span)

    def split(t):
        return t.reshape(b, nb, span, dilation, h, dh).transpose(0, 3, 4, 1, 2, 5)

    def with_prev(t):
        prev = jnp.pad(t, ((0, 0), (0, 0), (0, 0), (1, 0), (0, 0), (0, 0)))[:, :, :, :-1]
        return jnp.concatenate([prev, t], axis=4)

    qb = split(q)
    kb = with_prev(split(k))
    vb = with_prev(split(v))
    s = jnp.einsum('bchnqd,bchnkd->bchnqk', qb, kb,
                   preferred_element_type=jnp.float32) * (HEAD_DIM ** -0.5)
    qi = jnp.arange(span)[:, None]
    kj = jnp.arange(2 * span)[None, :]
    dist = span + qi - kj
    blk = jnp.arange(nb)[:, None, None]
    valid = (dist >= 0) & (dist <= span) & ((blk > 0) | (kj >= span))
    s = jnp.where(valid, s, -jnp.inf)
    mx = jnp.max(s, axis=-1, keepdims=True)
    p = jnp.exp(s - mx)
    den = jnp.sum(p, axis=-1)
    o = jnp.einsum('bchnqk,bchnkd->bchnqd', p, vb.astype(jnp.float32)) / den[..., None]
    lse = mx[..., 0] + jnp.log(den)
    o = o.transpose(0, 3, 4, 1, 2, 5).reshape(b, sp, h, dh)
    lse = lse.transpose(0, 3, 4, 1, 2).reshape(b, sp, h)
    return o, lse

def dilated_attention(q, k, v):
    b, s, h, dh = q.shape
    sp = -(-s // PAD_MULT) * PAD_MULT
    pad = ((0, 0), (0, sp - s), (0, 0), (0, 0))
    qp, kp, vp = jnp.pad(q, pad), jnp.pad(k, pad), jnp.pad(v, pad)
    outs, lses = [], []
    for window, dilation in DILATED_PATTERNS:
        o, l = dilated_branch(qp, kp, vp, window, dilation)
        outs.append(o)
        lses.append(l)
    wts = jax.nn.softmax(jnp.stack(lses, axis=0), axis=0)
    o = jnp.einsum('pbsh,pbshd->bshd', wts, jnp.stack(outs, axis=0))
    return o[:, :s].astype(q.dtype)

def causal_depthwise_conv(x, w, bias):
    c = x.shape[-1]
    y = lax.conv_general_dilated(x, w[:, None, :].astype(x.dtype), window_strides=(1,),
                                 padding=[(CONV_WIDTH_2 - 1, 0)],
                                 dimension_numbers=('NWC', 'WIO', 'NWC'),
                                 feature_group_count=c)
    return y + bias.astype(x.dtype)

def rg_lru(x, w_r, b_r, w_i, b_i, lam):
    b, s, c = x.shape
    xf = x.astype(jnp.float32)
    xb = xf.reshape(b, s, N_LRU_BLOCKS, LRU_BLOCK)
    r = jax.nn.sigmoid(jnp.einsum('bsnc,ncd->bsnd', xb, w_r.astype(jnp.float32)).reshape(b, s, c)
                       + b_r.astype(jnp.float32))
    i = jax.nn.sigmoid(jnp.einsum('bsnc,ncd->bsnd', xb, w_i.astype(jnp.float32)).reshape(b, s, c)
                       + b_i.astype(jnp.float32))
    log_a = -LRU_C * r * jax.nn.softplus(-lam.astype(jnp.float32))
    a = jnp.exp(log_a)
    u = jnp.sqrt(-jnp.expm1(2.0 * log_a)) * (i * xf)

    def combine(left, right):
        a_l, h_l = left
        a_r, h_r = right
        return a_l * a_r, a_r * h_l + h_r

    _, h = lax.associative_scan(combine, (a, u), axis=1)
    return h.astype(x.dtype)

def hybrid_mixer(h, w_in, conv_w, conv_b, w_r, b_r, w_i, b_i, lam, w_out):
    b, s, _ = h.shape
    z = h @ w_in
    q, k, v, xr, gr = jnp.split(
        z, [ATTN_WIDTH, 2 * ATTN_WIDTH, 3 * ATTN_WIDTH, 3 * ATTN_WIDTH + LRU_WIDTH], axis=-1)
    shp = (b, s, N_ATTN_HEADS, HEAD_DIM)
    attn = dilated_attention(q.reshape(shp), k.reshape(shp), v.reshape(shp)).reshape(b, s, ATTN_WIDTH)
    xr = causal_depthwise_conv(xr, conv_w, conv_b)
    rec = rg_lru(xr, w_r, b_r, w_i, b_i, lam) * jax.nn.gelu(gr)
    return jnp.concatenate([attn.astype(h.dtype), rec.astype(h.dtype)], axis=-1) @ w_out

def squared_relu_mlp(h, w1, w2):
    a = jax.nn.relu(h @ w1)
    return (a * a) @ w2

def second_inputs(seed: int = 0) -> dict:
    key = jax.random.key(seed)
    ks = jax.random.split(key, 20)
    f32 = jnp.float32

    def gain(k):
        return 1.0 + 0.05 * jax.random.normal(k, (DEPTH, D_MODEL), f32)

    u = jax.random.uniform(ks[10], (DEPTH, LRU_WIDTH), f32, 0.9, 0.999)
    a0 = u ** (1.0 / LRU_C)
    lru_lambda = jnp.log(a0) - jnp.log1p(-a0)
    return {
        "x": jax.random.normal(ks[0], (BATCH, SEQ, D_MODEL), f32),
        "mix_norm_pre": gain(ks[1]),
        "mix_norm_post": gain(ks[2]),
        "mlp_norm_pre": gain(ks[3]),
        "mlp_norm_post": gain(ks[4]),
        "w_in": jax.random.normal(ks[5], (DEPTH, D_MODEL, IN_WIDTH), f32) * D_MODEL ** -0.5,
        "conv_w": jax.random.normal(ks[6], (DEPTH, CONV_WIDTH_2, LRU_WIDTH), f32) * CONV_WIDTH_2 ** -0.5,
        "conv_b": 0.01 * jax.random.normal(ks[7], (DEPTH, LRU_WIDTH), f32),
        "w_rgate": jax.random.normal(ks[8], (DEPTH, N_LRU_BLOCKS, LRU_BLOCK, LRU_BLOCK), f32) * LRU_BLOCK ** -0.5,
        "b_rgate": 0.01 * jax.random.normal(ks[9], (DEPTH, LRU_WIDTH), f32),
        "w_igate": jax.random.normal(ks[11], (DEPTH, N_LRU_BLOCKS, LRU_BLOCK, LRU_BLOCK), f32) * LRU_BLOCK ** -0.5,
        "b_igate": 0.01 * jax.random.normal(ks[12], (DEPTH, LRU_WIDTH), f32),
        "lru_lambda": lru_lambda,
        "w_out": jax.random.normal(ks[13], (DEPTH, MIX_WIDTH, D_MODEL), f32) * MIX_WIDTH ** -0.5,
        "w_ff_in": jax.random.normal(ks[14], (DEPTH, D_MODEL, D_FF_2), f32) * D_MODEL ** -0.5,
        "w_ff_out": jax.random.normal(ks[15], (DEPTH, D_FF_2, D_MODEL), f32) * D_FF_2 ** -0.5,
    }

def second_block(x, mix_norm_pre, mix_norm_post, mlp_norm_pre, mlp_norm_post, w_in, conv_w, conv_b,
              w_rgate, b_rgate, w_igate, b_igate, lru_lambda, w_out, w_ff_in, w_ff_out):
    for l in range(DEPTH):
        h = rms_norm(x, mix_norm_pre[l])
        m = hybrid_mixer(h, w_in[l], conv_w[l], conv_b[l], w_rgate[l], b_rgate[l],
                         w_igate[l], b_igate[l], lru_lambda[l], w_out[l])
        x = x + rms_norm(m, mix_norm_post[l])
        h = rms_norm(x, mlp_norm_pre[l])
        x = x + rms_norm(squared_relu_mlp(h, w_ff_in[l], w_ff_out[l]), mlp_norm_post[l])
    return x


def setup_inputs(seed=0):
    out = dict(first_inputs(seed))
    for name, value in second_inputs(seed + 1).items():
        if name != "x":
            out[name + "_2"] = value
    return out


def reference(
    x, norm1_gain, w_in, q_norm_gain, k_norm_gain, lambda_q1, lambda_k1, lambda_q2, lambda_k2,
    subln_gain, w_attn_proj, ssm_a_re, ssm_a_im, ssm_log_dt, ssm_b_re, ssm_b_im, ssm_c_re,
    ssm_c_im, ssm_d, w_glu, b_glu, w_ssm_proj, w_out, norm2_gain, w_up, conv_w, conv_b, w_down,
    mix_norm_pre_2, mix_norm_post_2, mlp_norm_pre_2, mlp_norm_post_2, w_in_2, conv_w_2,
    conv_b_2, w_rgate_2, b_rgate_2, w_igate_2, b_igate_2, lru_lambda_2, w_out_2, w_ff_in_2,
    w_ff_out_2,
):
    x = first_block(
        x, norm1_gain, w_in, q_norm_gain, k_norm_gain, lambda_q1, lambda_k1, lambda_q2,
        lambda_k2, subln_gain, w_attn_proj, ssm_a_re, ssm_a_im, ssm_log_dt, ssm_b_re, ssm_b_im,
        ssm_c_re, ssm_c_im, ssm_d, w_glu, b_glu, w_ssm_proj, w_out, norm2_gain, w_up, conv_w,
        conv_b, w_down,
    )
    return second_block(
        x, mix_norm_pre_2, mix_norm_post_2, mlp_norm_pre_2, mlp_norm_post_2, w_in_2, conv_w_2,
        conv_b_2, w_rgate_2, b_rgate_2, w_igate_2, b_igate_2, lru_lambda_2, w_out_2, w_ff_in_2,
        w_ff_out_2,
    )


_drawn_inputs = setup_inputs


def setup_inputs(seed=0):
    import zlib

    import numpy as np

    out = dict(_drawn_inputs(seed))
    spreads = {}
    factors = {'q_norm_gain': 4.401,
     'k_norm_gain': 5.575,
     'lambda_q1': 64.0,
     'subln_gain': 3.762,
     'ssm_a_re': 64.0,
     'ssm_a_im': 32.296,
     'ssm_log_dt': 34.336,
     'ssm_b_re': 45.744,
     'ssm_b_im': 46.008,
     'ssm_c_re': 45.88,
     'ssm_c_im': 45.752,
     'b_glu': 49.986,
     'norm2_gain': 3.644,
     'conv_b': 3.052,
     'b_rgate_2': 64.0,
     'b_igate_2': 64.0,
     'mix_norm_pre_2': 7.285,
     'mix_norm_post_2': 8.0,
     'mlp_norm_pre_2': 8.0,
     'mlp_norm_post_2': 8.0,
     'conv_b_2': 8.0}
    for name, (base, spread) in spreads.items():
        noise = np.random.default_rng([zlib.crc32(name.encode()), seed]).standard_normal(out[name].shape)
        drawn = base * np.exp(spread * noise) if base else spread * noise
        out[name] = __import__('jax').numpy.asarray(drawn.astype(out[name].dtype))
    for name, factor in factors.items():
        out[name] = (out[name] * factor).astype(out[name].dtype)
    return out
```

```python
from contextlib import ExitStack

import concourse.bass as bass
from concourse import mybir

P = 128
T = 512
D = 1024
KT = D // P
HEADS = 8
QB = T // P
FF1 = 2816 // P
FF2 = 4096 // P
SSM_T = 512 // P
LANE_T = 2048 // P
PAIRS = 4
LRU_T = 512 // P
CHUNK = 8
EPS = 1e-6
LAM_INIT = 0.8 - 0.6
TWO_PI = 6.283185307179586
RING = 4
BIG = 12582912.0

F32 = mybir.dt.float32
F32R = mybir.dt.float32r
BF16 = mybir.dt.bfloat16
ALU = mybir.AluOpType
ACT = mybir.ActivationFunctionType
AX = mybir.AxisListType

C_ID, C_ONES, C_BLK, C_ROT, C_MULT, C_EPS, C_EPS64, C_HPI = 0, 128, 256, 384, 512, 1024, 1025, 1026
N_CONST = 1028
M_ID, M_TRI, M_UNI = 0, 128, 256
N_MASK = 256 + 512
PARAMS = {}
_at = 0
for _n, _w in (("norm1", 8), ("norm2", 8), ("mix_pre", 8), ("mix_post", 8), ("mlp_pre", 8), ("mlp_post", 8),
               ("qg", 1), ("kg", 1), ("subln", 1), ("lam", 4), ("cw", 3 * 44), ("cb", 44), ("b_glu", 4),
               ("ssm_d", 4), ("a_re", 16), ("a_im", 16), ("log_dt", 16), ("cw2", 16), ("cb2", 4),
               ("b_r", 4), ("b_i", 4), ("lru", 4)):
    PARAMS[_n] = (_at, _w)
    _at += _w
N_PARAM = _at


def chunks_of(tiles):
    return [(a, min(a + CHUNK, tiles)) for a in range(0, tiles, CHUNK)]


def ffn_order(tiles):
    n = len(chunks_of(tiles))
    out = [("up", 0)]
    for c in range(1, n):
        out += [("up", c), ("down", c - 1)]
    return out + [("down", n - 1)]


def unit_order():
    u = [("u", t) for t in range(SSM_T)] + [("gate", g) for g in range(16)]
    for h in range(HEADS):
        u += [("k", h), ("q", h), ("v", h)]
    u += [("glu", n) for n in range(2)] + [("ssm", n) for n in range(4)]
    u += [("attn", m) for m in range(KT)] + [("out", m) for m in range(KT)]
    for kind, c in ffn_order(FF1):
        a, b = chunks_of(FF1)[c]
        u += [(s, i) for i in range(a, b) for s in ("fgate", "fval")] if kind == "up" else \
            [("down", c, m) for m in range(KT)]
    u += [("xr", t) for t in range(4)]
    for j in range(PAIRS):
        u += [("k2", j), ("q2", j), ("v2", j), ("gr", j)]
    u += [("out2", m) for m in range(KT)]
    for kind, c in ffn_order(FF2):
        a, b = chunks_of(FF2)[c]
        u += [("ff", i) for i in range(a, b)] if kind == "up" else [("down2", c, m) for m in range(KT)]
    return u


UNITS = unit_order()
UNIT = {name: n for n, name in enumerate(UNITS)}
TILE = {}
TILES_AFTER = []
_o = 0
for _n in UNITS:
    if _n[0] in ("glu", "ssm"):
        TILE[(_n[0], 2 * _n[1])] = _o
        TILE[(_n[0], 2 * _n[1] + 1)] = _o + 1
        _o += 2
    else:
        TILE[_n] = _o
        _o += 1
    TILES_AFTER.append(_o)

SPLIT = {}
_o = 0
for _n, _w in (("norm1", 8), ("g", 4), ("s", 4), ("o", 8), ("mix", 8), ("norm2", 8), ("act", FF1),
               ("norm3", 8), ("rec", 4), ("norm4", 8), ("act2", FF2)):
    SPLIT[_n] = _o
    _o += _w


SRC = {}
_o = 0
for _n, _w in (("norm1", 8), ("s", 4), ("mix", 8), ("norm2", 8), ("act", FF1), ("norm3", 8), ("rec", 4),
               ("norm4", 8), ("act2", FF2)):
    SRC[_n] = _o
    _o += _w

(L_DT, L_Z, L_TH, L_N, L_R, L_MAG, L_TANH, L_S, L_C, L_SIN, L_CM1, L_COS, L_NR, L_NI, L_CR, L_CI,
 L_T1, L_T2, L_T3) = range(19)
LANE_MARK = 3
PI_1, PI_2, PI_3 = 6.28125, 0.0019350051879882812, 3.0199159795074593e-07


def aux_order():
    x, y, s = [("stat", 1), "lam"], [], []
    for t in range(LANE_T):
        x.append(("br", t))
        y.append(("bi", t))
    for h in range(HEADS + 1):
        if h > 0:
            s += [(h - 1, 0), (h - 1, 1)]
        if h < HEADS:
            x.append(("ssq_k", h))
            y.append(("rot_k", h))
        if h > 0:
            s.append((h - 1, 2))
            x.append(("at", h - 1, 0))
            y.append(("at", h - 1, 1))
        if h < HEADS:
            x.append(("ssq_q", h))
            y.append(("rot_q", h))
        if h > 0:
            s.append((h - 1, 3))
            x.append(("at", h - 1, 2))
        if h < HEADS:
            y.append(("vt", h))
        if h > 0:
            x.append(("at", h - 1, 3))
            y.append(("pv", h - 1))
            x.append(("ssq_o", h - 1))
    x += [("stat", 2), ("stat", 3)]
    for t in range(LRU_T):
        x.append(("rg", t))
        y.append(("ig", t))
    for j in range(PAIRS):
        y.append(("vt2", j))
        for i in range(QB):
            s.append(("p", j, i))
        for i in range(QB):
            x += [("at2", j, i, c) for c in range(2)]
        y.append(("pv2", j))
    x += [("stat", n) for n in (4, 5, 6)]
    return x, y, s


XUSE, YUSE, SUSE = ({name: n for n, name in enumerate(names)} for names in aux_order())




def build(nc, weights, x_dram, consts, rope, masks, params, ssm_b, ssm_c, lru_w, out):
    with ExitStack() as ctx:
        def sb(name, shape, dt=F32, scope=ctx):
            return scope.enter_context(nc.sbuf_tensor(name, shape, dt))

        def sem(name):
            return ctx.enter_context(nc.semaphore(name))

        w_raw = sb("w_raw", [P, RING, KT, P])
        w_hi = sb("w_hi", [P, RING, KT, P], F32R)
        w_lo = sb("w_lo", [P, RING, KT, P], F32R)
        x_hi = sb("x_hi", [P, KT, T], F32R)
        x_lo = sb("x_lo", [P, KT, T], F32R)
        cst = sb("cst", [P, N_CONST])
        msk = sb("msk", [P, N_MASK], BF16)
        prm = sb("prm", [P, N_PARAM])
        hid = sb("hid", [P, KT, T])
        nrm = sb("nrm", [P, 2, T])
        sqr = sb("sqr", [P, 2, T])
        rstd = sb("rstd", [P, T])
        lam_t = sb("lam_t", [P, 8])
        lcf = sb("lcf", [P, 8, LRU_T])

        with ExitStack() as first:
            gates = sb("gates", [P, 16, T], scope=first)
            y5 = sb("y5", [P, SSM_T, T], scope=first)
            with ExitStack() as s:
                b_in = sb("b_in", [P, SSM_T, 2, P], scope=s)
                c_in = sb("c_in", [P, 2, LANE_T * 32], scope=s)
                c_out = sb("c_out", [P, 2, LANE_T * 32], scope=s)
                lane = sb("lane", [P, 24, LANE_T], scope=s)
                e_lo = sb("e_lo", [P, 2, LANE_T, 32], scope=s)
                e_hi = sb("e_hi", [P, 2, LANE_T, 16], scope=s)
                rot = sb("rot", [P, 2, 2, T], scope=s)
                rot_m = sb("rot_m", [P, 2, T], scope=s)
                vz = sb("vz", [P, 2, T], scope=s)
                v_m = sb("v_m", [P, 2, T], scope=s)
                xs = sb("xs", [P, 2, 2, T], scope=s)
                x_m = sb("x_m", [P, 2, T], scope=s)
            with ExitStack() as s:
                rtab = sb("rtab", [P, 2, T], scope=s)
                kq_raw = sb("kq_raw", [P, 2, T], scope=s)
                kq_rs = sb("kq_rs", [P, 3, T], scope=s)
                rope_a = sb("rope_a", [P, 2, T], scope=s)
                kk = sb("kk", [P, 2, T], scope=s)
                qq = sb("qq", [P, 2, T], scope=s)
                v_raw = sb("v_raw", [P, T], scope=s)
                vv = sb("vv", [P, 2, QB, P], scope=s)
                pr = sb("pr", [P, 2, 2, T], scope=s)
                pa = sb("pa", [P, 2, T], scope=s)
                pt = sb("pt", [P, QB, T], scope=s)
                soft = sb("soft", [P, 2, 8], scope=s)
            mix_a = sb("mix_a", [P, 4, T], scope=first)
            mix_hi = sb("mix_hi", [P, KT, T], F32R, scope=first)
            mix_lo = sb("mix_lo", [P, KT, T], F32R, scope=first)
        with ExitStack() as s:
            act_hi = sb("act_hi", [P, 2, CHUNK, T], F32R, scope=s)
            act_lo = sb("act_lo", [P, 2, CHUNK, T], F32R, scope=s)
            cnv = sb("cnv", [P, 2, T], scope=s)
            hsrc = sb("hsrc", [P, 2, T], scope=s)
        acc = sb("acc", [P, KT, T])
        with ExitStack() as s:
            mx2_hi = sb("mx2_hi", [P, KT, T], F32R, scope=s)
            mx2_lo = sb("mx2_lo", [P, KT, T], F32R, scope=s)
            xc = sb("xc", [P, LRU_T, T], scope=s)
            tt = sb("tt", [P, LRU_T, T], scope=s)
            lru_b = sb("lru_b", [P, 2, LRU_T, P], scope=s)
            kk2 = sb("kk2", [P, T], scope=s)
            qq2 = sb("qq2", [P, T], scope=s)
            v_raw2 = sb("v_raw2", [P, T], scope=s)
            vv2 = sb("vv2", [P, QB, P], scope=s)
            pr2 = sb("pr2", [P, 2, T], scope=s)
            pt2 = sb("pt2", [P, 2, QB, P], scope=s)
            soft2 = sb("soft2", [P, 2, 8], scope=s)
        ra, ii = acc[:, 0:4], acc[:, 4:8]
        with ExitStack() as s:
            act2_hi = sb("act2_hi", [P, 2, CHUNK, T], F32R, scope=s)
            act2_lo = sb("act2_lo", [P, 2, CHUNK, T], F32R, scope=s)
            rel = sb("rel", [P, T], scope=s)

        msk_raw = gates[:, 0:2, :].rearrange("p a t -> p (a t)")[:, 0:N_MASK]
        kq_sq = [sqr[:, 0], sqr[:, 1], nrm[:, 0]]

        def mix(m):
            return mix_a[:, m] if m < 4 else y5[:, m - 4]

        def psum(name, shape):
            return ctx.enter_context(nc.psum_tensor(name, shape, F32))

        pg = [psum(f"pg{b}", [P, T]) for b in range(2)]
        px, py = psum("px", [P, T]), psum("py", [P, T])
        ps = [psum(f"ps{b}", [P, 2, T]) for b in range(2)]

        w_landed = [sem(f"w_landed{s}") for s in range(RING)]
        hi_done, lo_done = sem("hi_done"), sem("lo_done")
        tile_done = sem("tile_done")
        pg_free = [sem(f"pg_free{b}") for b in range(2)]
        px_full, px_free = sem("px_full"), sem("px_free")
        py_full, py_free = sem("py_full"), sem("py_free")
        ps_full, ps_free = sem("ps_full"), sem("ps_free")
        src_done, xhi_done, xlo_done = sem("src_done"), sem("xhi_done"), sem("xlo_done")
        c_landed, x_landed, p_landed, s_landed, r_landed, l_landed, x2_landed = (
            sem(n) for n in ("c_landed", "x_landed", "p_landed", "s_landed", "r_landed", "l_landed", "x2_landed"))
        stored = sem("stored")
        sq_done, sq_read, rs_done = sem("sq_done"), sem("sq_read"), sem("rs_done")
        lane_act, lane_dve, lam_dve = sem("lane_act"), sem("lane_dve"), sem("lam_dve")
        tab_mul, tab_add, in_add, scanned = sem("tab_mul"), sem("tab_add"), sem("in_add"), sem("scanned")
        out_mul, out_add, y_mm, ya_free = sem("out_mul"), sem("out_add"), sem("y_mm"), sem("ya_free")
        gelu_done = sem("gelu_done")
        act_c, dve_c = sem("act_c"), sem("dve_c")
        roped, maxed, combed, o_sq = sem("roped"), sem("maxed"), sem("combed"), sem("o_sq")
        cnv_act, silu_done, res_done, fin_done = sem("cnv_act"), sem("silu_done"), sem("res_done"), sem("fin_done")
        xc_act, la_done, tt_dve, tt_act, lru_h = (sem(n) for n in ("xc_act", "la_done", "tt_dve", "tt_act", "lru_h"))
        combed2, pv2_part, pv2_hi, rel_done = sem("combed2"), sem("pv2_part"), sem("pv2_hi"), sem("rel_done")

        ident = cst[:, C_ID:C_ID + P]
        ones = cst[:, C_ONES:C_ONES + P]
        block_ones = cst[:, C_BLK:C_BLK + P]
        rotate = cst[:, C_ROT:C_ROT + P]
        mult = cst[:, C_MULT:C_MULT + T]
        ident_b = msk[:, M_ID:M_ID + P]

        def par(name, i=0):
            a, w = PARAMS[name]
            return prm[:, a + i:a + i + 1]

        def pars(name):
            a, w = PARAMS[name]
            return prm[:, a:a + w]

        def cc(i):
            return cst[:, i:i + 1]

        def tiles_after(u):
            return TILES_AFTER[u]

        def evacuated(eng, name):
            eng.wait_ge(pg_free[TILE[name] % 2], TILE[name] // 2 + 1)

        def px_read(eng, name):
            eng.wait_ge(px_free, XUSE[name] + 1)

        def py_read(eng, name):
            eng.wait_ge(py_free, YUSE[name] + 1)

        def ps_read(eng, name):
            eng.wait_ge(ps_free, SUSE[name] + 1)

        block = ctx.enter_context(nc.Block())

        @block.sync
        def _(sp):
            sp.dma_start(hid[:], x_dram).then_inc(x_landed, 16)
            sp.dma_start(cst[:], consts).then_inc(c_landed, 16)
            sp.dma_start(msk_raw, masks).then_inc(c_landed, 16)
            sp.dma_start(prm[:], params).then_inc(p_landed, 16)
            for u in range(RING):
                sp.dma_start(w_raw[:, u], weights[u].rearrange("p (k m) -> p k m", k=KT)).then_inc(w_landed[u], 16)
                if u == 0:
                    sp.dma_start(b_in[:], ssm_b).then_inc(s_landed, 16)
                    sp.dma_start(c_in[:], ssm_c).then_inc(s_landed, 16)
            full = len(UNITS) // RING
            with sp.Fori(1, full) as r:
                for s in range(RING):
                    sp.wait_ge(lo_done, r * RING + (s + 1 - RING))
                    sp.dma_start(w_raw[:, s], weights[r * RING + s].rearrange("p (k m) -> p k m", k=KT))\
                        .then_inc(w_landed[s], 16)
            for u in range(full * RING, len(UNITS)):
                sp.wait_ge(lo_done, u + 1 - RING)
                sp.dma_start(w_raw[:, u % RING], weights[u].rearrange("p (k m) -> p k m", k=KT))\
                    .then_inc(w_landed[u % RING], 16)
            for k in range(KT):
                sp.wait_ge(fin_done, k + 1)
                sp.dma_start(out[:, k], hid[:, k]).then_inc(stored, 16)
            sp.wait_ge(stored, 16 * KT)

        @block.gpsimd
        def _(pool):
            def lo(u, s):
                pool.wait_ge(hi_done, u + 1)
                pool.tensor_tensor(w_lo[:, s], w_raw[:, s], w_hi[:, s].bitcast(F32), ALU.subtract)\
                    .then_inc(lo_done, 1)

            g0 = UNIT[("gate", 0)]
            for u in range(g0 + 3):
                lo(u, u % RING)
            pool.wait_ge(tab_mul, 1)
            pool.tensor_tensor(rot[:, 0, 0], rot[:, 0, 0], rot_m[:, 0], ALU.subtract).then_inc(tab_add, 1)
            pool.tensor_tensor(rot[:, 0, 1], rot[:, 0, 1], rot_m[:, 1], ALU.add).then_inc(tab_add, 1)
            for t in range(LANE_T):
                px_read(pool, ("br", t))
                py_read(pool, ("bi", t))
                pool.tensor_tensor(vz[:, 0], vz[:, 0], v_m[:, 0], ALU.add).then_inc(in_add, 1)
                pool.tensor_tensor(vz[:, 1], vz[:, 1], v_m[:, 1], ALU.subtract).then_inc(in_add, 1)
                lo(g0 + 3 + t, (g0 + 3 + t) % RING)
                if t + 1 < LANE_T:
                    n = (t + 1) % 2
                    pool.wait_ge(tab_mul, t + 2)
                    pool.tensor_tensor(rot[:, n, 0], rot[:, n, 0], rot_m[:, 0], ALU.subtract).then_inc(tab_add, 1)
                    pool.tensor_tensor(rot[:, n, 1], rot[:, n, 1], rot_m[:, 1], ALU.add).then_inc(tab_add, 1)
                pool.wait_ge(out_mul, t + 1)
                pool.tensor_tensor(xs[:, t % 2, 0], xs[:, t % 2, 0], x_m[:, 0], ALU.subtract).then_inc(out_add, 1)
                pool.tensor_tensor(xs[:, t % 2, 1], xs[:, t % 2, 1], x_m[:, 1], ALU.add).then_inc(out_add, 1)
            u = g0 + 3 + LANE_T
            while u % RING:
                lo(u, u % RING)
                u += 1
            full = len(UNITS) // RING
            with pool.Fori(u // RING, full) as r:
                for s in range(RING):
                    lo(r * RING + s, s)
            for u in range(full * RING, len(UNITS)):
                lo(u, u % RING)

        @block.tensor
        def _(pe):
            def tile(u, o, xh, xl, first_split=None, ks=range(KT), off=0):
                s, bank = u % RING, pg[o % 2]
                pe.wait_ge(lo_done, u + 1)
                if o >= 2:
                    pe.wait_ge(pg_free[o % 2], o // 2)
                ks = list(ks)
                for n, k in enumerate(ks):
                    if first_split is not None:
                        pe.wait_ge(xlo_done, first_split + n + 1)
                    wh, wl = w_hi[:, s, off + k, :], w_lo[:, s, off + k, :]
                    pe.matmul(bank[:], wh, xh(k), start=n == 0, stop=False)
                    pe.matmul(bank[:], wh, xl(k), start=False, stop=False)
                    last = pe.matmul(bank[:], wl, xh(k), start=False, stop=n == len(ks) - 1)
                last.then_inc(tile_done, 1)

            def named(name, xh, xl, **kw):
                tile(UNIT[name], TILE[name], xh, xl, **kw)

            def model(t_hi, t_lo):
                return (lambda k: t_hi[:, k]), (lambda k: t_lo[:, k])

            XH, XL = model(x_hi, x_lo)

            def x_use(name):
                if XUSE[name] > 0:
                    pe.wait_ge(px_free, XUSE[name])

            def y_use(name):
                if YUSE[name] > 0:
                    pe.wait_ge(py_free, YUSE[name])

            def s_use(name):
                n = SUSE[name]
                if n >= 2:
                    pe.wait_ge(ps_free, n - 1)
                return ps[n % 2]

            def stat_step(n, k):
                if k == 0:
                    x_use(("stat", n))
                pe.wait_ge(sq_done, KT * (n - 1) + k + 1)
                pe.matmul(px[:], ones, sqr[:, k % 2], start=k == 0, stop=k == KT - 1)\
                    .then_inc(px_full if k == KT - 1 else sq_read, 1)

            pe.wait_ge(c_landed, 32)
            for k in range(KT):
                stat_step(1, k)
            x_use("lam")
            pe.wait_ge(lam_dve, 1)
            pe.matmul(px[:, 0:2], ones, lam_t[:, 0:2], start=True, stop=True).then_inc(px_full, 1)

            for t in range(SSM_T):
                named(("u", t), XH, XL, first_split=SPLIT["norm1"] if t == 0 else None)

            def y_step(t):
                j, bank = t % 4, ps[(t // 4) % 2]
                if j == 0 and t >= 8:
                    pe.wait_ge(ya_free, t // 4 - 1)
                pe.wait_ge(out_add, 2 * t + 2)
                rows = bank[32 * j:32 * j + 32, 0, :]
                pe.matmul(rows, c_out[:, 0, 32 * t:32 * t + 32], xs[:, t % 2, 0], start=True, stop=False)
                pe.matmul(rows, c_out[:, 1, 32 * t:32 * t + 32], xs[:, t % 2, 1], start=False, stop=True)\
                    .then_inc(y_mm, 1)

            for t in range(LANE_T + 1):
                if t < LANE_T:
                    named(("gate", t), XH, XL)
                    j = t % 4
                    if t == 0:
                        pe.wait_ge(s_landed, 32)
                        evacuated(pe, ("u", SSM_T - 1))
                        evacuated(pe, ("u", SSM_T - 2))
                        pe.wait_ge(lane_dve, LANE_MARK)
                    for c, (bank, use, full, name) in enumerate(((px, x_use, px_full, "br"),
                                                                 (py, y_use, py_full, "bi"))):
                        use((name, t))
                        pe.matmul(bank[:], b_in[32 * j:32 * j + 32, t // 4, c, :], hid[32 * j:32 * j + 32, t // 4, :],
                                  start=True, stop=True).then_inc(full, 1)
                if t > 0:
                    y_step(t - 1)

            def scores(h, i):
                bank, w = s_use((h, i)), P * (i + 1)
                if h == 0 and i < 2:
                    pe.wait_ge(ya_free, SSM_T)
                pe.wait_ge(roped, 2 * h + 2)
                for c in range(2):
                    r = slice(64 * c, 64 * c + 64)
                    pe.matmul(bank[:, c, 0:w], qq[r, h % 2, P * i:P * i + P], kk[r, h % 2, 0:w], start=True, stop=False)
                    last = pe.matmul(bank[:, c, P * i:w], ident_b, msk[:, M_TRI:M_TRI + P], start=False, stop=True)
                last.then_inc(ps_full, 1)

            def turn(h, i, bank, full):
                pe.wait_ge(combed, 4 * h + i + 1)
                for j in range(i + 1):
                    last = pe.transpose(bank[:, P * j:P * j + P], pa[:, i % 2, P * j:P * j + P], ident)
                last.then_inc(full, 1)

            for h in range(HEADS + 1):
                g = h - 1
                if h < HEADS:
                    named(("k", h), XH, XL)
                if g >= 0:
                    scores(g, 0)
                    scores(g, 1)
                if h < HEADS:
                    named(("q", h), XH, XL)
                    x_use(("ssq_k", h))
                    evacuated(pe, ("k", h))
                    pe.matmul(px[:], block_ones, kq_sq[0], start=True, stop=True).then_inc(px_full, 1)
                    y_use(("rot_k", h))
                    pe.matmul(py[:], rotate, kq_raw[:, 0], start=True, stop=True).then_inc(py_full, 1)
                if g >= 0:
                    scores(g, 2)
                    x_use(("at", g, 0))
                    turn(g, 0, px, px_full)
                    y_use(("at", g, 1))
                    turn(g, 1, py, py_full)
                if h < HEADS:
                    named(("v", h), XH, XL)
                    x_use(("ssq_q", h))
                    evacuated(pe, ("q", h))
                    pe.matmul(px[:], block_ones, kq_sq[1], start=True, stop=True).then_inc(px_full, 1)
                    y_use(("rot_q", h))
                    pe.matmul(py[:], rotate, kq_raw[:, 1], start=True, stop=True).then_inc(py_full, 1)
                if g >= 0:
                    scores(g, 3)
                    x_use(("at", g, 2))
                    turn(g, 2, px, px_full)
                if h < HEADS:
                    y_use(("vt", h))
                    evacuated(pe, ("v", h))
                    for j in range(QB):
                        last = pe.transpose(py[:, P * j:P * j + P], v_raw[:, P * j:P * j + P], ident)
                    last.then_inc(py_full, 1)
                if g >= 0:
                    x_use(("at", g, 3))
                    turn(g, 3, px, px_full)
                    y_use(("pv", g))
                    px_read(pe, ("at", g, 3))
                    for j in range(QB):
                        last = pe.matmul(py[:, P * j:T], vv[:, g % 2, j, :], pt[:, j, P * j:T],
                                         start=j == 0, stop=j == QB - 1)
                    last.then_inc(py_full, 1)
                    x_use(("ssq_o", g))
                    pe.wait_ge(o_sq, g + 1)
                    pe.matmul(px[:], ones, kq_sq[2], start=True, stop=True).then_inc(px_full, 1)

            for m in range(4):
                tile(UNIT[("glu", m // 2)], TILE[("glu", m)], XH, XL, first_split=SPLIT["g"] if m == 0 else None,
                     ks=range(4), off=4 * (m % 2))
            for m in range(KT):
                tile(UNIT[("ssm", m // 2)], TILE[("ssm", m)], lambda k: x_hi[:, 4 + k], lambda k: x_lo[:, 4 + k],
                     first_split=SPLIT["s"] if m == 0 else None, ks=range(4), off=4 * (m % 2))
            for m in range(KT):
                named(("attn", m), XH, XL, first_split=SPLIT["o"] if m == 0 else None)
            MH, ML = model(mix_hi, mix_lo)
            for m in range(KT):
                named(("out", m), MH, ML, first_split=SPLIT["mix"] if m == 0 else None)
                if m > 0:
                    stat_step(2, m - 1)
            stat_step(2, KT - 1)

            def ffn(tiles, ups, down, split_in, split_act, hi, lo_, stat_n):
                order = ffn_order(tiles)
                for kind, c in order:
                    a, b = chunks_of(tiles)[c]
                    if kind == "up":
                        for i in range(a, b):
                            for n, up in enumerate(ups):
                                named((up, i), XH, XL, first_split=SPLIT[split_in] if i == 0 and n == 0 else None)
                    else:
                        for m in range(KT):
                            named((down, c, m), lambda k: hi[:, c % 2, k], lambda k: lo_[:, c % 2, k], ks=range(b - a),
                                  first_split=SPLIT[split_act] + a if m == 0 else None)
                            if (kind, c) == order[-1] and m > 0:
                                stat_step(stat_n, m - 1)
                stat_step(stat_n, KT - 1)

            ffn(FF1, ("fgate", "fval"), "down", "norm2", "act", act_hi, act_lo, 3)

            def lru_gate(t):
                for c, (bank, use, full, name) in enumerate(((px, x_use, px_full, "rg"), (py, y_use, py_full, "ig"))):
                    use((name, t))
                    if c == 0:
                        evacuated(pe, ("xr", t))
                        pe.wait_ge(l_landed, 16)
                    pe.matmul(bank[:], lru_b[:, c, t], xc[:, t], start=True, stop=True).then_inc(full, 1)

            for t in range(LRU_T):
                named(("xr", t), XH, XL, first_split=SPLIT["norm3"] if t == 0 else None)
                if t > 0:
                    lru_gate(t - 1)

            def scores2(j, i):
                bank, w = s_use(("p", j, i)), P * (i + 1)
                for c in range(2):
                    r = slice(64 * c, 64 * c + 64)
                    pe.matmul(bank[:, c, 0:w], qq2[r, P * i:P * i + P], kk2[r, 0:w], start=True, stop=False)
                    last = pe.matmul(bank[:, c, 0:w], ident_b, msk[:, M_UNI + T - w:M_UNI + T], start=False, stop=True)
                last.then_inc(ps_full, 1)

            def turn2(j, i, c):
                x_use(("at2", j, i, c))
                if c == 0:
                    pe.wait_ge(combed2, 4 * j + i + 1)
                for b in range(i + 1):
                    last = pe.transpose(px[:, P * b:P * b + P], pr2[:, c, P * b:P * b + P], ident)
                last.then_inc(px_full, 1)

            def values2(j, i):
                px_read(pe, ("at2", j, i, 1))
                for c in range(2):
                    r = slice(64 * c, 64 * c + 64)
                    for b in range(i + 1):
                        last = pe.matmul(py[r, P * i:P * i + P], vv2[:, b, r], pt2[:, c, b, :], start=b == 0, stop=b == i)
                if i == QB - 1:
                    last.then_inc(py_full, 1)
                else:
                    last.then_inc(pv2_part, 1)

            for j in range(PAIRS):
                named(("k2", j), XH, XL)
                if j == 0:
                    lru_gate(LRU_T - 1)
                named(("q2", j), XH, XL)
                named(("v2", j), XH, XL)
                evacuated(pe, ("k2", j))
                evacuated(pe, ("q2", j))
                evacuated(pe, ("v2", j))
                scores2(j, 0)
                scores2(j, 1)
                y_use(("vt2", j))
                for b in range(QB):
                    last = pe.transpose(py[:, P * b:P * b + P], v_raw2[:, P * b:P * b + P], ident)
                last.then_inc(py_full, 1)
                named(("gr", j), XH, XL)
                y_use(("pv2", j))
                for i in range(QB):
                    turn2(j, i, 0)
                    turn2(j, i, 1)
                    if i + 2 < QB:
                        scores2(j, i + 2)
                    values2(j, i)

            M2H, M2L = model(mx2_hi, mx2_lo)
            pe.wait_ge(xlo_done, SPLIT["rec"] + 4)
            py_read(pe, ("pv2", PAIRS - 1))
            for m in range(KT):
                named(("out2", m), M2H, M2L)
                if m > 0:
                    stat_step(4, m - 1)
            stat_step(4, KT - 1)
            for k in range(KT):
                stat_step(5, k)
            ffn(FF2, ("ff",), "down2", "norm4", "act2", act2_hi, act2_lo, 6)


        @block.scalar
        def _(act):
            sent = {}

            def put(ins, s):
                ins.then_inc(s, 1)
                sent[s.name] = sent.get(s.name, 0) + 1
                return sent[s.name]

            def hi(u):
                if u >= len(UNITS):
                    return
                s = u % RING
                act.wait_ge(w_landed[s], 16 * (u // RING + 1))
                if u >= RING:
                    act.wait_ge(tile_done, TILES_AFTER[u - RING])
                put(act.activation(w_hi[:, s], w_raw[:, s], ACT.Copy), hi_done)

            def ahead(name):
                hi(UNIT[name] + RING - 1)

            def done(name):
                act.wait_ge(tile_done, TILE[name] + 1)
                return pg[TILE[name] % 2][:]

            def free(ins, name):
                ins.then_inc(pg_free[TILE[name] % 2], 1)

            def px_ready(name):
                act.wait_ge(px_full, XUSE[name] + 1)

            def py_ready(name):
                act.wait_ge(py_full, YUSE[name] + 1)

            def split_hi(group, k, dst, src):
                act.wait_ge(src_done, SRC[group] + k + 1)
                put(act.activation(dst, src, ACT.Copy), xhi_done)

            def square(n, k, src):
                if k >= 2:
                    act.wait_ge(sq_read, (KT - 1) * (n - 1) + k - 1)
                elif n > 1:
                    act.wait_ge(px_full, XUSE[("stat", n - 1)] + 1)
                put(act.activation(sqr[:, k % 2], src, ACT.Square), sq_done)

            def root(n):
                px_ready(("stat", n))
                act.activation(rstd[:], px[:], ACT.Sqrt, bias=cc(C_EPS), scale=1.0 / D).then_inc(px_free, 1)

            for u in range(RING - 1):
                hi(u)
            act.wait_ge(x_landed, 16)
            act.wait_ge(c_landed, 32)
            for k in range(KT):
                square(1, k, hid[:, k])
            root(1)
            for k in range(KT):
                split_hi("norm1", k, x_hi[:, k], nrm[:, k % 2])
            act.wait_ge(p_landed, 16)
            put(act.activation(lane[:, L_DT], pars("log_dt"), ACT.Exp), lane_act)
            px_ready("lam")
            act.activation(lam_t[:, 2:4], px[:, 0:2], ACT.Exp).then_inc(px_free, 1)
            act.wait_ge(lane_dve, 1)
            put(act.activation(lane[:, L_MAG], lane[:, L_Z], ACT.Exp), lane_act)
            put(act.activation(lane[:, L_TANH], lane[:, L_Z], ACT.Tanh, scale=0.5), lane_act)
            put(act.activation(lcf[:, 1], lcf[:, 0], ACT.Exp, scale=-1.0), lane_act)
            ahead(("u", 0))
            act.wait_ge(lane_dve, 2)
            put(act.activation(lane[:, L_S], lane[:, L_R], ACT.Sin, scale=0.5), lane_act)
            put(act.activation(lane[:, L_C], lane[:, L_R], ACT.Sin, scale=0.5, bias=cc(C_HPI)), lane_act)
            for t in range(SSM_T):
                if t > 0:
                    ahead(("u", t))
                a = done(("u", t))
                free(act.activation(hid[:, t], a, ACT.Copy), ("u", t))
            for g in range(16):
                ahead(("gate", g))
                free(act.activation(gates[:, g], done(("gate", g)), ACT.Sigmoid), ("gate", g))
            act.wait_ge(ya_free, SSM_T)
            act.dma_start(rtab[:], rope).then_inc(r_landed, 16)
            for t in range(SSM_T):
                put(act.activation(y5[:, t], y5[:, t], ACT.Gelu_apprx_tanh), gelu_done)

            def exps(use, dst, w, i, sums):
                act.wait_ge(maxed, SUSE[use] + 1)
                for c in range(2):
                    kw = {"accum_out": sums[:, i % 2, 2 + c:3 + c]} if sums is not None else {}
                    negmax = (sums if sums is not None else soft2)[:, i % 2, c:c + 1]
                    ins = act.activation(dst[:, c, 0:w], ps[SUSE[use] % 2][:, c, 0:w], ACT.Exp, bias=negmax, **kw)
                    ins.then_inc(ps_free if c else act_c, 1)

            def exps1(h, i):
                if 4 * h + i >= 2:
                    act.wait_ge(combed, 4 * h + i - 1)
                exps((h, i), pr[:, i % 2], P * (i + 1), i, soft)

            def turned(h, i):
                w = P * (i + 1)
                px_ready(("at", h, i))
                if h > 0 and i == 0:
                    act.wait_ge(py_full, YUSE[("pv", h - 1)] + 1)
                act.activation(pt[:, 0:i + 1, P * i:w], px[:, 0:w].rearrange("p (j q) -> p j q", q=P), ACT.Copy)\
                    .then_inc(px_free, 1)

            def kq_out(h, name, n, gain):
                ahead((name, h))
                a = done((name, h))
                if h > 0:
                    act.wait_ge(roped, 2 * h - 1 + n)
                act.activation(kq_sq[n], a, ACT.Square)
                free(act.activation(kq_raw[:, n], a, ACT.Copy, scale=par(gain)), (name, h))

            def kq_root(h, name, n):
                px_ready((name, h))
                act.activation(kq_rs[:, n], px[:], ACT.Sqrt, bias=cc(C_EPS64 if n else C_EPS),
                               scale=1.0 if n else 1.0 / 64).then_inc(px_free, 1)

            for h in range(HEADS + 1):
                g = h - 1
                if h < HEADS:
                    kq_out(h, "k", 0, "kg")
                if g >= 0:
                    exps1(g, 0)
                    exps1(g, 1)
                if h < HEADS:
                    kq_out(h, "q", 1, "qg")
                    kq_root(h, "ssq_k", 0)
                if g >= 0:
                    exps1(g, 2)
                    turned(g, 0)
                if h < HEADS:
                    ahead(("v", h))
                    a = done(("v", h))
                    if h > 0:
                        act.wait_ge(py_full, YUSE[("vt", h - 1)] + 1)
                    free(act.activation(v_raw[:], a, ACT.Copy), ("v", h))
                    kq_root(h, "ssq_q", 1)
                if g >= 0:
                    exps1(g, 3)
                    turned(g, 2)
                if h < HEADS:
                    py_ready(("vt", h))
                    act.activation(vv[:, h % 2], py[:].rearrange("p (j d) -> p j d", d=P), ACT.Copy).then_inc(py_free, 1)
                if g >= 0:
                    turned(g, 3)
                    py_ready(("pv", g))
                    put(act.activation(kq_sq[2], py[:], ACT.Square), o_sq)
                    px_ready(("ssq_o", g))
                    act.activation(kq_rs[:, 2], px[:], ACT.Sqrt, bias=cc(C_EPS), scale=1.0 / P).then_inc(px_free, 1)

            act.wait_ge(tile_done, TILE[("v", HEADS - 1)] + 1)
            for t in range(SSM_T):
                act.wait_ge(gelu_done, t + 1)
                put(act.activation(x_hi[:, t], y5[:, t], ACT.Copy), xhi_done)
            for m in range(4):
                if m % 2 == 0:
                    ahead(("glu", m // 2))
                a = done(("glu", m))
                if m >= 2:
                    act.wait_ge(src_done, SRC["s"] + m - 1)
                free(act.activation(sqr[:, m % 2], a, ACT.Sigmoid, bias=par("b_glu", m)), ("glu", m))
                if m > 0:
                    split_hi("s", m - 1, x_hi[:, 3 + m], nrm[:, (m - 1) % 2])
            split_hi("s", 3, x_hi[:, 7], nrm[:, 1])
            for n in range(4):
                ahead(("ssm", n))
            act.wait_ge(tile_done, TILE[("ssm", KT - 1)] + 1)
            for h in range(HEADS):
                py_read(act, ("pv", h))
                put(act.activation(x_hi[:, h], hid[:, h], ACT.Copy), xhi_done)
            for m in range(KT):
                ahead(("attn", m))
                if m == 2:
                    act.wait_ge(xlo_done, SPLIT["o"] + KT)
                    act.dma_start(hid[:], x_dram).then_inc(x2_landed, 16)
                split_hi("mix", m, mix_hi[:, m], mix(m))
            for m in range(KT):
                ahead(("out", m))
                evacuated(act, ("out", m))
                square(2, m, hid[:, m])

            def normed(n, group):
                root(n)
                for k in range(KT):
                    split_hi(group, k, x_hi[:, k], nrm[:, k % 2])

            normed(2, "norm2")
            order = ffn_order(FF1)
            for kind, c in order:
                a, b = chunks_of(FF1)[c]
                if kind == "up":
                    if c >= 2:
                        act.wait_ge(tile_done, TILE[("down", c - 2, KT - 1)] + 1)
                    for i in range(a, b):
                        for n, (name, col) in enumerate((("fgate", i), ("fval", FF1 + i))):
                            ahead((name, i))
                            ps_ = done((name, i))
                            if i > 0 and n == 0:
                                act.wait_ge(src_done, SRC["act"] + i)
                            put(act.activation(cnv[:, n], ps_, ACT.Identity, bias=par("cb", col),
                                               scale=par("cw", 88 + col)), cnv_act)
                            if n == 0 and i > a:
                                split_hi("act", i - 1, act_hi[:, c % 2, i - 1 - a], hsrc[:, (i - 1) % 2])
                        evacuated(act, ("fgate", i))
                        put(act.activation(cnv[:, 0], cnv[:, 0], ACT.Silu), silu_done)
                    split_hi("act", b - 1, act_hi[:, c % 2, b - 1 - a], hsrc[:, (b - 1) % 2])
                else:
                    for m in range(KT):
                        ahead(("down", c, m))
                        if (kind, c) == order[-1]:
                            evacuated(act, ("down", c, m))
                            square(3, m, hid[:, m])
            act.dma_start(lru_b[:], lru_w).then_inc(l_landed, 16)
            normed(3, "norm3")

            def lru_gate(t):
                px_ready(("rg", t))
                act.activation(ra[:, t], px[:], ACT.Sigmoid, bias=par("b_r", t)).then_inc(px_free, 1)
                py_ready(("ig", t))
                act.activation(ii[:, t], py[:], ACT.Sigmoid, bias=par("b_i", t)).then_inc(py_free, 1)

            for t in range(LRU_T):
                ahead(("xr", t))
                put(act.activation(xc[:, t], done(("xr", t)), ACT.Identity, bias=par("cb2", t),
                                   scale=par("cw2", 12 + t)), xc_act)
                if t > 0:
                    lru_gate(t - 1)
            for j in range(PAIRS):
                ahead(("k2", j))
                a = done(("k2", j))
                if j > 0:
                    act.wait_ge(ps_full, SUSE[("p", j - 1, QB - 1)] + 1)
                free(act.activation(kk2[:], a, ACT.Copy), ("k2", j))
                if j == 0:
                    lru_gate(LRU_T - 1)
                    for t in range(LRU_T):
                        px_read(act, ("rg", t))
                        put(act.activation(tt[:, t], ra[:, t], ACT.Tanh, scale=lcf[:, 6, t:t + 1]), act_c)
                        put(act.activation(ra[:, t], ra[:, t], ACT.Exp, scale=lcf[:, 7, t:t + 1]), la_done)
                ahead(("q2", j))
                free(act.activation(qq2[:], done(("q2", j)), ACT.Copy, scale=0.125), ("q2", j))
                ahead(("v2", j))
                a = done(("v2", j))
                free(act.activation(v_raw2[:], a, ACT.Copy), ("v2", j))
                if j == 0:
                    for t in range(LRU_T):
                        act.wait_ge(tt_dve, t + 1)
                        put(act.activation(tt[:, t], tt[:, t], ACT.Sqrt), tt_act)

                def exps2(i):
                    if i > 0:
                        act.wait_ge(px_full, XUSE[("at2", j, i - 1, 1)] + 1)
                    exps(("p", j, i), pr2, P * (i + 1), i, None)

                exps2(0)
                py_ready(("vt2", j))
                act.activation(vv2[:], py[:].rearrange("p (b d) -> p b d", d=P), ACT.Copy).then_inc(py_free, 1)
                ahead(("gr", j))
                a = done(("gr", j))
                if j >= 2:
                    act.wait_ge(src_done, SRC["rec"] + j - 1)
                free(act.activation(sqr[:, j % 2], a, ACT.Gelu_apprx_tanh), ("gr", j))
                split_hi("rec", j, mx2_hi[:, 4 + j], nrm[:, j % 2])
                for i in range(QB):
                    for c in range(2):
                        px_ready(("at2", j, i, c))
                        if c == 0 and i > 0:
                            act.wait_ge(pv2_part, (QB - 1) * j + i)
                        act.activation(pt2[:, c, 0:i + 1, :], px[:, 0:P * (i + 1)].rearrange("p (b q) -> p b q", q=P),
                                       ACT.Copy).then_inc(px_free, 1)
                    if i + 1 < QB:
                        exps2(i + 1)
                py_ready(("pv2", j))
                put(act.activation(mx2_hi[:, j], py[:], ACT.Copy), pv2_hi)
            for m in range(KT):
                ahead(("out2", m))
                a = done(("out2", m))
                square(4, m, a)
                free(act.activation(acc[:, m], a, ACT.Copy), ("out2", m))
            root(4)
            for k in range(KT):
                act.wait_ge(res_done, k + 1)
                square(5, k, hid[:, k])
            normed(5, "norm4")
            order = ffn_order(FF2)
            for kind, c in order:
                a, b = chunks_of(FF2)[c]
                if kind == "up":
                    if c >= 2:
                        act.wait_ge(tile_done, TILE[("down2", c - 2, KT - 1)] + 1)
                    for i in range(a, b):
                        ahead(("ff", i))
                        ps_ = done(("ff", i))
                        if i > 0:
                            act.wait_ge(src_done, SRC["act2"] + i)
                        free(act.activation(rel[:], ps_, ACT.Relu), ("ff", i))
                        split_hi("act2", i, act2_hi[:, c % 2, i - a], nrm[:, i % 2])
                else:
                    for m in range(KT):
                        ahead(("down2", c, m))
                        if c == 0:
                            free(act.activation(acc[:, m], done(("down2", c, m)), ACT.Copy), ("down2", c, m))
                        if (kind, c) == order[-1]:
                            evacuated(act, ("down2", c, m))
                            square(6, m, acc[:, m])
            root(6)

        @block.vector
        def _(dve):
            sent = {}

            def put(ins, s):
                ins.then_inc(s, 1)
                sent[s.name] = sent.get(s.name, 0) + 1
                dve.wait_ge(s, sent[s.name])

            def link(ins):
                put(ins, dve_c)

            def done(name):
                dve.wait_ge(tile_done, TILE[name] + 1)
                return pg[TILE[name] % 2][:]

            def free(ins, name):
                ins.then_inc(pg_free[TILE[name] % 2], 1)
                evacuated(dve, name)

            def tt_(out_, a, b, op=ALU.mult):
                return dve.tensor_tensor(out_, a, b, op)

            def stt(out_, a, s, b, op0=ALU.mult, op1=ALU.mult):
                return dve.scalar_tensor_tensor(out_, a, s, b, op0, op1)

            def ts(out_, a, s1, op0, s2=None, op1=ALU.bypass):
                return dve.tensor_scalar(out_, a, s1, s2, op0, op1)

            def split_lo(n, dst, src, hi_):
                dve.wait_ge(xhi_done, n + 1)
                put(tt_(dst, src, hi_.bitcast(F32), ALU.subtract), xlo_done)

            def inverse_root(n):
                px_read(dve, ("stat", n))
                put(dve.reciprocal(rstd[:], rstd[:]), rs_done)

            def normed(n, group, gain):
                inverse_root(n)
                for k in range(KT + 1):
                    if k < KT:
                        put(stt(nrm[:, k % 2], hid[:, k], par(gain, k), rstd[:]), src_done)
                    if k > 0:
                        split_lo(SPLIT[group] + k - 1, x_lo[:, k - 1], nrm[:, (k - 1) % 2], x_hi[:, k - 1])

            dve.wait_ge(c_landed, 32)
            link(dve.tensor_copy(msk[:], msk_raw))
            dve.wait_ge(p_landed, 16)
            lam4 = pars("lam")
            tt_(lam_t[:, 0:1], lam4[:, 0:1], lam4[:, 1:2])
            put(tt_(lam_t[:, 1:2], lam4[:, 2:3], lam4[:, 3:4]), lam_dve)
            normed(1, "norm1", "norm1")

            def L(i):
                return lane[:, i]

            dve.wait_ge(lane_act, 1)
            tt_(L(L_TH), pars("a_im"), L(L_DT))
            link(ts(lcf[:, 0], pars("lru"), -1.0, ALU.mult))
            link(tt_(lcf[:, 0], lcf[:, 0], pars("lru"), ALU.max))
            put(tt_(L(L_Z), pars("a_re"), L(L_DT)), lane_dve)
            dve.wait_ge(lane_dve, 1)
            link(ts(L(L_N), L(L_TH), 1.0 / TWO_PI, ALU.mult, BIG, ALU.add))
            link(ts(L(L_N), L(L_N), BIG, ALU.subtract))
            link(stt(L(L_R), L(L_N), -PI_1, L(L_TH), ALU.mult, ALU.add))
            link(stt(L(L_R), L(L_N), -PI_2, L(L_R), ALU.mult, ALU.add))
            link(stt(L(L_R), L(L_N), -PI_3, L(L_R), ALU.mult, ALU.add))
            put(ts(L(L_R), L(L_R), 3.1415925, ALU.min, -3.1415925, ALU.max), lane_dve)
            px_read(dve, "lam")
            link(tt_(lam_t[:, 4:5], lam_t[:, 3:4], lam_t[:, 2:3], ALU.subtract))
            link(ts(lam_t[:, 5:6], lam_t[:, 4:5], -LAM_INIT, ALU.add))
            link(ts(lam_t[:, 6:7], par("subln"), 1.0 - LAM_INIT, ALU.mult))
            dve.wait_ge(lane_act, 4)
            link(ts(lcf[:, 2], lcf[:, 1], 2.0, ALU.add))
            link(dve.reciprocal(lcf[:, 2], lcf[:, 2]))
            link(tt_(lcf[:, 2], lcf[:, 2], lcf[:, 1]))
            link(tt_(lcf[:, 3], lcf[:, 2], lcf[:, 2]))
            link(ts(lcf[:, 4], lcf[:, 3], 1.0 / 17, ALU.mult))
            for n in (15, 13, 11, 9, 7, 5, 3):
                link(stt(lcf[:, 4], lcf[:, 4], 1.0 / n, lcf[:, 3], ALU.add, ALU.mult))
            link(stt(lcf[:, 4], lcf[:, 4], 1.0, lcf[:, 2], ALU.add, ALU.mult))
            link(ts(lcf[:, 5], pars("lru"), -1.0, ALU.mult, 0.0, ALU.max))
            link(stt(lcf[:, 5], lcf[:, 4], 2.0, lcf[:, 5], ALU.mult, ALU.add))
            link(ts(lcf[:, 6], lcf[:, 5], 8.0, ALU.mult))
            link(ts(lcf[:, 7], lcf[:, 5], -8.0, ALU.mult))
            dve.wait_ge(lane_act, 6)
            link(tt_(L(L_T1), L(L_S), L(L_C)))
            link(ts(L(L_SIN), L(L_T1), 2.0, ALU.mult))
            link(tt_(L(L_T2), L(L_S), L(L_S)))
            link(ts(L(L_CM1), L(L_T2), -2.0, ALU.mult))
            link(ts(L(L_COS), L(L_CM1), 1.0, ALU.add))
            link(stt(L(L_T1), L(L_MAG), 1.0, L(L_TANH), ALU.add, ALU.mult))
            link(tt_(L(L_T1), L(L_T1), L(L_COS)))
            link(tt_(L(L_NR), L(L_T1), L(L_CM1), ALU.add))
            link(tt_(L(L_NI), L(L_MAG), L(L_SIN)))
            link(tt_(L(L_T1), pars("a_re"), pars("a_re")))
            link(tt_(L(L_T2), pars("a_im"), pars("a_im")))
            link(tt_(L(L_T1), L(L_T1), L(L_T2), ALU.add))
            link(dve.reciprocal(L(L_T3), L(L_T1)))
            link(tt_(L(L_T1), L(L_NR), pars("a_re")))
            link(tt_(L(L_T2), L(L_NI), pars("a_im")))
            link(tt_(L(L_T1), L(L_T1), L(L_T2), ALU.add))
            link(tt_(L(L_CR), L(L_T1), L(L_T3)))
            link(tt_(L(L_T1), L(L_NI), pars("a_re")))
            link(tt_(L(L_T2), L(L_NR), pars("a_im")))
            link(tt_(L(L_T1), L(L_T1), L(L_T2), ALU.subtract))
            link(tt_(L(L_CI), L(L_T1), L(L_T3)))
            dve.wait_ge(s_landed, 32)

            def wide(i):
                return lane[:, i, :].rearrange("p (t o) -> p t o", o=1).broadcast_to([P, LANE_T, 32])

            def c3(a):
                return a.rearrange("p (t c) -> p t c", c=32)

            tmp0, tmp1 = nrm[:, 0], nrm[:, 1]
            tt_(c3(c_out[:, 0]), c3(c_in[:, 0]), wide(L_CR))
            link(tt_(c3(tmp0), c3(c_in[:, 1]), wide(L_CI)))
            tt_(c3(c_out[:, 1]), c3(c_in[:, 0]), wide(L_CI))
            link(tt_(c3(tmp1), c3(c_in[:, 1]), wide(L_CR)))
            link(tt_(c_out[:, 0], c_out[:, 0], tmp0, ALU.subtract))
            link(stt(c_out[:, 1], c_out[:, 1], -1.0, tmp1, ALU.mult, ALU.subtract))
            pc, pn = L_COS, L_SIN
            free_rows = [(L_T1, L_T2), (L_NR, L_NI)]
            n_sq = 0
            for table, width in ((e_lo, 32), (e_hi, 16)):
                dve.memset(table[:, 0, :, 0:1], 1.0)
                link(dve.memset(table[:, 1, :, 0:1], 0.0))
                n = 1
                while n < width:
                    def pw(i):
                        return lane[:, i, :].rearrange("p (t o) -> p t o", o=1).broadcast_to([P, LANE_T, n])

                    old_c, old_s = table[:, 0, :, 0:n], table[:, 1, :, 0:n]
                    new_c, new_s = table[:, 0, :, n:2 * n], table[:, 1, :, n:2 * n]
                    t0 = nrm[:, 0, 0:LANE_T * n].rearrange("p (t n) -> p t n", n=n)
                    t1 = nrm[:, 1, 0:LANE_T * n].rearrange("p (t n) -> p t n", n=n)
                    tt_(new_c, old_c, pw(pc))
                    tt_(t0, old_s, pw(pn))
                    tt_(new_s, old_s, pw(pc))
                    tt_(t1, old_c, pw(pn))
                    qc, qn = free_rows[n_sq % 2]
                    tt_(L(qc), L(pc), L(pc))
                    tt_(L(L_T3), L(pn), L(pn))
                    link(tt_(L(qn), L(pc), L(pn)))
                    tt_(new_c, new_c, t0, ALU.subtract)
                    tt_(new_s, new_s, t1, ALU.add)
                    tt_(L(qc), L(qc), L(L_T3), ALU.subtract)
                    link(ts(L(qn), L(qn), 2.0, ALU.mult))
                    pc, pn = qc, qn
                    n_sq += 1
                    n *= 2
            put(dve.tensor_copy(L(L_T3), L(pc)), lane_dve)
            dve.wait_ge(lane_dve, 3)

            def table_step(t):
                lo_ = [e_lo[:, c, t, :].rearrange("p (o b) -> p o b", o=1).broadcast_to([P, 16, 32]) for c in range(2)]
                hi_ = [e_hi[:, c, t, :].rearrange("p (a o) -> p a o", o=1).broadcast_to([P, 16, 32]) for c in range(2)]

                def ab(a):
                    return a.rearrange("p (a b) -> p a b", b=32)

                if t > 0:
                    dve.wait_ge(tab_add, 2 * t)
                tt_(ab(rot[:, t % 2, 0]), hi_[0], lo_[0])
                tt_(ab(rot_m[:, 0]), hi_[1], lo_[1])
                tt_(ab(rot[:, t % 2, 1]), hi_[1], lo_[0])
                put(tt_(ab(rot_m[:, 1]), hi_[0], lo_[1]), tab_mul)

            table_step(0)
            for t in range(LANE_T):
                co, si = rot[:, t % 2, 0], rot[:, t % 2, 1]
                dve.wait_ge(tab_add, 2 * t + 2)
                dve.wait_ge(px_full, XUSE[("br", t)] + 1)
                dve.wait_ge(py_full, YUSE[("bi", t)] + 1)
                tt_(vz[:, 0], px[:], co)
                tt_(vz[:, 1], py[:], co)
                tt_(v_m[:, 0], py[:], si).then_inc(py_free, 1)
                tt_(v_m[:, 1], px[:], si).then_inc(px_free, 1)
                px_read(dve, ("br", t))
                if t + 1 < LANE_T:
                    table_step(t + 1)
                dve.wait_ge(in_add, 2 * t + 2)
                mag = lane[:, L_MAG, t:t + 1].broadcast_to([P, T])
                dve.tensor_tensor_scan(vz[:, 0], mag, vz[:, 0], 0.0, ALU.mult, ALU.add)
                put(dve.tensor_tensor_scan(vz[:, 1], mag, vz[:, 1], 0.0, ALU.mult, ALU.add), scanned)
                if t >= 2:
                    dve.wait_ge(y_mm, t - 1)
                if t >= 1:
                    dve.wait_ge(out_add, 2 * t)
                x2 = xs[:, t % 2]
                tt_(x2[:, 0], vz[:, 0], co)
                tt_(x_m[:, 0], vz[:, 1], si)
                tt_(x2[:, 1], vz[:, 0], si)
                put(tt_(x_m[:, 1], vz[:, 1], co), out_mul)
                if t % 4 == 0 and t > 0:
                    dve.wait_ge(y_mm, t)
                    k = t // 4 - 1
                    put(stt(y5[:, k], hid[:, k], par("ssm_d", k), ps[k % 2][:, 0, :], ALU.mult, ALU.add), ya_free)
            dve.wait_ge(y_mm, LANE_T)
            put(stt(y5[:, 3], hid[:, 3], par("ssm_d", 3), ps[1][:, 0, :], ALU.mult, ALU.add), ya_free)

            def maximum(use, w, i, s):
                dve.wait_ge(ps_full, SUSE[use] + 1)
                put(dve.tensor_reduce(s[:, i % 2, 0:2], ps[SUSE[use] % 2][:, :, 0:w], AX.X, ALU.max, negate=True), maxed)

            def combine(h, i):
                w, s = P * (i + 1), soft[:, i % 2]
                ps_read(dve, (h, i))
                link(dve.reciprocal(s[:, 4:6], s[:, 2:4]))
                link(ts(s[:, 5:6], s[:, 5:6], lam_t[:, 5:6], ALU.mult))
                link(ts(pr[:, i % 2, 1, 0:w], pr[:, i % 2, 1, 0:w], s[:, 5:6], ALU.mult))
                if i >= 2:
                    if i == 2:
                        dve.wait_ge(px_full, XUSE[("at", h, 0)] + 1)
                    else:
                        dve.wait_ge(py_full, YUSE[("at", h, 1)] + 1)
                elif h > 0:
                    dve.wait_ge(px_full, XUSE[("at", h - 1, 2 + i)] + 1)
                put(stt(pa[:, i % 2, 0:w], pr[:, i % 2, 0, 0:w], s[:, 4:5], pr[:, i % 2, 1, 0:w], ALU.mult, ALU.add), combed)

            def rope_step(h, name, n, ssq, rt, dst):
                evacuated(dve, (name, h))
                link(tt_(rope_a[:, 0], kq_raw[:, n], rtab[:, 0]))
                px_read(dve, (ssq, h))
                put(dve.reciprocal(kq_rs[:, n], kq_rs[:, n]), rs_done)
                dve.wait_ge(py_full, YUSE[(rt, h)] + 1)
                tt_(rope_a[:, 1], py[:], rtab[:, 1]).then_inc(py_free, 1)
                py_read(dve, (rt, h))
                link(tt_(rope_a[:, 0], rope_a[:, 0], rope_a[:, 1], ALU.add))
                put(tt_(dst[:, h % 2], rope_a[:, 0], kq_rs[:, n]), roped)

            dve.wait_ge(r_landed, 16)
            for h in range(HEADS + 1):
                g = h - 1
                if g >= 0:
                    maximum((g, 0), P, 0, soft)
                    maximum((g, 1), 2 * P, 1, soft)
                    combine(g, 0)
                    combine(g, 1)
                if h < HEADS:
                    rope_step(h, "k", 0, "ssq_k", "rot_k", kk)
                if g >= 0:
                    maximum((g, 2), 3 * P, 2, soft)
                    dve.wait_ge(py_full, YUSE[("at", g, 1)] + 1)
                    dve.tensor_copy(pt[:, 0:2, P:2 * P], py[:, 0:2 * P].rearrange("p (j q) -> p j q", q=P))\
                        .then_inc(py_free, 1)
                    py_read(dve, ("at", g, 1))
                if h < HEADS:
                    rope_step(h, "q", 1, "ssq_q", "rot_q", qq)
                if g >= 0:
                    combine(g, 2)
                    maximum((g, 3), 4 * P, 3, soft)
                    combine(g, 3)
                    px_read(dve, ("ssq_o", g))
                    link(dve.reciprocal(kq_rs[:, 2], kq_rs[:, 2]))
                    stt(hid[:, g], py[:], lam_t[:, 6:7], kq_rs[:, 2]).then_inc(py_free, 1)
                    py_read(dve, ("pv", g))

            for t in range(SSM_T):
                split_lo(SPLIT["g"] + t, x_lo[:, t], y5[:, t], x_hi[:, t])
            for m in range(5):
                if m < 4:
                    evacuated(dve, ("glu", m))
                    put(tt_(nrm[:, m % 2], y5[:, m], sqr[:, m % 2]), src_done)
                if m > 0:
                    split_lo(SPLIT["s"] + m - 1, x_lo[:, 3 + m], nrm[:, (m - 1) % 2], x_hi[:, 3 + m])
            for m in range(KT):
                free(tt_(mix(m), done(("ssm", m)), gates[:, 8 + m]), ("ssm", m))
            for h in range(HEADS):
                split_lo(SPLIT["o"] + h, x_lo[:, h], hid[:, h], x_hi[:, h])
            for m in range(KT + 1):
                if m < KT:
                    free(tt_(nrm[:, m % 2], done(("attn", m)), gates[:, m]), ("attn", m))
                    evacuated(dve, ("attn", m))
                    put(tt_(mix(m), mix(m), nrm[:, m % 2], ALU.add), src_done)
                if m > 0:
                    split_lo(SPLIT["mix"] + m - 1, mix_lo[:, m - 1], mix(m - 1), mix_hi[:, m - 1])
            dve.wait_ge(x2_landed, 16)
            for m in range(KT):
                free(tt_(hid[:, m], hid[:, m], done(("out", m)), ALU.add), ("out", m))
            normed(2, "norm2", "norm2")

            order = ffn_order(FF1)
            for kind, c in order:
                a, b = chunks_of(FF1)[c]
                if kind == "up":
                    for i in range(a, b):
                        for n, (name, col) in enumerate((("fgate", i), ("fval", FF1 + i))):
                            src = done((name, i))
                            dve.wait_ge(cnv_act, 2 * i + n + 1)
                            link(stt(cnv[:, n, 1:T], src[:, 0:T - 1], par("cw", 44 + col), cnv[:, n, 1:T], ALU.mult, ALU.add))
                            free(stt(cnv[:, n, 2:T], src[:, 0:T - 2], par("cw", col), cnv[:, n, 2:T], ALU.mult, ALU.add),
                                 (name, i))
                            if n == 0 and i > a:
                                split_lo(SPLIT["act"] + i - 1, act_lo[:, c % 2, i - 1 - a], hsrc[:, (i - 1) % 2],
                                         act_hi[:, c % 2, i - 1 - a])
                        evacuated(dve, ("fval", i))
                        dve.wait_ge(silu_done, i + 1)
                        put(tt_(hsrc[:, i % 2], cnv[:, 0], cnv[:, 1]), src_done)
                    split_lo(SPLIT["act"] + b - 1, act_lo[:, c % 2, b - 1 - a], hsrc[:, (b - 1) % 2],
                             act_hi[:, c % 2, b - 1 - a])
                else:
                    for m in range(KT):
                        if c > 0:
                            evacuated(dve, ("down", c - 1, m))
                        free(tt_(hid[:, m], hid[:, m], done(("down", c, m)), ALU.add), ("down", c, m))
            normed(3, "norm3", "mix_pre")

            for t in range(LRU_T):
                src = done(("xr", t))
                dve.wait_ge(xc_act, t + 1)
                for d in (1, 2, 3):
                    ins = stt(xc[:, t, d:T], src[:, 0:T - d], par("cw2", 4 * (3 - d) + t), xc[:, t, d:T], ALU.mult, ALU.add)
                    if d < 3:
                        link(ins)
                    else:
                        free(ins, ("xr", t))
            for t in range(LRU_T):
                dve.wait_ge(la_done, t + 1)
                link(tt_(nrm[:, t % 2], ra[:, t], ra[:, t]))
                put(stt(tt[:, t], nrm[:, t % 2], 1.0, tt[:, t], ALU.add, ALU.mult), tt_dve)
                py_read(dve, ("ig", t))
                link(tt_(ii[:, t], ii[:, t], xc[:, t]))
            for t in range(LRU_T):
                dve.wait_ge(tt_act, t + 1)
                link(tt_(ii[:, t], ii[:, t], tt[:, t]))
                put(dve.tensor_tensor_scan(xc[:, t], ra[:, t], ii[:, t], 0.0, ALU.mult, ALU.add), lru_h)
            for j in range(PAIRS):
                def combine2(i):
                    w, s = P * (i + 1), soft2[:, i % 2]
                    ps_read(dve, ("p", j, i))
                    for c in range(2):
                        link(dve.tensor_tensor_reduce(pr2[:, c, 0:w], pr2[:, c, 0:w], mult[:, T - w:T], 1.0, 0.0,
                                                      ALU.mult, ALU.add, s[:, 2 + c:3 + c]))
                    link(dve.reciprocal(s[:, 4:6], s[:, 2:4]))
                    ts(pr2[:, 0, 0:w], pr2[:, 0, 0:w], s[:, 4:5], ALU.mult)
                    put(ts(pr2[:, 1, 0:w], pr2[:, 1, 0:w], s[:, 5:6], ALU.mult), combed2)

                maximum(("p", j, 0), P, 0, soft2)
                maximum(("p", j, 1), 2 * P, 1, soft2)
                combine2(0)
                evacuated(dve, ("gr", j))
                dve.wait_ge(lru_h, j + 1)
                put(tt_(nrm[:, j % 2], xc[:, j], sqr[:, j % 2]), src_done)
                split_lo(SPLIT["rec"] + j, mx2_lo[:, 4 + j], nrm[:, j % 2], mx2_hi[:, 4 + j])
                maximum(("p", j, 2), 3 * P, 2, soft2)
                combine2(1)
                maximum(("p", j, 3), 4 * P, 3, soft2)
                combine2(2)
                combine2(3)
                dve.wait_ge(pv2_hi, j + 1)
                tt_(mx2_lo[:, j], py[:], mx2_hi[:, j].bitcast(F32), ALU.subtract).then_inc(py_free, 1)
                py_read(dve, ("pv2", j))

            def add_normed(n, gain, signal):
                inverse_root(n)
                for k in range(KT):
                    link(stt(nrm[:, k % 2], acc[:, k], par(gain, k), rstd[:]))
                    put(tt_(hid[:, k], hid[:, k], nrm[:, k % 2], ALU.add), signal)

            add_normed(4, "mix_post", res_done)
            dve.wait_ge(res_done, KT)
            normed(5, "norm4", "mlp_pre")
            order = ffn_order(FF2)
            for kind, c in order:
                a, b = chunks_of(FF2)[c]
                if kind == "up":
                    for i in range(a, b):
                        evacuated(dve, ("ff", i))
                        put(tt_(nrm[:, i % 2], rel[:], rel[:]), src_done)
                        split_lo(SPLIT["act2"] + i, act2_lo[:, c % 2, i - a], nrm[:, i % 2], act2_hi[:, c % 2, i - a])
                elif c > 0:
                    for m in range(KT):
                        evacuated(dve, ("down2", c - 1, m))
                        free(tt_(acc[:, m], acc[:, m], done(("down2", c, m)), ALU.add), ("down2", c, m))
            evacuated(dve, ("down2", len(chunks_of(FF2)) - 1, KT - 1))
            add_normed(6, "mlp_post", fin_done)


def _units(i):
    import numpy as np

    def tiles(w, m):
        return w[:, m * P:(m + 1) * P].reshape(-1, P, P).transpose(1, 0, 2)

    w_in, w_up, w_down = i["w_in"][0], i["w_up"][0], i["w_down"][0]
    w_in2, f_in, f_out = i["w_in_2"][0], i["w_ff_in_2"][0], i["w_ff_out_2"][0]

    def piece(name):
        kind, n = name[0], name[1]
        if kind in ("glu", "ssm"):
            w = i["w_glu"][0] if kind == "glu" else i["w_ssm_proj"][0]
            return np.concatenate([tiles(w, 2 * n), tiles(w, 2 * n + 1)], axis=1)
        if kind in ("down", "down2"):
            a, b = chunks_of(FF1 if kind == "down" else FF2)[n]
            w = (w_down if kind == "down" else f_out)[a * P:b * P]
            return tiles(w, name[2])
        w, m = {"q": (w_in, n), "k": (w_in, 8 + n), "v": (w_in, 16 + n), "u": (w_in, 24 + n), "gate": (w_in, 28 + n),
                "attn": (i["w_attn_proj"][0], n), "out": (i["w_out"][0], n), "fgate": (w_up, n),
                "fval": (w_up, FF1 + n), "q2": (w_in2, n), "k2": (w_in2, 4 + n), "v2": (w_in2, 8 + n),
                "xr": (w_in2, 12 + n), "gr": (w_in2, 16 + n), "out2": (i["w_out_2"][0], n), "ff": (f_in, n)}[kind]
        return tiles(w, m)

    out = np.zeros((len(UNITS), P, KT * P), np.float32)
    for n, name in enumerate(UNITS):
        p = piece(name)
        out[n, :, :p.shape[1] * P] = p.reshape(P, -1)
    return out


def _constants():
    import numpy as np

    c = np.zeros((P, N_CONST), np.float32)
    c[:, C_ID:C_ID + P] = np.eye(P)
    c[:, C_ONES:C_ONES + P] = 1
    c[:64, C_BLK:C_BLK + 64] = 1
    c[64:, C_BLK + 64:C_BLK + 128] = 1
    for b in (0, 64):
        for d in range(32):
            c[b + d + 32, C_ROT + b + d] = -1
            c[b + d, C_ROT + b + d + 32] = 1
    q, k = np.arange(P)[:, None], np.arange(T)[None, :]
    dist = q + (T - P) - k
    count = ((dist >= 0) & (dist <= 128)).astype(int) + ((dist >= 0) & (dist % 4 == 0)) + ((dist >= 0) & (dist % 16 == 0))
    c[:, C_MULT:C_MULT + T] = count
    c[:, C_EPS], c[:, C_EPS64], c[:, C_HPI] = EPS, 64 * EPS, np.pi / 2
    m = np.zeros((P, N_MASK), np.float32)
    m[:, M_ID:M_ID + P] = np.eye(P)
    m[:, M_TRI:M_TRI + P] = np.where(np.arange(P)[None, :] <= q, 0, -1e30)
    m[:, M_UNI:M_UNI + T] = np.where(count > 0, 0, -1e30)
    inv = (1.0 / (10000.0 ** (np.arange(0, 64, 2, dtype=np.float32) / 64))).astype(np.float32)
    ang = (np.arange(T, dtype=np.float32)[None, :] * inv[:, None]).astype(np.float32)
    rope = np.stack([np.tile(np.cos(ang.astype(np.float64)), (4, 1)), np.tile(np.sin(ang.astype(np.float64)), (4, 1))], axis=1)
    return c, m, rope.astype(np.float32)


def _parameters(i):
    import numpy as np

    def cols(a):
        return np.asarray(a).reshape(-1, P).T

    def lanes(a):
        return np.asarray(a).reshape(LANE_T, P).T

    lam = np.zeros((P, 4), np.float32)
    for n, name in enumerate(("lambda_q1", "lambda_k1", "lambda_q2", "lambda_k2")):
        lam[:64, n] = i[name][0]
    parts = {
        "norm1": cols(i["norm1_gain"][0]), "norm2": cols(i["norm2_gain"][0]),
        "mix_pre": cols(i["mix_norm_pre_2"][0]), "mix_post": cols(i["mix_norm_post_2"][0]),
        "mlp_pre": cols(i["mlp_norm_pre_2"][0]), "mlp_post": cols(i["mlp_norm_post_2"][0]),
        "qg": cols(np.tile(i["q_norm_gain"][0], 2)), "kg": cols(np.tile(i["k_norm_gain"][0], 2)),
        "subln": cols(i["subln_gain"][0]), "lam": lam,
        "cw": np.concatenate([cols(i["conv_w"][0][j]) for j in range(3)], axis=1), "cb": cols(i["conv_b"][0]),
        "b_glu": cols(i["b_glu"][0]), "ssm_d": cols(i["ssm_d"][0]),
        "a_re": lanes(i["ssm_a_re"][0]), "a_im": lanes(i["ssm_a_im"][0]),
        "log_dt": lanes(np.repeat(i["ssm_log_dt"][0], 64)),
        "cw2": np.concatenate([cols(i["conv_w_2"][0][j]) for j in range(4)], axis=1), "cb2": cols(i["conv_b_2"][0]),
        "b_r": cols(i["b_rgate_2"][0]), "b_i": cols(i["b_igate_2"][0]), "lru": cols(i["lru_lambda_2"][0]),
    }
    out = np.zeros((P, N_PARAM), np.float32)
    for name, (a, w) in PARAMS.items():
        out[:, a:a + w] = parts[name]
    b = np.zeros((P, SSM_T, 2, P), np.float32)
    c = np.zeros((P, 2, LANE_T, 32), np.float32)
    for n, (bn, cn) in enumerate((("ssm_b_re", "ssm_c_re"), ("ssm_b_im", "ssm_c_im"))):
        for g in range(32):
            h = g % 2
            b[16 * (g % 8):16 * (g % 8) + 16, g // 8, n, 64 * h:64 * h + 64] = i[bn][0][g].T
            c[64 * h:64 * h + 64, n, g // 2, 16 * h:16 * h + 16] = i[cn][0][g].T
    lru = np.zeros((P, 2, LRU_T, P), np.float32)
    for n, name in enumerate(("w_rgate_2", "w_igate_2")):
        for k in range(8):
            h = k % 2
            lru[64 * h:64 * h + 64, n, k // 2, 64 * h:64 * h + 64] = i[name][0][k]
    return out, b, c.reshape(P, 2, LANE_T * 32), lru


def kernel(**inputs):
    import concourse.bacc as _bacc
    import numpy as _np
    from concourse.bass_utils import run_bass_kernel_spmd as _run

    i = {n: _np.asarray(a) for n, a in inputs.items()}
    consts, masks, rope = _constants()
    params, ssm_b, ssm_c, lru = _parameters(i)
    arrays = {
        "weights": _units(i), "x": _np.ascontiguousarray(i["x"][0].T.reshape(KT, P, T).transpose(1, 0, 2)),
        "consts": consts, "rope": rope, "masks": masks, "params": params, "ssm_b": ssm_b, "ssm_c": ssm_c, "lru_w": lru,
    }
    nc = _bacc.Bacc("TRN2", target_bir_lowering=False, num_devices=1)
    args = [nc.dram_tensor(n, a.shape, mybir.dt.from_np(a.dtype), kind="ExternalInput").ap() for n, a in arrays.items()]
    args.append(nc.dram_tensor("out", (P, KT, T), F32, kind="ExternalOutput").ap())
    build(nc, *args)
    got = _run(nc, [arrays], core_ids=[0]).results[0]["out"]
    return got.transpose(1, 0, 2).reshape(D, T).T[None]
```

```python
from contextlib import ExitStack

import concourse.bass as bass
from concourse import mybir

P = 128
T = 512
D = 1024
KT = D // P
HEADS = 8
QB = T // P
FF1 = 2816 // P
FF2 = 4096 // P
SSM_T = 512 // P
LANE_T = 2048 // P
PAIRS = 4
LRU_T = 512 // P
CHUNK = 8
EPS = 1e-6
LAM_INIT = 0.8 - 0.6
TWO_PI = 6.283185307179586
RING = 4
BIG = 12582912.0

F32 = mybir.dt.float32
F32R = mybir.dt.float32r
BF16 = mybir.dt.bfloat16
ALU = mybir.AluOpType
ACT = mybir.ActivationFunctionType
AX = mybir.AxisListType

C_ID, C_ONES, C_BLK, C_ROT, C_MULT, C_EPS, C_EPS64, C_HPI = 0, 128, 256, 384, 512, 1024, 1025, 1026
N_CONST = 1028
M_ID, M_TRI, M_UNI = 0, 128, 256
N_MASK = 256 + 512
PARAMS = {}
_at = 0
for _n, _w in (("norm1", 8), ("norm2", 8), ("mix_pre", 8), ("mix_post", 8), ("mlp_pre", 8), ("mlp_post", 8),
               ("qg", 1), ("kg", 1), ("subln", 1), ("lam", 4), ("cw", 3 * 44), ("cb", 44), ("b_glu", 4),
               ("ssm_d", 4), ("a_re", 16), ("a_im", 16), ("log_dt", 16), ("cw2", 16), ("cb2", 4),
               ("b_r", 4), ("b_i", 4), ("lru", 4)):
    PARAMS[_n] = (_at, _w)
    _at += _w
N_PARAM = _at


def chunks_of(tiles):
    return [(a, min(a + CHUNK, tiles)) for a in range(0, tiles, CHUNK)]


def ffn_order(tiles):
    n = len(chunks_of(tiles))
    out = [("up", 0)]
    for c in range(1, n):
        out += [("up", c), ("down", c - 1)]
    return out + [("down", n - 1)]


def unit_order():
    u = [("u", t) for t in range(SSM_T)] + [("gate", g) for g in range(16)]
    for h in range(HEADS):
        u += [("k", h), ("q", h), ("v", h)]
    u += [("glu", n) for n in range(2)] + [("ssm", n) for n in range(4)]
    u += [("attn", m) for m in range(KT)] + [("out", m) for m in range(KT)]
    for kind, c in ffn_order(FF1):
        a, b = chunks_of(FF1)[c]
        u += [(s, i) for i in range(a, b) for s in ("fgate", "fval")] if kind == "up" else \
            [("down", c, m) for m in range(KT)]
    u += [("xr", t) for t in range(4)]
    for j in range(PAIRS):
        u += [("k2", j), ("q2", j), ("v2", j), ("gr", j)]
    u += [("out2", m) for m in range(KT)]
    for kind, c in ffn_order(FF2):
        a, b = chunks_of(FF2)[c]
        u += [("ff", i) for i in range(a, b)] if kind == "up" else [("down2", c, m) for m in range(KT)]
    return u


UNITS = unit_order()
UNIT = {name: n for n, name in enumerate(UNITS)}
TILE = {}
TILES_AFTER = []
_o = 0
for _n in UNITS:
    if _n[0] in ("glu", "ssm"):
        TILE[(_n[0], 2 * _n[1])] = _o
        TILE[(_n[0], 2 * _n[1] + 1)] = _o + 1
        _o += 2
    else:
        TILE[_n] = _o
        _o += 1
    TILES_AFTER.append(_o)

SPLIT = {}
_o = 0
for _n, _w in (("norm1", 8), ("g", 4), ("s", 4), ("o", 8), ("mix", 8), ("norm2", 8), ("act", FF1),
               ("norm3", 8), ("rec", 4), ("norm4", 8), ("act2", FF2)):
    SPLIT[_n] = _o
    _o += _w


SRC = {}
_o = 0
for _n, _w in (("norm1", 8), ("s", 4), ("mix", 8), ("norm2", 8), ("act", FF1), ("norm3", 8), ("rec", 4),
               ("norm4", 8), ("act2", FF2)):
    SRC[_n] = _o
    _o += _w

(L_DT, L_Z, L_TH, L_N, L_R, L_MAG, L_TANH, L_S, L_C, L_SIN, L_CM1, L_COS, L_NR, L_NI, L_CR, L_CI,
 L_T1, L_T2, L_T3) = range(19)
LANE_MARK = 3
PI_1, PI_2, PI_3 = 6.28125, 0.0019350051879882812, 3.0199159795074593e-07


def aux_order():
    x, y, s = [("stat", 1), "lam"], [], []
    for t in range(LANE_T):
        x.append(("br", t))
        y.append(("bi", t))
    for h in range(HEADS + 2):
        g = h - 1
        if 0 <= g < HEADS:
            x.append(("vt", g))
            s += [("s", g, 0), ("s", g, 1)]
        if h >= 2:
            y.append(("pv", h - 2))
            x.append(("ssq_o", h - 2))
        if 0 <= g < HEADS:
            s += [("t", g, 0), ("t", g, 1)]
        if h < HEADS:
            x.append(("ssq_k", h))
            y.append(("rot_k", h))
        if 0 <= g < HEADS:
            s += [("s", g, 2), ("s", g, 3)]
        if h < HEADS:
            x.append(("ssq_q", h))
            y.append(("rot_q", h))
        if 0 <= g < HEADS:
            s += [("t", g, 2), ("t", g, 3)]
    x += [("stat", 2), ("stat", 3)]
    for t in range(LRU_T):
        x.append(("rg", t))
        y.append(("ig", t))
    for j in range(PAIRS + 1):
        if j > 0:
            for i in (0, 2):
                s += [("p", j - 1, i), ("p", j - 1, i + 1), ("t2", j - 1, i), ("t2", j - 1, i + 1)]
            y.append(("pv2", j - 1))
        if j < PAIRS:
            x.append(("vt2", j))
    x += [("stat", n) for n in (4, 5, 6)]
    return x, y, s


EXPS = {name: n for n, name in enumerate(u for u in aux_order()[2] if u[0] in ("s", "p"))}
XUSE, YUSE, SUSE = ({name: n for n, name in enumerate(names)} for names in aux_order())




def build(nc, weights, x_dram, consts, rope, masks, params, ssm_b, ssm_c, lru_w, out):
    with ExitStack() as ctx:
        def sb(name, shape, dt=F32, scope=ctx):
            return scope.enter_context(nc.sbuf_tensor(name, shape, dt))

        def sem(name):
            return ctx.enter_context(nc.semaphore(name))

        w_raw = sb("w_raw", [P, RING, KT, P])
        w_hi = sb("w_hi", [P, RING, KT, P], F32R)
        w_lo = sb("w_lo", [P, RING, KT, P], F32R)
        x_hi = sb("x_hi", [P, KT, T], F32R)
        x_lo = sb("x_lo", [P, KT, T], F32R)
        cst = sb("cst", [P, N_CONST])
        msk = sb("msk", [P, N_MASK], BF16)
        prm = sb("prm", [P, N_PARAM])
        hid = sb("hid", [P, KT, T])
        nrm = sb("nrm", [P, 2, T])
        sqr = sb("sqr", [P, 2, T])
        rstd = sb("rstd", [P, T])
        lam_t = sb("lam_t", [P, 8])
        lcf = sb("lcf", [P, 8, LRU_T])

        with ExitStack() as first:
            gates = sb("gates", [P, 16, T], scope=first)
            y5 = sb("y5", [P, SSM_T, T], scope=first)
            with ExitStack() as s:
                b_in = sb("b_in", [P, SSM_T, 2, P], scope=s)
                c_out = sb("c_out", [P, 2, LANE_T * 32], scope=s)
                lane = sb("lane", [P, 24, LANE_T], scope=s)
                e_lo = sb("e_lo", [P, 2, LANE_T, 32], scope=s)
                e_hi = sb("e_hi", [P, 2, LANE_T, 16], scope=s)
                rot = sb("rot", [P, 2, 2, T], scope=s)
                rot_m = sb("rot_m", [P, 2, T], scope=s)
                vz = sb("vz", [P, 2, T], scope=s)
                v_m = sb("v_m", [P, 2, T], scope=s)
                xs = sb("xs", [P, 2, 4, T], scope=s)
            with ExitStack() as s:
                rtab = sb("rtab", [P, 2, T], scope=s)
                kq_raw = sb("kq_raw", [P, 2, T], scope=s)
                kq_rs = sb("kq_rs", [P, 3, T], scope=s)
                rope_a = sb("rope_a", [P, 2, T], scope=s)
                kk = sb("kk", [P, 2, T], scope=s)
                qq = sb("qq", [P, 2, T], scope=s)
                v_raw = sb("v_raw", [P, T], scope=s)
                vv = sb("vv", [P, 2, QB, P], scope=s)
                pr = sb("pr", [P, 2, 2, T], scope=s)
                pa = sb("pa", [P, 2, T], scope=s)
                pt = sb("pt", [P, QB, T], scope=s)
                soft = sb("soft", [P, 2, 8], scope=s)
            mix_a = sb("mix_a", [P, 4, T], scope=first)
            mix_hi = sb("mix_hi", [P, KT, T], F32R, scope=first)
            mix_lo = sb("mix_lo", [P, KT, T], F32R, scope=first)
        with ExitStack() as s:
            act_hi = sb("act_hi", [P, 2, CHUNK, T], F32R, scope=s)
            act_lo = sb("act_lo", [P, 2, CHUNK, T], F32R, scope=s)
            cnv = sb("cnv", [P, 2, T], scope=s)
            hsrc = sb("hsrc", [P, 2, T], scope=s)
            cu = sb("cu", [P, 2, T], scope=s)
        acc = sb("acc", [P, KT, T])
        with ExitStack() as s:
            mx2_hi = sb("mx2_hi", [P, KT, T], F32R, scope=s)
            mx2_lo = sb("mx2_lo", [P, KT, T], F32R, scope=s)
            xc = sb("xc", [P, LRU_T, T], scope=s)
            tt = sb("tt", [P, LRU_T, T], scope=s)
            lru_b = sb("lru_b", [P, 2, LRU_T, P], scope=s)
            kk2 = sb("kk2", [P, 2, T], scope=s)
            qq2 = sb("qq2", [P, 2, T], scope=s)
            v_raw2 = sb("v_raw2", [P, T], scope=s)
            vv2 = sb("vv2", [P, QB, P], scope=s)
            soft2 = sb("soft2", [P, 2, 8], scope=s)
        ra, ii = acc[:, 0:4], acc[:, 4:8]
        pr2 = acc[:, 0:4].rearrange("p (n c) t -> p n c t", c=2)
        pt2 = acc[:, 4:8].rearrange("p (n c) (b q) -> p n c b q", c=2, q=P)
        with ExitStack() as s:
            act2_hi = sb("act2_hi", [P, 2, CHUNK, T], F32R, scope=s)
            act2_lo = sb("act2_lo", [P, 2, CHUNK, T], F32R, scope=s)
            rel = sb("rel", [P, T], scope=s)
            rstd_sq = sb("rstd_sq", [P, T], scope=s)
            nrm_t = sb("nrm_t", [P, T], scope=s)

        c_in = gates[:, 2:4, :]
        msk_raw = gates[:, 0:2, :].rearrange("p a t -> p (a t)")[:, 0:N_MASK]
        kq_sq = [sqr[:, 0], sqr[:, 1], nrm[:, 0]]

        def mix(m):
            return mix_a[:, m] if m < 4 else y5[:, m - 4]

        def psum(name, shape):
            return ctx.enter_context(nc.psum_tensor(name, shape, F32))

        pg = [psum(f"pg{b}", [P, T]) for b in range(2)]
        px, py = psum("px", [P, T]), psum("py", [P, T])
        ps = [psum(f"ps{b}", [P, 2, T]) for b in range(2)]

        w_landed = [sem(f"w_landed{s}") for s in range(RING)]
        hi_done, lo_done = sem("hi_done"), sem("lo_done")
        tile_done = sem("tile_done")
        pg_free = [sem(f"pg_free{b}") for b in range(2)]
        px_full, px_free = sem("px_full"), sem("px_free")
        py_full, py_free = sem("py_full"), sem("py_free")
        ps_full, ps_free = sem("ps_full"), [sem(f"ps_free{b}") for b in range(2)]
        src_done, xhi_done, xlo_done = sem("src_done"), sem("xhi_done"), sem("xlo_done")
        c_landed, x_landed, p_landed, s_landed, r_landed, l_landed, x2_landed = (
            sem(n) for n in ("c_landed", "x_landed", "p_landed", "s_landed", "r_landed", "l_landed", "x2_landed"))
        stored = sem("stored")
        sq_done, sq_read, rstd_ready = sem("sq_done"), sem("sq_read"), sem("rstd_ready")
        lane_act, lane_dve, lam_dve = sem("lane_act"), sem("lane_dve"), sem("lam_dve")
        tab_mul, tab_add, in_add, scanned = sem("tab_mul"), sem("tab_add"), sem("in_add"), sem("scanned")
        out_mul, y_mm, ya_free = sem("out_mul"), sem("y_mm"), sem("ya_free")
        gelu_done = sem("gelu_done")
        act_c, dve_c = sem("act_c"), sem("dve_c")
        roped, maxed, combed, o_sq, o_done = (sem(n) for n in ("roped", "maxed", "combed", "o_sq", "o_done"))
        rs_k, rs_q, rs_o = sem("rs_k"), sem("rs_q"), sem("rs_o")
        cnv_act, silu_done, res_done, fin_done = sem("cnv_act"), sem("silu_done"), sem("res_done"), sem("fin_done")
        xc_act, xc_done, la_done, tt_dve, tt_act, lru_h = (sem(n) for n in ("xc_act", "xc_done", "la_done", "tt_dve", "tt_act", "lru_h"))
        pv2_hi, cnv_done, gelu2_done, acc_done = sem("pv2_hi"), sem("cnv_done"), sem("gelu2_done"), sem("acc_done")
        x_mul = sem("x_mul")

        ident = cst[:, C_ID:C_ID + P]
        ones = cst[:, C_ONES:C_ONES + P]
        block_ones = cst[:, C_BLK:C_BLK + P]
        rotate = cst[:, C_ROT:C_ROT + P]
        mult = cst[:, C_MULT:C_MULT + T]
        ident_b = msk[:, M_ID:M_ID + P]

        def par(name, i=0):
            a, w = PARAMS[name]
            return prm[:, a + i:a + i + 1]

        def pars(name):
            a, w = PARAMS[name]
            return prm[:, a:a + w]

        def cc(i):
            return cst[:, i:i + 1]

        def tiles_after(u):
            return TILES_AFTER[u]

        def evacuated(eng, name):
            eng.wait_ge(pg_free[TILE[name] % 2], TILE[name] // 2 + 1)

        def px_read(eng, name):
            eng.wait_ge(px_free, XUSE[name] + 1)

        def py_read(eng, name):
            eng.wait_ge(py_free, YUSE[name] + 1)

        def ps_read(eng, name):
            eng.wait_ge(ps_free[SUSE[name] % 2], SUSE[name] // 2 + 1)

        def ps_ready(eng, name):
            eng.wait_ge(ps_full, SUSE[name] + 1)
            return ps[SUSE[name] % 2]

        block = ctx.enter_context(nc.Block())

        @block.sync
        def _(sp):
            sp.dma_start(hid[:], x_dram).then_inc(x_landed, 16)
            sp.dma_start(cst[:], consts).then_inc(c_landed, 16)
            sp.dma_start(msk_raw, masks).then_inc(c_landed, 16)
            sp.dma_start(prm[:], params).then_inc(p_landed, 16)
            for u in range(RING):
                sp.dma_start(w_raw[:, u], weights[u].rearrange("p (k m) -> p k m", k=KT)).then_inc(w_landed[u], 16)
                if u == 0:
                    sp.dma_start(b_in[:], ssm_b).then_inc(s_landed, 16)
                    sp.dma_start(c_in[:], ssm_c).then_inc(s_landed, 16)
            full = len(UNITS) // RING
            with sp.Fori(1, full) as r:
                for s in range(RING):
                    sp.wait_ge(lo_done, r * RING + (s + 1 - RING))
                    sp.dma_start(w_raw[:, s], weights[r * RING + s].rearrange("p (k m) -> p k m", k=KT))\
                        .then_inc(w_landed[s], 16)
            for u in range(full * RING, len(UNITS)):
                sp.wait_ge(lo_done, u + 1 - RING)
                sp.dma_start(w_raw[:, u % RING], weights[u].rearrange("p (k m) -> p k m", k=KT))\
                    .then_inc(w_landed[u % RING], 16)
            for k in range(KT):
                sp.wait_ge(fin_done, k + 1)
                sp.dma_start(out[:, k], hid[:, k]).then_inc(stored, 16)
            sp.wait_ge(stored, 16 * KT)

        @block.gpsimd
        def _(pool):
            def lo(u, s):
                pool.wait_ge(hi_done, u + 1)
                pool.tensor_tensor(w_lo[:, s], w_raw[:, s], w_hi[:, s].bitcast(F32), ALU.subtract)\
                    .then_inc(lo_done, 1)

            g0 = UNIT[("gate", 0)]
            for u in range(g0 + 3):
                lo(u, u % RING)
            pool.wait_ge(tab_mul, 1)
            pool.tensor_tensor(rot[:, 0, 0], rot[:, 0, 0], rot_m[:, 0], ALU.subtract).then_inc(tab_add, 1)
            pool.tensor_tensor(rot[:, 0, 1], rot[:, 0, 1], rot_m[:, 1], ALU.add).then_inc(tab_add, 1)
            for t in range(LANE_T):
                px_read(pool, ("br", t))
                py_read(pool, ("bi", t))
                pool.tensor_tensor(vz[:, 0], vz[:, 0], v_m[:, 0], ALU.add).then_inc(in_add, 1)
                pool.tensor_tensor(vz[:, 1], vz[:, 1], v_m[:, 1], ALU.subtract).then_inc(in_add, 1)
                lo(g0 + 3 + t, (g0 + 3 + t) % RING)
                if t + 1 < LANE_T:
                    n = (t + 1) % 2
                    pool.wait_ge(tab_mul, t + 2)
                    pool.tensor_tensor(rot[:, n, 0], rot[:, n, 0], rot_m[:, 0], ALU.subtract).then_inc(tab_add, 1)
                    pool.tensor_tensor(rot[:, n, 1], rot[:, n, 1], rot_m[:, 1], ALU.add).then_inc(tab_add, 1)
                pool.wait_ge(scanned, t + 1)
                if t >= 2:
                    pool.wait_ge(y_mm, t - 1)
                pool.tensor_tensor(xs[:, t % 2, 3], vz[:, 1], rot[:, t % 2, 0], ALU.mult).then_inc(x_mul, 1)
            u = g0 + 3 + LANE_T
            while u % RING:
                lo(u, u % RING)
                u += 1
            full = len(UNITS) // RING
            with pool.Fori(u // RING, full) as r:
                for s in range(RING):
                    lo(r * RING + s, s)
            for u in range(full * RING, len(UNITS)):
                lo(u, u % RING)

        @block.tensor
        def _(pe):
            def tile(u, o, xh, xl, first_split=None, ks=range(KT), off=0):
                s, bank = u % RING, pg[o % 2]
                pe.wait_ge(lo_done, u + 1)
                if o >= 2:
                    pe.wait_ge(pg_free[o % 2], o // 2)
                ks = list(ks)
                for n, k in enumerate(ks):
                    if first_split is not None:
                        pe.wait_ge(xlo_done, first_split + n + 1)
                    wh, wl = w_hi[:, s, off + k, :], w_lo[:, s, off + k, :]
                    pe.matmul(bank[:], wh, xh(k), start=n == 0, stop=False)
                    pe.matmul(bank[:], wh, xl(k), start=False, stop=False)
                    last = pe.matmul(bank[:], wl, xh(k), start=False, stop=n == len(ks) - 1)
                last.then_inc(tile_done, 1)

            def named(name, xh, xl, **kw):
                tile(UNIT[name], TILE[name], xh, xl, **kw)

            def model(t_hi, t_lo):
                return (lambda k: t_hi[:, k]), (lambda k: t_lo[:, k])

            XH, XL = model(x_hi, x_lo)

            def x_use(name):
                if XUSE[name] > 0:
                    pe.wait_ge(px_free, XUSE[name])

            def y_use(name):
                if YUSE[name] > 0:
                    pe.wait_ge(py_free, YUSE[name])

            def s_use(name):
                n = SUSE[name]
                if n >= 2:
                    pe.wait_ge(ps_free[n % 2], n // 2)
                return ps[n % 2]

            def stat_step(n, k):
                if k == 0:
                    x_use(("stat", n))
                pe.wait_ge(sq_done, KT * (n - 1) + k + 1)
                pe.matmul(px[:], ones, sqr[:, k % 2], start=k == 0, stop=k == KT - 1)\
                    .then_inc(px_full if k == KT - 1 else sq_read, 1)

            pe.wait_ge(c_landed, 32)
            for k in range(KT):
                stat_step(1, k)
            x_use("lam")
            pe.wait_ge(lam_dve, 1)
            pe.matmul(px[:, 0:2], ones, lam_t[:, 0:2], start=True, stop=True).then_inc(px_full, 1)

            for t in range(SSM_T):
                named(("u", t), XH, XL, first_split=SPLIT["norm1"] if t == 0 else None)

            def y_step(t):
                j, bank = t % 4, ps[(t // 4) % 2]
                if j == 0 and t >= 8:
                    pe.wait_ge(ya_free, t // 4 - 1)
                pe.wait_ge(out_mul, t + 1)
                pe.wait_ge(x_mul, t + 1)
                rows = bank[32 * j:32 * j + 32, 0, :]
                for n in range(4):
                    last = pe.matmul(rows, c_out[:, n // 2, 32 * t:32 * t + 32], xs[:, t % 2, n], start=n == 0, stop=n == 3)
                last.then_inc(y_mm, 1)

            for t in range(LANE_T + 1):
                if t < LANE_T:
                    named(("gate", t), XH, XL)
                    j = t % 4
                    if t == 0:
                        pe.wait_ge(s_landed, 32)
                        evacuated(pe, ("u", SSM_T - 1))
                        evacuated(pe, ("u", SSM_T - 2))
                        pe.wait_ge(lane_dve, LANE_MARK)
                    for c, (bank, use, full, name) in enumerate(((px, x_use, px_full, "br"),
                                                                 (py, y_use, py_full, "bi"))):
                        use((name, t))
                        pe.matmul(bank[:], b_in[32 * j:32 * j + 32, t // 4, c, :], hid[32 * j:32 * j + 32, t // 4, :],
                                  start=True, stop=True).then_inc(full, 1)
                if t > 0:
                    y_step(t - 1)

            def scores(h, i):
                bank, w = s_use(("s", h, i)), P * (i + 1)
                if h == 0 and i == 0:
                    pe.wait_ge(ya_free, SSM_T)
                pe.wait_ge(roped, 2 * h + 2)
                for c in range(2):
                    r = slice(64 * c, 64 * c + 64)
                    pe.matmul(bank[:, c, 0:w], qq[r, h % 2, P * i:P * i + P], kk[r, h % 2, 0:w], start=True, stop=False)
                    last = pe.matmul(bank[:, c, P * i:w], ident_b, msk[:, M_TRI:M_TRI + P], start=False, stop=True)
                last.then_inc(ps_full, 1)

            def turn(h, i):
                bank = s_use(("t", h, i))
                pe.wait_ge(combed, 4 * h + i + 1)
                for j in range(i + 1):
                    last = pe.transpose(bank[:, 0, P * j:P * j + P], pa[:, i % 2, P * j:P * j + P], ident)
                last.then_inc(ps_full, 1)

            def kq_sums(h, name, n):
                x_use(("ssq_" + name, h))
                evacuated(pe, (name, h))
                pe.matmul(px[:], block_ones, kq_sq[n], start=True, stop=True).then_inc(px_full, 1)
                y_use(("rot_" + name, h))
                pe.matmul(py[:], rotate, kq_raw[:, n], start=True, stop=True).then_inc(py_full, 1)

            for h in range(HEADS + 2):
                g = h - 1
                attends = 0 <= g < HEADS
                if h < HEADS:
                    named(("k", h), XH, XL)
                if attends:
                    x_use(("vt", g))
                    evacuated(pe, ("v", g))
                    for j in range(QB):
                        last = pe.transpose(px[:, P * j:P * j + P], v_raw[:, P * j:P * j + P], ident)
                    last.then_inc(px_full, 1)
                    scores(g, 0)
                    scores(g, 1)
                if h >= 2:
                    y_use(("pv", h - 2))
                    px_read(pe, ("vt", h - 2))
                    ps_read(pe, ("t", h - 2, 2))
                    ps_read(pe, ("t", h - 2, 3))
                    for j in range(QB):
                        last = pe.matmul(py[:, P * j:T], vv[:, h % 2, j, :], pt[:, j, P * j:T],
                                         start=j == 0, stop=j == QB - 1)
                    last.then_inc(py_full, 1)
                if h < HEADS:
                    named(("q", h), XH, XL)
                if h >= 2:
                    x_use(("ssq_o", h - 2))
                    pe.wait_ge(o_sq, h - 1)
                    pe.matmul(px[:], ones, kq_sq[2], start=True, stop=True).then_inc(px_full, 1)
                if attends:
                    turn(g, 0)
                    turn(g, 1)
                if h < HEADS:
                    kq_sums(h, "k", 0)
                if attends:
                    scores(g, 2)
                    scores(g, 3)
                if h < HEADS:
                    named(("v", h), XH, XL)
                    kq_sums(h, "q", 1)
                if attends:
                    turn(g, 2)
                    turn(g, 3)

            for m in range(4):
                tile(UNIT[("glu", m // 2)], TILE[("glu", m)], XH, XL, first_split=SPLIT["g"] if m == 0 else None,
                     ks=range(4), off=4 * (m % 2))
            for m in range(KT):
                tile(UNIT[("ssm", m // 2)], TILE[("ssm", m)], lambda k: x_hi[:, 4 + k], lambda k: x_lo[:, 4 + k],
                     first_split=SPLIT["s"] if m == 0 else None, ks=range(4), off=4 * (m % 2))
            for m in range(KT):
                named(("attn", m), XH, XL, first_split=SPLIT["o"] if m == 0 else None)
            MH, ML = model(mix_hi, mix_lo)
            for m in range(KT):
                named(("out", m), MH, ML, first_split=SPLIT["mix"] if m == 0 else None)
                if m > 0:
                    stat_step(2, m - 1)
            stat_step(2, KT - 1)

            def ffn(tiles, ups, down, split_in, split_act, hi, lo_, stat_n):
                order = ffn_order(tiles)
                for kind, c in order:
                    a, b = chunks_of(tiles)[c]
                    if kind == "up":
                        for i in range(a, b):
                            for n, up in enumerate(ups):
                                named((up, i), XH, XL, first_split=SPLIT[split_in] if i == 0 and n == 0 else None)
                    else:
                        for m in range(KT):
                            named((down, c, m), lambda k: hi[:, c % 2, k], lambda k: lo_[:, c % 2, k], ks=range(b - a),
                                  first_split=SPLIT[split_act] + a if m == 0 else None)
                            if (kind, c) == order[-1] and m > 0:
                                stat_step(stat_n, m - 1)
                stat_step(stat_n, KT - 1)

            ffn(FF1, ("fgate", "fval"), "down", "norm2", "act", act_hi, act_lo, 3)

            def lru_gate(t):
                for c, (bank, use, full, name) in enumerate(((px, x_use, px_full, "rg"), (py, y_use, py_full, "ig"))):
                    use((name, t))
                    if c == 0:
                        pe.wait_ge(xc_done, 3 * t + 3)
                        pe.wait_ge(l_landed, 16)
                    pe.matmul(bank[:], lru_b[:, c, t], xc[:, t], start=True, stop=True).then_inc(full, 1)

            for t in range(LRU_T):
                named(("xr", t), XH, XL, first_split=SPLIT["norm3"] if t == 0 else None)
                if t > 0:
                    lru_gate(t - 1)

            def scores2(j, i):
                bank, w = s_use(("p", j, i)), P * (i + 1)
                for c in range(2):
                    r = slice(64 * c, 64 * c + 64)
                    pe.matmul(bank[:, c, 0:w], qq2[r, j % 2, P * i:P * i + P], kk2[r, j % 2, 0:w], start=True, stop=False)
                    last = pe.matmul(bank[:, c, 0:w], ident_b, msk[:, M_UNI + T - w:M_UNI + T], start=False, stop=True)
                last.then_inc(ps_full, 1)

            def turn2(j, i):
                bank = s_use(("t2", j, i))
                pe.wait_ge(combed, 4 * (HEADS + j) + i + 1)
                for c in range(2):
                    for b in range(i + 1):
                        last = pe.transpose(bank[:, c, P * b:P * b + P], pr2[:, i % 2, c, P * b:P * b + P], ident)
                last.then_inc(ps_full, 1)

            def values2(j, i):
                if i == 0:
                    y_use(("pv2", j))
                ps_read(pe, ("t2", j, i))
                for c in range(2):
                    r = slice(64 * c, 64 * c + 64)
                    for b in range(i + 1):
                        last = pe.matmul(py[r, P * i:P * i + P], vv2[:, b, r], pt2[:, i % 2, c, b, :],
                                         start=b == 0, stop=b == i)
                if i == QB - 1:
                    last.then_inc(py_full, 1)

            for j in range(PAIRS + 1):
                g = j - 1
                if j < PAIRS:
                    named(("k2", j), XH, XL)
                    if j == 0:
                        lru_gate(LRU_T - 1)
                if g >= 0:
                    evacuated(pe, ("k2", g))
                    evacuated(pe, ("q2", g))
                    scores2(g, 0)
                    scores2(g, 1)
                if j < PAIRS:
                    named(("q2", j), XH, XL)
                if g >= 0:
                    turn2(g, 0)
                    turn2(g, 1)
                    scores2(g, 2)
                    scores2(g, 3)
                if j < PAIRS:
                    named(("v2", j), XH, XL)
                if g >= 0:
                    px_read(pe, ("vt2", g))
                    values2(g, 0)
                    values2(g, 1)
                    turn2(g, 2)
                    turn2(g, 3)
                if j < PAIRS:
                    named(("gr", j), XH, XL)
                if g >= 0:
                    values2(g, 2)
                    values2(g, 3)
                if j < PAIRS:
                    x_use(("vt2", j))
                    evacuated(pe, ("v2", j))
                    for b in range(QB):
                        last = pe.transpose(px[:, P * b:P * b + P], v_raw2[:, P * b:P * b + P], ident)
                    last.then_inc(px_full, 1)

            M2H, M2L = model(mx2_hi, mx2_lo)
            pe.wait_ge(xlo_done, SPLIT["rec"] + 4)
            py_read(pe, ("pv2", PAIRS - 1))
            for m in range(KT):
                named(("out2", m), M2H, M2L)
                if m > 0:
                    stat_step(4, m - 1)
            stat_step(4, KT - 1)
            for k in range(KT):
                stat_step(5, k)
            ffn(FF2, ("ff",), "down2", "norm4", "act2", act2_hi, act2_lo, 6)


        @block.scalar
        def _(act):
            sent = {}

            def put(ins, s):
                ins.then_inc(s, 1)
                sent[s.name] = sent.get(s.name, 0) + 1
                return sent[s.name]

            def hi(u):
                if u >= len(UNITS):
                    return
                s = u % RING
                act.wait_ge(w_landed[s], 16 * (u // RING + 1))
                if u >= RING:
                    act.wait_ge(tile_done, TILES_AFTER[u - RING])
                put(act.activation(w_hi[:, s], w_raw[:, s], ACT.Copy), hi_done)

            def ahead(name):
                hi(UNIT[name] + RING - 1)

            def done(name):
                act.wait_ge(tile_done, TILE[name] + 1)
                return pg[TILE[name] % 2][:]

            def free(ins, name):
                ins.then_inc(pg_free[TILE[name] % 2], 1)

            def px_ready(name):
                act.wait_ge(px_full, XUSE[name] + 1)

            def py_ready(name):
                act.wait_ge(py_full, YUSE[name] + 1)

            def split_hi(group, k, dst, src):
                act.wait_ge(src_done, SRC[group] + k + 1)
                put(act.activation(dst, src, ACT.Copy), xhi_done)

            def square(n, k, src):
                if k >= 2:
                    act.wait_ge(sq_read, (KT - 1) * (n - 1) + k - 1)
                elif n > 1:
                    act.wait_ge(px_full, XUSE[("stat", n - 1)] + 1)
                put(act.activation(sqr[:, k % 2], src, ACT.Square), sq_done)

            def inverse_root(n, dst, power=-0.5):
                px_ready(("stat", n))
                act.activation(dst[:], px[:], ACT.Ln, bias=cc(C_EPS), scale=1.0 / D).then_inc(px_free, 1)
                px_read(act, ("stat", n))
                put(act.activation(dst[:], dst[:], ACT.Exp, scale=power), rstd_ready)

            for u in range(RING - 1):
                hi(u)
            act.wait_ge(x_landed, 16)
            act.wait_ge(c_landed, 32)
            for k in range(KT):
                square(1, k, hid[:, k])
            inverse_root(1, rstd)
            for k in range(KT):
                split_hi("norm1", k, x_hi[:, k], nrm[:, k % 2])
            act.wait_ge(p_landed, 16)
            put(act.activation(lane[:, L_DT], pars("log_dt"), ACT.Exp), lane_act)
            px_ready("lam")
            act.activation(lam_t[:, 2:4], px[:, 0:2], ACT.Exp).then_inc(px_free, 1)
            act.wait_ge(lane_dve, 1)
            put(act.activation(lane[:, L_MAG], lane[:, L_Z], ACT.Exp), lane_act)
            put(act.activation(lane[:, L_TANH], lane[:, L_Z], ACT.Tanh, scale=0.5), lane_act)
            put(act.activation(lcf[:, 1], lcf[:, 0], ACT.Exp, scale=-1.0), lane_act)
            ahead(("u", 0))
            act.wait_ge(lane_dve, 2)
            put(act.activation(lane[:, L_S], lane[:, L_R], ACT.Sin, scale=0.5), lane_act)
            put(act.activation(lane[:, L_C], lane[:, L_R], ACT.Sin, scale=0.5, bias=cc(C_HPI)), lane_act)
            for t in range(SSM_T):
                if t > 0:
                    ahead(("u", t))
                a = done(("u", t))
                free(act.activation(hid[:, t], a, ACT.Copy), ("u", t))
            for g in range(16):
                ahead(("gate", g))
                free(act.activation(gates[:, g], done(("gate", g)), ACT.Sigmoid), ("gate", g))
            act.wait_ge(ya_free, SSM_T)
            act.dma_start(rtab[:], rope).then_inc(r_landed, 16)
            for t in range(SSM_T):
                put(act.activation(y5[:, t], y5[:, t], ACT.Gelu_apprx_tanh), gelu_done)

            def exps(use, dst, w, i, negmax, sums):
                act.wait_ge(maxed, EXPS[use] + 1)
                bank = ps_ready(act, use)
                for c in range(2):
                    kw = {"accum_out": sums[:, i % 2, 2 + c:3 + c]} if sums is not None else {}
                    ins = act.activation(dst[:, c, 0:w], bank[:, c, 0:w], ACT.Exp, bias=negmax[:, i % 2, c:c + 1], **kw)
                    ins.then_inc(ps_free[SUSE[use] % 2] if c else act_c, 1)

            def exps1(h, i):
                if 4 * h + i >= 2:
                    act.wait_ge(combed, 4 * h + i - 1)
                exps(("s", h, i), pr[:, i % 2], P * (i + 1), i, soft, soft)

            def turned(h, i):
                w = P * (i + 1)
                bank = ps_ready(act, ("t", h, i))
                act.activation(pt[:, 0:i + 1, P * i:w], bank[:, 0, 0:w].rearrange("p (j q) -> p j q", q=P), ACT.Copy)\
                    .then_inc(ps_free[SUSE[("t", h, i)] % 2], 1)

            def kq_out(h, name, n, gain):
                ahead((name, h))
                a = done((name, h))
                if h > 0:
                    act.wait_ge(roped, 2 * h - 1 + n)
                act.activation(kq_sq[n], a, ACT.Square)
                free(act.activation(kq_raw[:, n], a, ACT.Copy, scale=par(gain)), (name, h))

            def head_root(use, n, eps, scale, ready):
                px_ready(use)
                act.activation(kq_rs[:, n], px[:], ACT.Ln, bias=cc(eps), scale=scale).then_inc(px_free, 1)
                px_read(act, use)
                put(act.activation(kq_rs[:, n], kq_rs[:, n], ACT.Exp, scale=-0.5), ready)

            for h in range(HEADS + 2):
                g = h - 1
                attends = 0 <= g < HEADS
                if h < HEADS:
                    kq_out(h, "k", 0, "kg")
                if attends:
                    px_ready(("vt", g))
                    act.activation(vv[:, g % 2], px[:].rearrange("p (j d) -> p j d", d=P), ACT.Copy).then_inc(px_free, 1)
                    exps1(g, 0)
                    exps1(g, 1)
                if h >= 2:
                    py_ready(("pv", h - 2))
                    put(act.activation(kq_sq[2], py[:], ACT.Square), o_sq)
                    act.activation(hid[:, h - 2], py[:], ACT.Copy).then_inc(py_free, 1)
                if h < HEADS:
                    kq_out(h, "q", 1, "qg")
                if h >= 2:
                    if h >= 3:
                        act.wait_ge(o_done, h - 2)
                    head_root(("ssq_o", h - 2), 2, C_EPS, 1.0 / P, rs_o)
                if attends:
                    turned(g, 0)
                if h < HEADS:
                    head_root(("ssq_k", h), 0, C_EPS, 1.0 / 64, rs_k)
                if attends:
                    exps1(g, 2)
                    exps1(g, 3)
                if h < HEADS:
                    ahead(("v", h))
                    free(act.activation(v_raw[:], done(("v", h)), ACT.Copy), ("v", h))
                    head_root(("ssq_q", h), 1, C_EPS64, 1.0, rs_q)
                if attends:
                    turned(g, 2)

            act.wait_ge(tile_done, TILE[("v", HEADS - 1)] + 1)
            for t in range(SSM_T):
                act.wait_ge(gelu_done, t + 1)
                put(act.activation(x_hi[:, t], y5[:, t], ACT.Copy), xhi_done)
            for m in range(4):
                if m % 2 == 0:
                    ahead(("glu", m // 2))
                a = done(("glu", m))
                if m >= 2:
                    act.wait_ge(src_done, SRC["s"] + m - 1)
                free(act.activation(sqr[:, m % 2], a, ACT.Sigmoid, bias=par("b_glu", m)), ("glu", m))
                if m > 0:
                    split_hi("s", m - 1, x_hi[:, 3 + m], nrm[:, (m - 1) % 2])
            split_hi("s", 3, x_hi[:, 7], nrm[:, 1])
            for n in range(4):
                ahead(("ssm", n))
            act.wait_ge(tile_done, TILE[("ssm", KT - 1)] + 1)
            for h in range(HEADS):
                act.wait_ge(o_done, h + 1)
                put(act.activation(x_hi[:, h], hid[:, h], ACT.Copy), xhi_done)
            for m in range(KT):
                ahead(("attn", m))
                if m == 2:
                    act.wait_ge(xlo_done, SPLIT["o"] + KT)
                    act.dma_start(hid[:], x_dram).then_inc(x2_landed, 16)
                split_hi("mix", m, mix_hi[:, m], mix(m))
            for m in range(KT):
                ahead(("out", m))
                evacuated(act, ("out", m))
                square(2, m, hid[:, m])
                split_hi("norm2", m, x_hi[:, m], nrm[:, m % 2])
            inverse_root(2, rstd)
            order = ffn_order(FF1)
            for kind, c in order:
                a, b = chunks_of(FF1)[c]
                if kind == "up":
                    if c >= 2:
                        act.wait_ge(tile_done, TILE[("down", c - 2, KT - 1)] + 1)
                    for i in range(a, b):
                        for n, (name, col) in enumerate((("fgate", i), ("fval", FF1 + i))):
                            ahead((name, i))
                            evacuated(act, (name, i))
                            if i > 0 and n == 0:
                                act.wait_ge(src_done, SRC["act"] + i)
                            put(act.activation(cnv[:, n], cu[:, n], ACT.Identity, bias=par("cb", col),
                                               scale=par("cw", 88 + col)), cnv_act)
                            if n == 0 and i > a:
                                split_hi("act", i - 1, act_hi[:, c % 2, i - 1 - a], hsrc[:, (i - 1) % 2])
                        act.wait_ge(cnv_done, 2 * i + 1)
                        put(act.activation(cnv[:, 0], cnv[:, 0], ACT.Silu), silu_done)
                    split_hi("act", b - 1, act_hi[:, c % 2, b - 1 - a], hsrc[:, (b - 1) % 2])
                else:
                    for m in range(KT):
                        ahead(("down", c, m))
                        if (kind, c) == order[-1]:
                            evacuated(act, ("down", c, m))
                            square(3, m, hid[:, m])
                            split_hi("norm3", m, x_hi[:, m], nrm[:, m % 2])
            act.dma_start(lru_b[:], lru_w).then_inc(l_landed, 16)
            inverse_root(3, rstd)

            def lru_gate(t):
                px_ready(("rg", t))
                act.activation(ra[:, t], px[:], ACT.Sigmoid, bias=par("b_r", t)).then_inc(px_free, 1)
                py_ready(("ig", t))
                act.activation(ii[:, t], py[:], ACT.Sigmoid, bias=par("b_i", t)).then_inc(py_free, 1)

            for t in range(LRU_T):
                ahead(("xr", t))
                evacuated(act, ("xr", t))
                put(act.activation(xc[:, t], sqr[:, t % 2], ACT.Identity, bias=par("cb2", t),
                                   scale=par("cw2", 12 + t)), xc_act)
                if t > 0:
                    lru_gate(t - 1)

            def turned2(j, i):
                w = P * (i + 1)
                bank = ps_ready(act, ("t2", j, i))
                act.activation(pt2[:, i % 2, :, 0:i + 1, :], bank[:, :, 0:w].rearrange("p c (b q) -> p c b q", q=P), ACT.Copy)\
                    .then_inc(ps_free[SUSE[("t2", j, i)] % 2], 1)

            def exps2(j, i):
                n = 4 * j + i
                if n >= 2:
                    ps_ready(act, ("t2", (n - 2) // 4, (n - 2) % 4))
                exps(("p", j, i), pr2[:, i % 2], P * (i + 1), i, soft2, None)

            for j in range(PAIRS + 1):
                g = j - 1
                if j < PAIRS:
                    ahead(("k2", j))
                if j == 0:
                    lru_gate(LRU_T - 1)
                    for t in range(LRU_T):
                        px_read(act, ("rg", t))
                        put(act.activation(tt[:, t], ra[:, t], ACT.Tanh, scale=lcf[:, 6, t:t + 1]), act_c)
                        put(act.activation(ra[:, t], ra[:, t], ACT.Exp, scale=lcf[:, 7, t:t + 1]), la_done)
                if g >= 0:
                    if g == 0:
                        act.wait_ge(lru_h, LRU_T)
                    exps2(g, 0)
                    exps2(g, 1)
                if j < PAIRS:
                    ahead(("q2", j))
                if g >= 0:
                    turned2(g, 0)
                    exps2(g, 2)
                    exps2(g, 3)
                if j < PAIRS:
                    ahead(("v2", j))
                if j == 0:
                    for t in range(LRU_T):
                        act.wait_ge(tt_dve, t + 1)
                        put(act.activation(tt[:, t], tt[:, t], ACT.Sqrt), tt_act)
                if g >= 0:
                    turned2(g, 2)
                if j < PAIRS:
                    ahead(("gr", j))
                    evacuated(act, ("gr", j))
                    put(act.activation(sqr[:, j % 2], sqr[:, j % 2], ACT.Gelu_apprx_tanh), gelu2_done)
                    split_hi("rec", j, mx2_hi[:, 4 + j], nrm[:, j % 2])
                if g >= 0:
                    py_ready(("pv2", g))
                    put(act.activation(mx2_hi[:, g], py[:], ACT.Copy), pv2_hi)
                if j < PAIRS:
                    px_ready(("vt2", j))
                    act.activation(vv2[:], px[:].rearrange("p (b d) -> p b d", d=P), ACT.Copy).then_inc(px_free, 1)
            for m in range(KT):
                ahead(("out2", m))
                a = done(("out2", m))
                square(4, m, a)
                free(act.activation(acc[:, m], a, ACT.Copy), ("out2", m))
            inverse_root(4, rstd)
            for k in range(KT):
                act.wait_ge(res_done, k + 1)
                square(5, k, hid[:, k])
                split_hi("norm4", k, x_hi[:, k], nrm[:, k % 2])
            inverse_root(5, rstd_sq, -1.0)
            order = ffn_order(FF2)
            for kind, c in order:
                a, b = chunks_of(FF2)[c]
                if kind == "up":
                    if c >= 2:
                        act.wait_ge(tile_done, TILE[("down2", c - 2, KT - 1)] + 1)
                    for i in range(a, b):
                        ahead(("ff", i))
                        ps_ = done(("ff", i))
                        if i > 0:
                            act.wait_ge(src_done, SRC["act2"] + i)
                        free(act.activation(rel[:], ps_, ACT.Relu), ("ff", i))
                        split_hi("act2", i, act2_hi[:, c % 2, i - a], nrm[:, i % 2])
                else:
                    for m in range(KT):
                        ahead(("down2", c, m))
                        if c == 0:
                            free(act.activation(acc[:, m], done(("down2", c, m)), ACT.Copy), ("down2", c, m))
                        if (kind, c) == order[-1]:
                            act.wait_ge(acc_done, m + 1)
                            square(6, m, acc[:, m])
            inverse_root(6, rstd)

        @block.vector
        def _(dve):
            sent = {}

            def put(ins, s):
                ins.then_inc(s, 1)
                sent[s.name] = sent.get(s.name, 0) + 1
                dve.wait_ge(s, sent[s.name])

            def link(ins):
                put(ins, dve_c)

            def done(name):
                dve.wait_ge(tile_done, TILE[name] + 1)
                return pg[TILE[name] % 2][:]

            def free(ins, name):
                ins.then_inc(pg_free[TILE[name] % 2], 1)
                evacuated(dve, name)

            def tt_(out_, a, b, op=ALU.mult):
                return dve.tensor_tensor(out_, a, b, op)

            def stt(out_, a, s, b, op0=ALU.mult, op1=ALU.mult):
                return dve.scalar_tensor_tensor(out_, a, s, b, op0, op1)

            def ts(out_, a, s1, op0, s2=None, op1=ALU.bypass):
                return dve.tensor_scalar(out_, a, s1, s2, op0, op1)

            def split_lo(n, dst, src, hi_):
                dve.wait_ge(xhi_done, n + 1)
                put(tt_(dst, src, hi_.bitcast(F32), ALU.subtract), xlo_done)

            def root_ready(n):
                dve.wait_ge(rstd_ready, n)

            def scaled(group, m, gain, last=KT - 1):
                put(ts(nrm[:, m % 2], hid[:, m], par(gain, m), ALU.mult), src_done)
                for k in ([m - 1] if m > 0 else []) + ([m] if m == last else []):
                    split_lo(SPLIT[group] + k, x_lo[:, k], nrm[:, k % 2], x_hi[:, k])

            dve.wait_ge(c_landed, 32)
            link(dve.tensor_copy(msk[:], msk_raw))
            dve.wait_ge(p_landed, 16)
            lam4 = pars("lam")
            tt_(lam_t[:, 0:1], lam4[:, 0:1], lam4[:, 1:2])
            put(tt_(lam_t[:, 1:2], lam4[:, 2:3], lam4[:, 3:4]), lam_dve)
            root_ready(1)
            for k in range(KT + 1):
                if k < KT:
                    put(stt(nrm[:, k % 2], hid[:, k], par("norm1", k), rstd[:]), src_done)
                if k > 0:
                    split_lo(SPLIT["norm1"] + k - 1, x_lo[:, k - 1], nrm[:, (k - 1) % 2], x_hi[:, k - 1])

            def L(i):
                return lane[:, i]

            dve.wait_ge(lane_act, 1)
            tt_(L(L_TH), pars("a_im"), L(L_DT))
            link(ts(lcf[:, 0], pars("lru"), -1.0, ALU.mult))
            link(tt_(lcf[:, 0], lcf[:, 0], pars("lru"), ALU.max))
            put(tt_(L(L_Z), pars("a_re"), L(L_DT)), lane_dve)
            dve.wait_ge(lane_dve, 1)
            link(ts(L(L_N), L(L_TH), 1.0 / TWO_PI, ALU.mult, BIG, ALU.add))
            link(ts(L(L_N), L(L_N), BIG, ALU.subtract))
            link(stt(L(L_R), L(L_N), -PI_1, L(L_TH), ALU.mult, ALU.add))
            link(stt(L(L_R), L(L_N), -PI_2, L(L_R), ALU.mult, ALU.add))
            link(stt(L(L_R), L(L_N), -PI_3, L(L_R), ALU.mult, ALU.add))
            put(ts(L(L_R), L(L_R), 3.1415925, ALU.min, -3.1415925, ALU.max), lane_dve)
            px_read(dve, "lam")
            link(tt_(lam_t[:, 4:5], lam_t[:, 3:4], lam_t[:, 2:3], ALU.subtract))
            link(ts(lam_t[:, 5:6], lam_t[:, 4:5], -LAM_INIT, ALU.add))
            link(ts(lam_t[:, 6:7], par("subln"), 1.0 - LAM_INIT, ALU.mult))
            dve.wait_ge(lane_act, 4)
            link(ts(lcf[:, 2], lcf[:, 1], 2.0, ALU.add))
            link(dve.reciprocal(lcf[:, 2], lcf[:, 2]))
            link(tt_(lcf[:, 2], lcf[:, 2], lcf[:, 1]))
            link(tt_(lcf[:, 3], lcf[:, 2], lcf[:, 2]))
            link(ts(lcf[:, 4], lcf[:, 3], 1.0 / 17, ALU.mult))
            for n in (15, 13, 11, 9, 7, 5, 3):
                link(stt(lcf[:, 4], lcf[:, 4], 1.0 / n, lcf[:, 3], ALU.add, ALU.mult))
            link(stt(lcf[:, 4], lcf[:, 4], 1.0, lcf[:, 2], ALU.add, ALU.mult))
            link(ts(lcf[:, 5], pars("lru"), -1.0, ALU.mult, 0.0, ALU.max))
            link(stt(lcf[:, 5], lcf[:, 4], 2.0, lcf[:, 5], ALU.mult, ALU.add))
            link(ts(lcf[:, 6], lcf[:, 5], 8.0, ALU.mult))
            link(ts(lcf[:, 7], lcf[:, 5], -8.0, ALU.mult))
            dve.wait_ge(lane_act, 6)
            link(tt_(L(L_T1), L(L_S), L(L_C)))
            link(ts(L(L_SIN), L(L_T1), 2.0, ALU.mult))
            link(tt_(L(L_T2), L(L_S), L(L_S)))
            link(ts(L(L_CM1), L(L_T2), -2.0, ALU.mult))
            link(ts(L(L_COS), L(L_CM1), 1.0, ALU.add))
            link(stt(L(L_T1), L(L_MAG), 1.0, L(L_TANH), ALU.add, ALU.mult))
            link(tt_(L(L_T1), L(L_T1), L(L_COS)))
            link(tt_(L(L_NR), L(L_T1), L(L_CM1), ALU.add))
            link(tt_(L(L_NI), L(L_MAG), L(L_SIN)))
            link(tt_(L(L_T1), pars("a_re"), pars("a_re")))
            link(tt_(L(L_T2), pars("a_im"), pars("a_im")))
            link(tt_(L(L_T1), L(L_T1), L(L_T2), ALU.add))
            link(dve.reciprocal(L(L_T3), L(L_T1)))
            link(tt_(L(L_T1), L(L_NR), pars("a_re")))
            link(tt_(L(L_T2), L(L_NI), pars("a_im")))
            link(tt_(L(L_T1), L(L_T1), L(L_T2), ALU.add))
            link(tt_(L(L_CR), L(L_T1), L(L_T3)))
            link(tt_(L(L_T1), L(L_NI), pars("a_re")))
            link(tt_(L(L_T2), L(L_NR), pars("a_im")))
            link(tt_(L(L_T1), L(L_T1), L(L_T2), ALU.subtract))
            link(tt_(L(L_CI), L(L_T1), L(L_T3)))
            dve.wait_ge(s_landed, 32)

            def wide(i):
                return lane[:, i, :].rearrange("p (t o) -> p t o", o=1).broadcast_to([P, LANE_T, 32])

            def c3(a):
                return a.rearrange("p (t c) -> p t c", c=32)

            tmp0, tmp1 = nrm[:, 0], nrm[:, 1]
            tt_(c3(c_out[:, 0]), c3(c_in[:, 0]), wide(L_CR))
            link(tt_(c3(tmp0), c3(c_in[:, 1]), wide(L_CI)))
            tt_(c3(c_out[:, 1]), c3(c_in[:, 0]), wide(L_CI))
            link(tt_(c3(tmp1), c3(c_in[:, 1]), wide(L_CR)))
            link(tt_(c_out[:, 0], c_out[:, 0], tmp0, ALU.subtract))
            link(stt(c_out[:, 1], c_out[:, 1], -1.0, tmp1, ALU.mult, ALU.subtract))
            pc, pn = L_COS, L_SIN
            free_rows = [(L_T1, L_T2), (L_NR, L_NI)]
            n_sq = 0
            for table, width in ((e_lo, 32), (e_hi, 16)):
                dve.memset(table[:, 0, :, 0:1], 1.0)
                link(dve.memset(table[:, 1, :, 0:1], 0.0))
                n = 1
                while n < width:
                    def pw(i):
                        return lane[:, i, :].rearrange("p (t o) -> p t o", o=1).broadcast_to([P, LANE_T, n])

                    old_c, old_s = table[:, 0, :, 0:n], table[:, 1, :, 0:n]
                    new_c, new_s = table[:, 0, :, n:2 * n], table[:, 1, :, n:2 * n]
                    t0 = nrm[:, 0, 0:LANE_T * n].rearrange("p (t n) -> p t n", n=n)
                    t1 = nrm[:, 1, 0:LANE_T * n].rearrange("p (t n) -> p t n", n=n)
                    tt_(new_c, old_c, pw(pc))
                    tt_(t0, old_s, pw(pn))
                    tt_(new_s, old_s, pw(pc))
                    tt_(t1, old_c, pw(pn))
                    qc, qn = free_rows[n_sq % 2]
                    tt_(L(qc), L(pc), L(pc))
                    tt_(L(L_T3), L(pn), L(pn))
                    link(tt_(L(qn), L(pc), L(pn)))
                    tt_(new_c, new_c, t0, ALU.subtract)
                    tt_(new_s, new_s, t1, ALU.add)
                    tt_(L(qc), L(qc), L(L_T3), ALU.subtract)
                    link(ts(L(qn), L(qn), 2.0, ALU.mult))
                    pc, pn = qc, qn
                    n_sq += 1
                    n *= 2
            put(dve.tensor_copy(L(L_T3), L(pc)), lane_dve)
            dve.wait_ge(lane_dve, 3)

            def table_step(t):
                lo_ = [e_lo[:, c, t, :].rearrange("p (o b) -> p o b", o=1).broadcast_to([P, 16, 32]) for c in range(2)]
                hi_ = [e_hi[:, c, t, :].rearrange("p (a o) -> p a o", o=1).broadcast_to([P, 16, 32]) for c in range(2)]

                def ab(a):
                    return a.rearrange("p (a b) -> p a b", b=32)

                if t > 0:
                    dve.wait_ge(tab_add, 2 * t)
                tt_(ab(rot[:, t % 2, 0]), hi_[0], lo_[0])
                tt_(ab(rot_m[:, 0]), hi_[1], lo_[1])
                tt_(ab(rot[:, t % 2, 1]), hi_[1], lo_[0])
                put(tt_(ab(rot_m[:, 1]), hi_[0], lo_[1]), tab_mul)

            table_step(0)
            for t in range(LANE_T):
                co, si = rot[:, t % 2, 0], rot[:, t % 2, 1]
                dve.wait_ge(tab_add, 2 * t + 2)
                dve.wait_ge(px_full, XUSE[("br", t)] + 1)
                dve.wait_ge(py_full, YUSE[("bi", t)] + 1)
                if t > 0:
                    dve.wait_ge(x_mul, t)
                tt_(vz[:, 0], px[:], co)
                tt_(vz[:, 1], py[:], co)
                tt_(v_m[:, 0], py[:], si).then_inc(py_free, 1)
                tt_(v_m[:, 1], px[:], si).then_inc(px_free, 1)
                px_read(dve, ("br", t))
                if t + 1 < LANE_T:
                    table_step(t + 1)
                dve.wait_ge(in_add, 2 * t + 2)
                mag = lane[:, L_MAG, t:t + 1].broadcast_to([P, T])
                dve.tensor_tensor_scan(vz[:, 0], mag, vz[:, 0], 0.0, ALU.mult, ALU.add)
                put(dve.tensor_tensor_scan(vz[:, 1], mag, vz[:, 1], 0.0, ALU.mult, ALU.add), scanned)
                if t >= 2:
                    dve.wait_ge(y_mm, t - 1)
                x2 = xs[:, t % 2]
                tt_(x2[:, 0], vz[:, 0], co)
                stt(x2[:, 1], vz[:, 1], -1.0, si)
                put(tt_(x2[:, 2], vz[:, 0], si), out_mul)
                if t % 4 == 0 and t > 0:
                    dve.wait_ge(y_mm, t)
                    k = t // 4 - 1
                    put(stt(y5[:, k], hid[:, k], par("ssm_d", k), ps[k % 2][:, 0, :], ALU.mult, ALU.add), ya_free)
            dve.wait_ge(y_mm, LANE_T)
            put(stt(y5[:, 3], hid[:, 3], par("ssm_d", 3), ps[1][:, 0, :], ALU.mult, ALU.add), ya_free)

            def maximum(use, w, i, s):
                bank = ps_ready(dve, use)
                put(dve.tensor_reduce(s[:, i % 2, 0:2], bank[:, :, 0:w], AX.X, ALU.max, negate=True), maxed)

            def combine(h, i):
                w, s = P * (i + 1), soft[:, i % 2]
                ps_read(dve, ("s", h, i))
                link(dve.reciprocal(s[:, 4:6], s[:, 2:4]))
                link(ts(s[:, 5:6], s[:, 5:6], lam_t[:, 5:6], ALU.mult))
                link(ts(pr[:, i % 2, 1, 0:w], pr[:, i % 2, 1, 0:w], s[:, 5:6], ALU.mult))
                n = 4 * h + i
                if n >= 2:
                    ps_ready(dve, ("t", (n - 2) // 4, (n - 2) % 4))
                put(stt(pa[:, i % 2, 0:w], pr[:, i % 2, 0, 0:w], s[:, 4:5], pr[:, i % 2, 1, 0:w], ALU.mult, ALU.add), combed)

            def turned(h, i):
                w = P * (i + 1)
                bank = ps_ready(dve, ("t", h, i))
                dve.tensor_copy(pt[:, 0:i + 1, P * i:w], bank[:, 0, 0:w].rearrange("p (j q) -> p j q", q=P))\
                    .then_inc(ps_free[SUSE[("t", h, i)] % 2], 1)
                ps_read(dve, ("t", h, i))

            def rope_step(h, name, n, ready, dst):
                evacuated(dve, (name, h))
                tt_(rope_a[:, 0], kq_raw[:, n], rtab[:, 0])
                dve.wait_ge(py_full, YUSE[("rot_" + name, h)] + 1)
                tt_(rope_a[:, 1], py[:], rtab[:, 1]).then_inc(py_free, 1)
                py_read(dve, ("rot_" + name, h))
                link(tt_(rope_a[:, 0], rope_a[:, 0], rope_a[:, 1], ALU.add))
                dve.wait_ge(ready, h + 1)
                put(tt_(dst[:, h % 2], rope_a[:, 0], kq_rs[:, n]), roped)

            dve.wait_ge(r_landed, 16)
            for h in range(HEADS + 2):
                g = h - 1
                attends = 0 <= g < HEADS
                if attends:
                    maximum(("s", g, 0), P, 0, soft)
                    maximum(("s", g, 1), 2 * P, 1, soft)
                    combine(g, 0)
                    combine(g, 1)
                if h >= 2:
                    py_read(dve, ("pv", h - 2))
                    dve.wait_ge(rs_o, h - 1)
                    put(stt(hid[:, h - 2], hid[:, h - 2], lam_t[:, 6:7], kq_rs[:, 2]), o_done)
                if attends:
                    turned(g, 1)
                    maximum(("s", g, 2), 3 * P, 2, soft)
                    maximum(("s", g, 3), 4 * P, 3, soft)
                if h < HEADS:
                    rope_step(h, "k", 0, rs_k, kk)
                if attends:
                    combine(g, 2)
                    combine(g, 3)
                if h < HEADS:
                    rope_step(h, "q", 1, rs_q, qq)
                if attends:
                    turned(g, 3)

            for t in range(SSM_T):
                split_lo(SPLIT["g"] + t, x_lo[:, t], y5[:, t], x_hi[:, t])
            for m in range(5):
                if m < 4:
                    evacuated(dve, ("glu", m))
                    put(tt_(nrm[:, m % 2], y5[:, m], sqr[:, m % 2]), src_done)
                if m > 0:
                    split_lo(SPLIT["s"] + m - 1, x_lo[:, 3 + m], nrm[:, (m - 1) % 2], x_hi[:, 3 + m])
            for m in range(KT):
                free(tt_(mix(m), done(("ssm", m)), gates[:, 8 + m]), ("ssm", m))
            for h in range(HEADS):
                split_lo(SPLIT["o"] + h, x_lo[:, h], hid[:, h], x_hi[:, h])
            for m in range(KT + 1):
                if m < KT:
                    free(tt_(nrm[:, m % 2], done(("attn", m)), gates[:, m]), ("attn", m))
                    evacuated(dve, ("attn", m))
                    put(tt_(mix(m), mix(m), nrm[:, m % 2], ALU.add), src_done)
                if m > 0:
                    split_lo(SPLIT["mix"] + m - 1, mix_lo[:, m - 1], mix(m - 1), mix_hi[:, m - 1])
            dve.wait_ge(x2_landed, 16)
            for m in range(KT):
                free(tt_(hid[:, m], hid[:, m], done(("out", m)), ALU.add), ("out", m))
                scaled("norm2", m, "norm2")
            root_ready(2)

            order = ffn_order(FF1)
            for kind, c in order:
                a, b = chunks_of(FF1)[c]
                if kind == "up":
                    for i in range(a, b):
                        for n, (name, col) in enumerate((("fgate", i), ("fval", FF1 + i))):
                            free(tt_(cu[:, n], done((name, i)), rstd[:]), (name, i))
                            if n == 0 and i > a:
                                split_lo(SPLIT["act"] + i - 1, act_lo[:, c % 2, i - 1 - a], hsrc[:, (i - 1) % 2],
                                         act_hi[:, c % 2, i - 1 - a])
                            dve.wait_ge(cnv_act, 2 * i + n + 1)
                            link(stt(cnv[:, n, 1:T], cu[:, n, 0:T - 1], par("cw", 44 + col), cnv[:, n, 1:T], ALU.mult, ALU.add))
                            put(stt(cnv[:, n, 2:T], cu[:, n, 0:T - 2], par("cw", col), cnv[:, n, 2:T], ALU.mult, ALU.add),
                                cnv_done)
                        dve.wait_ge(silu_done, i + 1)
                        put(tt_(hsrc[:, i % 2], cnv[:, 0], cnv[:, 1]), src_done)
                    split_lo(SPLIT["act"] + b - 1, act_lo[:, c % 2, b - 1 - a], hsrc[:, (b - 1) % 2],
                             act_hi[:, c % 2, b - 1 - a])
                else:
                    for m in range(KT):
                        if c > 0:
                            evacuated(dve, ("down", c - 1, m))
                        free(tt_(hid[:, m], hid[:, m], done(("down", c, m)), ALU.add), ("down", c, m))
                        if (kind, c) == order[-1]:
                            scaled("norm3", m, "mix_pre")
            root_ready(3)

            for t in range(LRU_T):
                free(tt_(sqr[:, t % 2], done(("xr", t)), rstd[:]), ("xr", t))
                dve.wait_ge(xc_act, t + 1)
                for d in (1, 2, 3):
                    put(stt(xc[:, t, d:T], sqr[:, t % 2, 0:T - d], par("cw2", 4 * (3 - d) + t), xc[:, t, d:T], ALU.mult,
                            ALU.add), xc_done)
            free(tt_(kk2[:, 0], done(("k2", 0)), rstd[:]), ("k2", 0))
            free(stt(qq2[:, 0], done(("q2", 0)), 0.125, rstd[:]), ("q2", 0))
            for t in range(LRU_T):
                dve.wait_ge(la_done, t + 1)
                link(tt_(nrm[:, t % 2], ra[:, t], ra[:, t]))
                put(stt(tt[:, t], nrm[:, t % 2], 1.0, tt[:, t], ALU.add, ALU.mult), tt_dve)
                py_read(dve, ("ig", t))
                link(tt_(ii[:, t], ii[:, t], xc[:, t]))
            for t in range(LRU_T):
                dve.wait_ge(tt_act, t + 1)
                link(tt_(ii[:, t], ii[:, t], tt[:, t]))
                put(dve.tensor_tensor_scan(xc[:, t], ra[:, t], ii[:, t], 0.0, ALU.mult, ALU.add), lru_h)
            def combine2(j, i):
                w, s = P * (i + 1), soft2[:, i % 2]
                ps_read(dve, ("p", j, i))
                for c in range(2):
                    link(dve.tensor_tensor_reduce(pr2[:, i % 2, c, 0:w], pr2[:, i % 2, c, 0:w], mult[:, T - w:T], 1.0, 0.0,
                                                  ALU.mult, ALU.add, s[:, 2 + c:3 + c]))
                link(dve.reciprocal(s[:, 4:6], s[:, 2:4]))
                ts(pr2[:, i % 2, 0, 0:w], pr2[:, i % 2, 0, 0:w], s[:, 4:5], ALU.mult)
                put(ts(pr2[:, i % 2, 1, 0:w], pr2[:, i % 2, 1, 0:w], s[:, 5:6], ALU.mult), combed)

            def turned2(j, i):
                w = P * (i + 1)
                bank = ps_ready(dve, ("t2", j, i))
                dve.tensor_copy(pt2[:, i % 2, :, 0:i + 1, :], bank[:, :, 0:w].rearrange("p c (b q) -> p c b q", q=P))\
                    .then_inc(ps_free[SUSE[("t2", j, i)] % 2], 1)
                ps_read(dve, ("t2", j, i))

            for j in range(PAIRS + 1):
                g = j - 1
                if 0 < j < PAIRS:
                    free(tt_(kk2[:, j % 2], done(("k2", j)), rstd[:]), ("k2", j))
                if g >= 0:
                    maximum(("p", g, 0), P, 0, soft2)
                    maximum(("p", g, 1), 2 * P, 1, soft2)
                    combine2(g, 0)
                    combine2(g, 1)
                if 0 < j < PAIRS:
                    free(stt(qq2[:, j % 2], done(("q2", j)), 0.125, rstd[:]), ("q2", j))
                if g >= 0:
                    turned2(g, 1)
                    maximum(("p", g, 2), 3 * P, 2, soft2)
                    maximum(("p", g, 3), 4 * P, 3, soft2)
                    combine2(g, 2)
                    combine2(g, 3)
                if j < PAIRS:
                    free(tt_(v_raw2[:], done(("v2", j)), rstd[:]), ("v2", j))
                if g >= 0:
                    turned2(g, 3)
                if j < PAIRS:
                    free(tt_(sqr[:, j % 2], done(("gr", j)), rstd[:]), ("gr", j))
                    dve.wait_ge(lru_h, j + 1)
                    dve.wait_ge(gelu2_done, j + 1)
                    put(tt_(nrm[:, j % 2], xc[:, j], sqr[:, j % 2]), src_done)
                    split_lo(SPLIT["rec"] + j, mx2_lo[:, 4 + j], nrm[:, j % 2], mx2_hi[:, 4 + j])
                if g >= 0:
                    dve.wait_ge(pv2_hi, g + 1)
                    tt_(mx2_lo[:, g], py[:], mx2_hi[:, g].bitcast(F32), ALU.subtract).then_inc(py_free, 1)
                    py_read(dve, ("pv2", g))

            root_ready(4)
            for m in range(KT):
                link(stt(nrm_t[:], acc[:, m], par("mix_post", m), rstd[:]))
                put(tt_(hid[:, m], hid[:, m], nrm_t[:], ALU.add), res_done)
                scaled("norm4", m, "mlp_pre")
            order = ffn_order(FF2)
            for kind, c in order:
                a, b = chunks_of(FF2)[c]
                if kind == "up":
                    for i in range(a, b):
                        evacuated(dve, ("ff", i))
                        put(tt_(nrm[:, i % 2], rel[:], rel[:]), src_done)
                        split_lo(SPLIT["act2"] + i, act2_lo[:, c % 2, i - a], nrm[:, i % 2], act2_hi[:, c % 2, i - a])
                elif c > 0:
                    for m in range(KT):
                        evacuated(dve, ("down2", c - 1, m))
                        free(tt_(acc[:, m], acc[:, m], done(("down2", c, m)), ALU.add), ("down2", c, m))
                        if (kind, c) == order[-1]:
                            if m == 0:
                                root_ready(5)
                            put(tt_(acc[:, m], acc[:, m], rstd_sq[:]), acc_done)
            root_ready(6)
            for m in range(KT):
                link(stt(nrm[:, m % 2], acc[:, m], par("mlp_post", m), rstd[:]))
                put(tt_(hid[:, m], hid[:, m], nrm[:, m % 2], ALU.add), fin_done)


def _units(i):
    import numpy as np

    def tiles(w, m):
        return w[:, m * P:(m + 1) * P].reshape(-1, P, P).transpose(1, 0, 2)

    w_in, w_up, w_down = i["w_in"][0], i["w_up"][0], i["w_down"][0]
    w_in2, f_in, f_out = i["w_in_2"][0], i["w_ff_in_2"][0], i["w_ff_out_2"][0]

    def piece(name):
        kind, n = name[0], name[1]
        if kind in ("glu", "ssm"):
            w = i["w_glu"][0] if kind == "glu" else i["w_ssm_proj"][0]
            return np.concatenate([tiles(w, 2 * n), tiles(w, 2 * n + 1)], axis=1)
        if kind in ("down", "down2"):
            a, b = chunks_of(FF1 if kind == "down" else FF2)[n]
            w = (w_down if kind == "down" else f_out)[a * P:b * P]
            return tiles(w, name[2])
        w, m = {"q": (w_in, n), "k": (w_in, 8 + n), "v": (w_in, 16 + n), "u": (w_in, 24 + n), "gate": (w_in, 28 + n),
                "attn": (i["w_attn_proj"][0], n), "out": (i["w_out"][0], n), "fgate": (w_up, n),
                "fval": (w_up, FF1 + n), "q2": (w_in2, n), "k2": (w_in2, 4 + n), "v2": (w_in2, 8 + n),
                "xr": (w_in2, 12 + n), "gr": (w_in2, 16 + n), "out2": (i["w_out_2"][0], n), "ff": (f_in, n)}[kind]
        return tiles(w, m)

    out = np.zeros((len(UNITS), P, KT * P), np.float32)
    for n, name in enumerate(UNITS):
        p = piece(name)
        out[n, :, :p.shape[1] * P] = p.reshape(P, -1)
    return out


def _constants():
    import numpy as np

    c = np.zeros((P, N_CONST), np.float32)
    c[:, C_ID:C_ID + P] = np.eye(P)
    c[:, C_ONES:C_ONES + P] = 1
    c[:64, C_BLK:C_BLK + 64] = 1
    c[64:, C_BLK + 64:C_BLK + 128] = 1
    for b in (0, 64):
        for d in range(32):
            c[b + d + 32, C_ROT + b + d] = -1
            c[b + d, C_ROT + b + d + 32] = 1
    q, k = np.arange(P)[:, None], np.arange(T)[None, :]
    dist = q + (T - P) - k
    count = ((dist >= 0) & (dist <= 128)).astype(int) + ((dist >= 0) & (dist % 4 == 0)) + ((dist >= 0) & (dist % 16 == 0))
    c[:, C_MULT:C_MULT + T] = count
    c[:, C_EPS], c[:, C_EPS64], c[:, C_HPI] = EPS, 64 * EPS, np.pi / 2
    m = np.zeros((P, N_MASK), np.float32)
    m[:, M_ID:M_ID + P] = np.eye(P)
    m[:, M_TRI:M_TRI + P] = np.where(np.arange(P)[None, :] <= q, 0, -1e30)
    m[:, M_UNI:M_UNI + T] = np.where(count > 0, 0, -1e30)
    inv = (1.0 / (10000.0 ** (np.arange(0, 64, 2, dtype=np.float32) / 64))).astype(np.float32)
    ang = (np.arange(T, dtype=np.float32)[None, :] * inv[:, None]).astype(np.float32)
    rope = np.stack([np.tile(np.cos(ang.astype(np.float64)), (4, 1)), np.tile(np.sin(ang.astype(np.float64)), (4, 1))], axis=1)
    return c, m, rope.astype(np.float32)


def _parameters(i):
    import numpy as np

    def cols(a):
        return np.asarray(a).reshape(-1, P).T

    def lanes(a):
        return np.asarray(a).reshape(LANE_T, P).T

    lam = np.zeros((P, 4), np.float32)
    for n, name in enumerate(("lambda_q1", "lambda_k1", "lambda_q2", "lambda_k2")):
        lam[:64, n] = i[name][0]
    parts = {
        "norm1": cols(i["norm1_gain"][0]), "norm2": cols(i["norm2_gain"][0]),
        "mix_pre": cols(i["mix_norm_pre_2"][0]), "mix_post": cols(i["mix_norm_post_2"][0]),
        "mlp_pre": cols(i["mlp_norm_pre_2"][0]), "mlp_post": cols(i["mlp_norm_post_2"][0]),
        "qg": cols(np.tile(i["q_norm_gain"][0], 2)), "kg": cols(np.tile(i["k_norm_gain"][0], 2)),
        "subln": cols(i["subln_gain"][0]), "lam": lam,
        "cw": np.concatenate([cols(i["conv_w"][0][j]) for j in range(3)], axis=1), "cb": cols(i["conv_b"][0]),
        "b_glu": cols(i["b_glu"][0]), "ssm_d": cols(i["ssm_d"][0]),
        "a_re": lanes(i["ssm_a_re"][0]), "a_im": lanes(i["ssm_a_im"][0]),
        "log_dt": lanes(np.repeat(i["ssm_log_dt"][0], 64)),
        "cw2": np.concatenate([cols(i["conv_w_2"][0][j]) for j in range(4)], axis=1), "cb2": cols(i["conv_b_2"][0]),
        "b_r": cols(i["b_rgate_2"][0]), "b_i": cols(i["b_igate_2"][0]), "lru": cols(i["lru_lambda_2"][0]),
    }
    out = np.zeros((P, N_PARAM), np.float32)
    for name, (a, w) in PARAMS.items():
        out[:, a:a + w] = parts[name]
    b = np.zeros((P, SSM_T, 2, P), np.float32)
    c = np.zeros((P, 2, LANE_T, 32), np.float32)
    for n, (bn, cn) in enumerate((("ssm_b_re", "ssm_c_re"), ("ssm_b_im", "ssm_c_im"))):
        for g in range(32):
            h = g % 2
            b[16 * (g % 8):16 * (g % 8) + 16, g // 8, n, 64 * h:64 * h + 64] = i[bn][0][g].T
            c[64 * h:64 * h + 64, n, g // 2, 16 * h:16 * h + 16] = i[cn][0][g].T
    lru = np.zeros((P, 2, LRU_T, P), np.float32)
    for n, name in enumerate(("w_rgate_2", "w_igate_2")):
        for k in range(8):
            h = k % 2
            lru[64 * h:64 * h + 64, n, k // 2, 64 * h:64 * h + 64] = i[name][0][k]
    return out, b, c.reshape(P, 2, LANE_T * 32), lru


def kernel(**inputs):
    import concourse.bacc as _bacc
    import numpy as _np
    from concourse.bass_utils import run_bass_kernel_spmd as _run

    i = {n: _np.asarray(a) for n, a in inputs.items()}
    consts, masks, rope = _constants()
    params, ssm_b, ssm_c, lru = _parameters(i)
    arrays = {
        "weights": _units(i), "x": _np.ascontiguousarray(i["x"][0].T.reshape(KT, P, T).transpose(1, 0, 2)),
        "consts": consts, "rope": rope, "masks": masks, "params": params, "ssm_b": ssm_b, "ssm_c": ssm_c, "lru_w": lru,
    }
    nc = _bacc.Bacc("TRN2", target_bir_lowering=False, num_devices=1)
    args = [nc.dram_tensor(n, a.shape, mybir.dt.from_np(a.dtype), kind="ExternalInput").ap() for n, a in arrays.items()]
    args.append(nc.dram_tensor("out", (P, KT, T), F32, kind="ExternalOutput").ap())
    build(nc, *args)
    got = _run(nc, [arrays], core_ids=[0]).results[0]["out"]
    return got.transpose(1, 0, 2).reshape(D, T).T[None]
```

```python
from contextlib import ExitStack

import concourse.bass as bass
from concourse import mybir

P = 128
T = 512
D = 1024
KT = D // P
HEADS = 8
QB = T // P
FF1 = 2816 // P
FF2 = 4096 // P
SSM_T = 512 // P
LANE_T = 2048 // P
PAIRS = 4
LRU_T = 512 // P
CHUNK = 8
EPS = 1e-6
LAM_INIT = 0.8 - 0.6
TWO_PI = 6.283185307179586
RING = 4
BIG = 12582912.0

F32 = mybir.dt.float32
F32R = mybir.dt.float32r
BF16 = mybir.dt.bfloat16
ALU = mybir.AluOpType
ACT = mybir.ActivationFunctionType
AX = mybir.AxisListType

C_ID, C_ONES, C_BLK, C_ROT, C_MULT, C_EPS, C_EPS64, C_HPI = 0, 128, 256, 384, 512, 1024, 1025, 1026
N_CONST = 1028
M_ID, M_TRI, M_UNI = 0, 128, 256
N_MASK = 256 + 512
PARAMS = {}
_at = 0
for _n, _w in (("norm1", 8), ("norm2", 8), ("mix_pre", 8), ("mix_post", 8), ("mlp_pre", 8), ("mlp_post", 8),
               ("qg", 1), ("kg", 1), ("subln", 1), ("lam", 4), ("cw", 3 * 44), ("cb", 44), ("b_glu", 4),
               ("ssm_d", 4), ("a_re", 16), ("a_im", 16), ("log_dt", 16), ("cw2", 16), ("cb2", 4),
               ("b_r", 4), ("b_i", 4), ("lru", 4)):
    PARAMS[_n] = (_at, _w)
    _at += _w
N_PARAM = _at


def chunks_of(tiles):
    return [(a, min(a + CHUNK, tiles)) for a in range(0, tiles, CHUNK)]


def ffn_order(tiles):
    n = len(chunks_of(tiles))
    out = [("up", 0)]
    for c in range(1, n):
        out += [("up", c), ("down", c - 1)]
    return out + [("down", n - 1)]


def unit_order():
    u = [("u", t) for t in range(SSM_T)] + [("gate", g) for g in range(16)]
    for h in range(HEADS):
        u += [("k", h), ("q", h), ("v", h)]
    u += [("glu", n) for n in range(2)] + [("ssm", n) for n in range(4)]
    u += [("attn", m) for m in range(KT)] + [("out", m) for m in range(KT)]
    for kind, c in ffn_order(FF1):
        a, b = chunks_of(FF1)[c]
        u += [(s, i) for i in range(a, b) for s in ("fgate", "fval")] if kind == "up" else \
            [("down", c, m) for m in range(KT)]
    u += [("xr", t) for t in range(4)]
    for j in range(PAIRS):
        u += [("k2", j), ("q2", j), ("v2", j)] + [("gr", j - 1)] * (0 < j < 3)
    u += [("gr", 2), ("gr", 3)]
    u += [("out2", m) for m in range(KT)]
    for kind, c in ffn_order(FF2):
        a, b = chunks_of(FF2)[c]
        u += [("ff", i) for i in range(a, b)] if kind == "up" else [("down2", c, m) for m in range(KT)]
    return u


UNITS = unit_order()
UNIT = {name: n for n, name in enumerate(UNITS)}
TILE = {}
TILES_AFTER = []
_o = 0
for _n in UNITS:
    if _n[0] in ("glu", "ssm"):
        TILE[(_n[0], 2 * _n[1])] = _o
        TILE[(_n[0], 2 * _n[1] + 1)] = _o + 1
        _o += 2
    else:
        TILE[_n] = _o
        _o += 1
    TILES_AFTER.append(_o)

SPLIT = {}
_o = 0
for _n, _w in (("norm1", 8), ("g", 4), ("s", 4), ("o", 8), ("mix", 8), ("norm2", 8), ("act", FF1),
               ("norm3", 8), ("rec", 4), ("norm4", 8), ("act2", FF2)):
    SPLIT[_n] = _o
    _o += _w


GR_AT = [[], [0], [1], [], [2, 3]]

SRC = {}
_o = 0
for _n, _w in (("norm1", 8), ("s", 4), ("mix", 8), ("norm2", 8), ("act", FF1), ("norm3", 8), ("rec", 4),
               ("act2", FF2)):
    SRC[_n] = _o
    _o += _w

(L_DT, L_Z, L_TH, L_N, L_R, L_MAG, L_TANH, L_S, L_C, L_SIN, L_CM1, L_COS, L_NR, L_NI, L_CR, L_CI,
 L_T1, L_T2, L_T3) = range(19)
L_POW = 19
GATES_FIRST, GATES_LAST = 3, 1
GATE_STEPS = (16 - GATES_FIRST - GATES_LAST) * KT // LANE_T
GATE_AT = [[GATES_FIRST + n for n in range(16 - GATES_FIRST - GATES_LAST) if (n * KT + KT - 1) // GATE_STEPS == t]
           for t in range(LANE_T)]
PI_1, PI_2, PI_3 = 6.28125, 0.0019350051879882812, 3.0199159795074593e-07


def aux_order():
    x, y, s = [("stat", 1), "lam"], [], []
    for t in range(LANE_T):
        x.append(("br", t))
        y.append(("bi", t))
    for h in range(HEADS + 2):
        g = h - 1
        if 0 <= g < HEADS:
            x.append(("vt", g))
            s += [("s", g, 0), ("s", g, 1)]
        if h >= 2:
            y.append(("pv", h - 2))
        if 0 <= g < HEADS:
            s += [("t", g, 0), ("t", g, 1)]
        if h < HEADS:
            x.append(("ssq_k", h))
            y.append(("rot_k", h))
        if h >= 2:
            x.append(("ssq_o", h - 2))
        if 0 <= g < HEADS:
            s += [("s", g, 2), ("s", g, 3)]
        if h < HEADS:
            x.append(("ssq_q", h))
            y.append(("rot_q", h))
        if 0 <= g < HEADS:
            s += [("t", g, 2), ("t", g, 3)]
    x += [("stat", 2), ("stat", 3)]
    for t in range(LRU_T):
        x.append(("rg", t))
        y.append(("ig", t))
    for j in range(PAIRS + 1):
        if j > 0:
            for i in (0, 2):
                s += [("p", j - 1, i), ("p", j - 1, i + 1), ("t2", j - 1, i), ("t2", j - 1, i + 1)]
            y.append(("pv2", j - 1))
        if j < PAIRS:
            x.append(("vt2", j))
    x += [("stat", n) for n in (4, 5, 6)]
    return x, y, s


EXPS = {name: n for n, name in enumerate(u for u in aux_order()[2] if u[0] in ("s", "p"))}
XUSE, YUSE, SUSE = ({name: n for n, name in enumerate(names)} for names in aux_order())



def build(nc, weights, x_dram, consts, rope, masks, params, ssm_b, ssm_c, lru_w, out):
    with ExitStack() as ctx:
        def sb(name, shape, dt=F32, scope=ctx):
            return scope.enter_context(nc.sbuf_tensor(name, shape, dt))

        def sem(name):
            return ctx.enter_context(nc.semaphore(name))

        w_raw = sb("w_raw", [P, RING, KT, P])
        w_hi = sb("w_hi", [P, RING, KT, P], F32R)
        w_lo = sb("w_lo", [P, RING, KT, P], F32R)
        x_hi = sb("x_hi", [P, KT, T], F32R)
        x_lo = sb("x_lo", [P, KT, T], F32R)
        cst = sb("cst", [P, N_CONST])
        msk = sb("msk", [P, N_MASK], BF16)
        prm = sb("prm", [P, N_PARAM])
        hid = sb("hid", [P, KT, T])
        nrm = sb("nrm", [P, 2, T])
        sqr = sb("sqr", [P, 2, T])
        rstd = sb("rstd", [P, T])
        lam_t = sb("lam_t", [P, 8])
        lcf = sb("lcf", [P, 8, LRU_T])

        with ExitStack() as first:
            gates = sb("gates", [P, 16, T], scope=first)
            y5 = sb("y5", [P, SSM_T, T], scope=first)
            with ExitStack() as s:
                b_in = sb("b_in", [P, SSM_T, 2, P], scope=s)
                c_out = sb("c_out", [P, 2, LANE_T * 32], scope=s)
                lane = sb("lane", [P, L_POW + 9, LANE_T], scope=s)
                powers = sb("powers", [P, 2, LANE_T, 64], scope=s)
                rot = sb("rot", [P, 3, 2, T], scope=s)
                rot_m = sb("rot_m", [P, 2, T // 2], scope=s)
                v_m = sb("v_m", [P, 2, T], scope=s)
                xs = sb("xs", [P, 2, 4, T], scope=s)
            with ExitStack() as s:
                rtab = sb("rtab", [P, 2, T], scope=s)
                kq_raw = sb("kq_raw", [P, 2, T], scope=s)
                kq_rs = sb("kq_rs", [P, 3, T], scope=s)
                rope_a = sb("rope_a", [P, 2, T], scope=s)
                kk = sb("kk", [P, 2, T], scope=s)
                qq = sb("qq", [P, 2, T], scope=s)
                v_raw = sb("v_raw", [P, T], scope=s)
                vv = sb("vv", [P, 2, QB, P], scope=s)
                pr = sb("pr", [P, 2, 2, T], scope=s)
                pa = sb("pa", [P, 2, T], scope=s)
                pt = sb("pt", [P, QB, T], scope=s)
                soft = sb("soft", [P, 2, 8], scope=s)
            mix_hi = sb("mix_hi", [P, KT, T], F32R, scope=first)
            mix_lo = sb("mix_lo", [P, KT, T], F32R, scope=first)
        with ExitStack() as s:
            act_hi = sb("act_hi", [P, 2, CHUNK, T], F32R, scope=s)
            act_lo = sb("act_lo", [P, 2, CHUNK, T], F32R, scope=s)
            cnv = sb("cnv", [P, 2, T], scope=s)
            hsrc = sb("hsrc", [P, 2, T], scope=s)
            cu = sb("cu", [P, 2, T], scope=s)
        acc = sb("acc", [P, KT, T])
        with ExitStack() as s:
            mx2_hi = sb("mx2_hi", [P, KT, T], F32R, scope=s)
            mx2_lo = sb("mx2_lo", [P, KT, T], F32R, scope=s)
            xc = sb("xc", [P, LRU_T, T], scope=s)
            tt = sb("tt", [P, LRU_T, T], scope=s)
            lru_b = sb("lru_b", [P, 2, LRU_T, P], scope=s)
            kk2 = sb("kk2", [P, 2, T], scope=s)
            qq2 = sb("qq2", [P, 2, T], scope=s)
            v_raw2 = sb("v_raw2", [P, T], scope=s)
            vv2 = sb("vv2", [P, QB, P], scope=s)
            soft2 = sb("soft2", [P, 2, 8], scope=s)
        ra, ii = acc[:, 0:4], acc[:, 4:8]
        pr2 = acc[:, 0:4].rearrange("p (n c) t -> p n c t", c=2)
        pt2 = acc[:, 4:8].rearrange("p (n c) (b q) -> p n c b q", c=2, q=P)
        with ExitStack() as s:
            act2_hi = sb("act2_hi", [P, 2, CHUNK, T], F32R, scope=s)
            act2_lo = sb("act2_lo", [P, 2, CHUNK, T], F32R, scope=s)
            rel = sb("rel", [P, T], scope=s)
            rstd_sq = sb("rstd_sq", [P, T], scope=s)
            nrm_t = sb("nrm_t", [P, T], scope=s)

        vz = hid[:, 4:8].rearrange("p (n c) t -> p n c t", c=2)
        sq_sum = rstd
        c_in = gates[:, 14:16, :]
        msk_raw = gates[:, 0:2, :].rearrange("p a t -> p (a t)")[:, 0:N_MASK]
        kq_sq = [sqr[:, 0], sqr[:, 1], nrm[:, 0]]

        def mix(m):
            return gates[:, 8 + m]

        def psum(name, shape):
            return ctx.enter_context(nc.psum_tensor(name, shape, F32))

        pg = [psum(f"pg{b}", [P, T]) for b in range(2)]
        px, py = psum("px", [P, T]), psum("py", [P, T])
        ps = [psum(f"ps{b}", [P, 2, T]) for b in range(2)]

        w_landed = [sem(f"w_landed{s}") for s in range(RING)]
        hi_done, lo_done = sem("hi_done"), sem("lo_done")
        tile_done = sem("tile_done")
        pg_free = [sem(f"pg_free{b}") for b in range(2)]
        px_full, px_free = sem("px_full"), sem("px_free")
        py_full, py_free = sem("py_full"), sem("py_free")
        ps_full, ps_free = sem("ps_full"), [sem(f"ps_free{b}") for b in range(2)]
        src_done, xhi_done, xlo_done = sem("src_done"), sem("xhi_done"), sem("xlo_done")
        x_landed = [sem(f"x_landed{n}") for n in range(4)]
        m_landed = sem("m_landed")
        c_landed, p_landed, s_landed, r_landed, l_landed, x2_landed = (
            sem(n) for n in ("c_landed", "p_landed", "s_landed", "r_landed", "l_landed", "x2_landed"))
        stored = sem("stored")
        sq_done, sq_read, rstd_ready = sem("sq_done"), sem("sq_read"), sem("rstd_ready")
        sq5_read, gained = sem("sq5_read"), sem("gained")
        lane_act, lane_dve, lam_dve = sem("lane_act"), sem("lane_dve"), sem("lam_dve")
        tab_act, tab_dve = sem("tab_act"), sem("tab_dve")
        in_add, scanned = sem("in_add"), sem("scanned")
        out_mul, x_mul, y_mm, ya_free = sem("out_mul"), sem("x_mul"), sem("y_mm"), sem("ya_free")
        gelu_done = sem("gelu_done")
        act_c, dve_c = sem("act_c"), sem("dve_c")
        roped, maxed, combed, o_sq, o_done = (sem(n) for n in ("roped", "maxed", "combed", "o_sq", "o_done"))
        rs_k, rs_q, rs_o = sem("rs_k"), sem("rs_q"), sem("rs_o")
        cnv_act, silu_done, res_done, fin_done = sem("cnv_act"), sem("silu_done"), sem("res_done"), sem("fin_done")
        fin_mul, fin_pool = sem("fin_mul"), sem("fin_pool")
        xc_act, xc_done, la_done, tt_dve, tt_act, lru_h = (sem(n) for n in ("xc_act", "xc_done", "la_done", "tt_dve", "tt_act", "lru_h"))
        pv2_hi, cnv_done, gelu2_done, acc_done = sem("pv2_hi"), sem("cnv_done"), sem("gelu2_done"), sem("acc_done")

        ident = cst[:, C_ID:C_ID + P]
        ones = cst[:, C_ONES:C_ONES + P]
        block_ones = cst[:, C_BLK:C_BLK + P]
        rotate = cst[:, C_ROT:C_ROT + P]
        mult = cst[:, C_MULT:C_MULT + T]
        ident_b = msk[:, M_ID:M_ID + P]

        def par(name, i=0):
            a, w = PARAMS[name]
            return prm[:, a + i:a + i + 1]

        def pars(name):
            a, w = PARAMS[name]
            return prm[:, a:a + w]

        def cc(i):
            return cst[:, i:i + 1]

        def evacuated(eng, name):
            eng.wait_ge(pg_free[TILE[name] % 2], TILE[name] // 2 + 1)

        def px_read(eng, name):
            eng.wait_ge(px_free, XUSE[name] + 1)

        def py_read(eng, name):
            eng.wait_ge(py_free, YUSE[name] + 1)

        def ps_read(eng, name):
            eng.wait_ge(ps_free[SUSE[name] % 2], SUSE[name] // 2 + 1)

        def ps_ready(eng, name):
            eng.wait_ge(ps_full, SUSE[name] + 1)
            return ps[SUSE[name] % 2]

        block = ctx.enter_context(nc.Block())

        @block.sync
        def _(sp):
            for n in range(4):
                sp.dma_start(hid[:, 2 * n:2 * n + 2], x_dram[:, 2 * n:2 * n + 2]).then_inc(x_landed[n], 16)
            def weights_to(u):
                sp.dma_start(w_raw[:, u], weights[u].rearrange("p (k m) -> p k m", k=KT)).then_inc(w_landed[u], 16)

            sp.dma_start(cst[:], consts).then_inc(c_landed, 16)
            weights_to(0)
            sp.dma_start(prm[:], params).then_inc(p_landed, 16)
            weights_to(1)
            sp.dma_start(msk_raw, masks).then_inc(m_landed, 16)
            sp.dma_start(b_in[:], ssm_b).then_inc(s_landed, 16)
            sp.dma_start(c_in[:], ssm_c).then_inc(s_landed, 16)
            weights_to(2)
            weights_to(3)
            full = len(UNITS) // RING
            with sp.Fori(1, full) as r:
                for s in range(RING):
                    sp.wait_ge(lo_done, r * RING + (s + 1 - RING))
                    sp.dma_start(w_raw[:, s], weights[r * RING + s].rearrange("p (k m) -> p k m", k=KT))\
                        .then_inc(w_landed[s], 16)
            for u in range(full * RING, len(UNITS)):
                sp.wait_ge(lo_done, u + 1 - RING)
                sp.dma_start(w_raw[:, u % RING], weights[u].rearrange("p (k m) -> p k m", k=KT))\
                    .then_inc(w_landed[u % RING], 16)
            for k in range(KT):
                sp.wait_ge(fin_pool if k % 2 else fin_done, k // 2 + 1)
                sp.dma_start(out[:, k], hid[:, k]).then_inc(stored, 16)
            sp.wait_ge(stored, 16 * KT)

        @block.gpsimd
        def _(pool):
            def lo(u, s):
                pool.wait_ge(hi_done, u + 1)
                pool.tensor_tensor(w_lo[:, s], w_raw[:, s], w_hi[:, s].bitcast(F32), ALU.subtract)\
                    .then_inc(lo_done, 1)

            g0 = UNIT[("gate", 0)]
            u = g0 + GATES_FIRST + 2
            for v in range(u):
                lo(v, v % RING)
            for t in range(LANE_T):
                v = vz[:, t % 2]
                px_read(pool, ("br", t))
                py_read(pool, ("bi", t))
                pool.tensor_tensor(v[:, 0], v[:, 0], v_m[:, 0], ALU.add).then_inc(in_add, 1)
                pool.tensor_tensor(v[:, 1], v[:, 1], v_m[:, 1], ALU.subtract).then_inc(in_add, 1)
                for _ in GATE_AT[t]:
                    lo(u, u % RING)
                    u += 1
                pool.wait_ge(scanned, t + 1)
                if t >= 2:
                    pool.wait_ge(y_mm, t - 1)
                pool.tensor_tensor(xs[:, t % 2, 2], v[:, 0], rot[:, t % 3, 1], ALU.mult)
                pool.tensor_tensor(xs[:, t % 2, 3], v[:, 1], rot[:, t % 3, 0], ALU.mult).then_inc(x_mul, 1)
            while u % RING:
                lo(u, u % RING)
                u += 1
            full = len(UNITS) // RING
            with pool.Fori(u // RING, full) as r:
                for s in range(RING):
                    lo(r * RING + s, s)
            for u in range(full * RING, len(UNITS)):
                lo(u, u % RING)
            for m in range(1, KT, 2):
                pool.wait_ge(fin_mul, m + 1)
                pool.tensor_tensor(hid[:, m], hid[:, m], acc[:, m], ALU.add).then_inc(fin_pool, 1)

        @block.tensor
        def _(pe):
            def tile(u, o, xh, xl, first_split=None, ks=range(KT), off=0, ahead_of=None):
                s, bank = u % RING, pg[o % 2]
                pe.wait_ge(lo_done, u + 1)
                if o >= 2:
                    pe.wait_ge(pg_free[o % 2], o // 2)
                ks = list(ks)
                for n, k in enumerate(ks):
                    if ahead_of is not None:
                        ahead_of(k)
                    if first_split is not None:
                        pe.wait_ge(xlo_done, first_split + n + 1)
                    wh, wl = w_hi[:, s, off + k, :], w_lo[:, s, off + k, :]
                    pe.matmul(bank[:], wh, xh(k), start=n == 0, stop=False)
                    pe.matmul(bank[:], wh, xl(k), start=False, stop=False)
                    last = pe.matmul(bank[:], wl, xh(k), start=False, stop=n == len(ks) - 1)
                last.then_inc(tile_done, 1)

            def named(name, xh, xl, **kw):
                tile(UNIT[name], TILE[name], xh, xl, **kw)

            def model(t_hi, t_lo):
                return (lambda k: t_hi[:, k]), (lambda k: t_lo[:, k])

            XH, XL = model(x_hi, x_lo)

            def x_use(name):
                if XUSE[name] > 0:
                    pe.wait_ge(px_free, XUSE[name])

            def y_use(name):
                if YUSE[name] > 0:
                    pe.wait_ge(py_free, YUSE[name])

            def s_use(name):
                n = SUSE[name]
                if n >= 2:
                    pe.wait_ge(ps_free[n % 2], n // 2)
                return ps[n % 2]

            def statistic(n):
                x_use(("stat", n))
                pe.wait_ge(sq_read, (KT - 2) * (n if n < 5 else n - 1))
                pe.matmul(px[:], ones, sq_sum[:], start=True, stop=False)
                pe.wait_ge(sq_done, KT * n)
                pe.matmul(px[:], ones, sqr[:, (KT - 1) % 2], start=False, stop=True).then_inc(px_full, 1)

            def stat5(k):
                if k == 0:
                    x_use(("stat", 5))
                pe.wait_ge(sq_done, KT * 4 + k + 1)
                pe.matmul(px[:], ones, sqr[:, k % 2], start=k == 0, stop=k == KT - 1)\
                    .then_inc(px_full if k == KT - 1 else sq5_read, 1)

            pe.wait_ge(c_landed, 16)
            statistic(1)
            x_use("lam")
            pe.wait_ge(lam_dve, 1)
            pe.matmul(px[:, 0:2], ones, lam_t[:, 0:2], start=True, stop=True).then_inc(px_full, 1)

            for t in range(SSM_T):
                named(("u", t), XH, XL, first_split=SPLIT["norm1"] if t == 0 else None)

            def y_step(t):
                j, bank = t % 4, ps[(t // 4) % 2]
                if j == 0 and t >= 8:
                    pe.wait_ge(ya_free, t // 4 - 1)
                pe.wait_ge(out_mul, t + 1)
                pe.wait_ge(x_mul, t + 1)
                rows = bank[32 * j:32 * j + 32, 0, :]
                for n in range(4):
                    last = pe.matmul(rows, c_out[:, n // 2, 32 * t:32 * t + 32], xs[:, t % 2, n], start=n == 0, stop=n == 3)
                last.then_inc(y_mm, 1)

            for g in range(GATES_FIRST):
                named(("gate", g), XH, XL)
            def gate_step(n):
                name = ("gate", GATES_FIRST + n // KT)
                k, o, slot = n % KT, TILE[name], UNIT[name] % RING
                bank = pg[o % 2]
                if k == 0:
                    pe.wait_ge(lo_done, UNIT[name] + 1)
                    pe.wait_ge(pg_free[o % 2], o // 2)
                wh, wl = w_hi[:, slot, k, :], w_lo[:, slot, k, :]
                pe.matmul(bank[:], wh, x_hi[:, k], start=k == 0, stop=False)
                pe.matmul(bank[:], wh, x_lo[:, k], start=False, stop=False)
                last = pe.matmul(bank[:], wl, x_hi[:, k], start=False, stop=k == KT - 1)
                if k == KT - 1:
                    last.then_inc(tile_done, 1)

            def input_step(t):
                j = t % 4
                for c, (bank, use, full, name) in enumerate(((px, x_use, px_full, "br"),
                                                             (py, y_use, py_full, "bi"))):
                    use((name, t))
                    pe.matmul(bank[:], b_in[32 * j:32 * j + 32, t // 4, c, :], hid[32 * j:32 * j + 32, t // 4, :],
                              start=True, stop=True).then_inc(full, 1)

            pe.wait_ge(s_landed, 32)
            evacuated(pe, ("u", SSM_T - 1))
            evacuated(pe, ("u", SSM_T - 2))
            input_step(0)
            for t in range(LANE_T):
                for n in range(GATE_STEPS * t, GATE_STEPS * (t + 1)):
                    gate_step(n)
                if t + 1 < LANE_T:
                    input_step(t + 1)
                if t > 0:
                    y_step(t - 1)
            for g in range(16 - GATES_LAST, 16):
                named(("gate", g), XH, XL)
            y_step(LANE_T - 1)

            def scores(h, i):
                bank, w = s_use(("s", h, i)), P * (i + 1)
                if h == 0 and i == 0:
                    pe.wait_ge(ya_free, SSM_T)
                pe.wait_ge(roped, 2 * h + 2)
                for c in range(2):
                    r = slice(64 * c, 64 * c + 64)
                    pe.matmul(bank[:, c, 0:w], qq[r, h % 2, P * i:P * i + P], kk[r, h % 2, 0:w], start=True, stop=False)
                    last = pe.matmul(bank[:, c, P * i:w], ident_b, msk[:, M_TRI:M_TRI + P], start=False, stop=True)
                last.then_inc(ps_full, 1)

            def turn(h, i):
                bank = s_use(("t", h, i))
                pe.wait_ge(combed, 4 * h + i + 1)
                for j in range(i + 1):
                    last = pe.transpose(bank[:, 0, P * j:P * j + P], pa[:, i % 2, P * j:P * j + P], ident)
                last.then_inc(ps_full, 1)

            def kq_sums(h, name, n):
                x_use(("ssq_" + name, h))
                evacuated(pe, (name, h))
                pe.matmul(px[:], block_ones, kq_sq[n], start=True, stop=True).then_inc(px_full, 1)
                y_use(("rot_" + name, h))
                pe.matmul(py[:], rotate, kq_raw[:, n], start=True, stop=True).then_inc(py_full, 1)

            def glu(m):
                tile(UNIT[("glu", m // 2)], TILE[("glu", m)], XH, XL, first_split=SPLIT["g"] if m == 0 else None,
                     ks=range(4), off=4 * (m % 2))

            for h in range(HEADS + 2):
                g = h - 1
                attends = 0 <= g < HEADS
                if h < HEADS:
                    named(("k", h), XH, XL)
                if attends:
                    x_use(("vt", g))
                    evacuated(pe, ("v", g))
                    for j in range(QB):
                        last = pe.transpose(px[:, P * j:P * j + P], v_raw[:, P * j:P * j + P], ident)
                    last.then_inc(px_full, 1)
                    scores(g, 0)
                    scores(g, 1)
                if h == HEADS + 1:
                    glu(2)
                if h >= 2:
                    y_use(("pv", h - 2))
                    px_read(pe, ("vt", h - 2))
                    ps_read(pe, ("t", h - 2, 2))
                    ps_read(pe, ("t", h - 2, 3))
                    for j in range(QB):
                        last = pe.matmul(py[:, P * j:T], vv[:, h % 2, j, :], pt[:, j, P * j:T],
                                         start=j == 0, stop=j == QB - 1)
                    last.then_inc(py_full, 1)
                if h < HEADS:
                    named(("q", h), XH, XL)
                if h == HEADS + 1:
                    glu(3)
                if attends:
                    turn(g, 0)
                    turn(g, 1)
                if h < HEADS:
                    kq_sums(h, "k", 0)
                if h >= 2:
                    x_use(("ssq_o", h - 2))
                    pe.wait_ge(o_sq, h - 1)
                    pe.matmul(px[:], ones, kq_sq[2], start=True, stop=True).then_inc(px_full, 1)
                if attends:
                    scores(g, 2)
                    scores(g, 3)
                if h < HEADS:
                    named(("v", h), XH, XL)
                    kq_sums(h, "q", 1)
                if h == HEADS:
                    glu(0)
                    glu(1)
                if attends:
                    turn(g, 2)
                    turn(g, 3)

            for m in range(KT):
                tile(UNIT[("ssm", m // 2)], TILE[("ssm", m)], lambda k: x_hi[:, 4 + k], lambda k: x_lo[:, 4 + k],
                     first_split=SPLIT["s"] if m == 0 else None, ks=range(4), off=4 * (m % 2))
            for m in range(KT):
                named(("attn", m), XH, XL, first_split=SPLIT["o"] if m == 0 else None)
            MH, ML = model(mix_hi, mix_lo)
            for m in range(KT):
                named(("out", m), MH, ML, first_split=SPLIT["mix"] if m == 0 else None)
            statistic(2)

            def ffn(tiles, ups, down, split_in, split_act, hi, lo_, stat_n):
                order = ffn_order(tiles)
                for kind, c in order:
                    a, b = chunks_of(tiles)[c]
                    if kind == "up":
                        for i in range(a, b):
                            for n, up in enumerate(ups):
                                first = i == 0 and n == 0
                                named((up, i), XH, XL, first_split=SPLIT[split_in] if first else None,
                                      ahead_of=stat5 if first and stat_n == 6 else None)
                    else:
                        for m in range(KT):
                            named((down, c, m), lambda k: hi[:, c % 2, k], lambda k: lo_[:, c % 2, k], ks=range(b - a),
                                  first_split=SPLIT[split_act] + a if m == 0 else None)
                statistic(stat_n)

            ffn(FF1, ("fgate", "fval"), "down", "norm2", "act", act_hi, act_lo, 3)

            def lru_gate(t):
                for c, (bank, use, full, name) in enumerate(((px, x_use, px_full, "rg"), (py, y_use, py_full, "ig"))):
                    use((name, t))
                    if c == 0:
                        pe.wait_ge(xc_done, 3 * t + 3)
                        pe.wait_ge(l_landed, 16)
                    pe.matmul(bank[:], lru_b[:, c, t], xc[:, t], start=True, stop=True).then_inc(full, 1)

            for t in range(LRU_T):
                named(("xr", t), XH, XL, first_split=SPLIT["norm3"] if t == 0 else None)
                if t > 0:
                    lru_gate(t - 1)

            def scores2(j, i):
                bank, w = s_use(("p", j, i)), P * (i + 1)
                for c in range(2):
                    r = slice(64 * c, 64 * c + 64)
                    pe.matmul(bank[:, c, 0:w], qq2[r, j % 2, P * i:P * i + P], kk2[r, j % 2, 0:w], start=True, stop=False)
                    last = pe.matmul(bank[:, c, 0:w], ident_b, msk[:, M_UNI + T - w:M_UNI + T], start=False, stop=True)
                last.then_inc(ps_full, 1)

            def turn2(j, i):
                bank = s_use(("t2", j, i))
                pe.wait_ge(combed, 4 * (HEADS + j) + i + 1)
                for c in range(2):
                    for b in range(i + 1):
                        last = pe.transpose(bank[:, c, P * b:P * b + P], pr2[:, i % 2, c, P * b:P * b + P], ident)
                last.then_inc(ps_full, 1)

            def values2(j, i):
                if i == 0:
                    y_use(("pv2", j))
                ps_read(pe, ("t2", j, i))
                for c in range(2):
                    r = slice(64 * c, 64 * c + 64)
                    for b in range(i + 1):
                        last = pe.matmul(py[r, P * i:P * i + P], vv2[:, b, r], pt2[:, i % 2, c, b, :],
                                         start=b == 0, stop=b == i)
                if i == QB - 1:
                    last.then_inc(py_full, 1)

            for j in range(PAIRS + 1):
                g = j - 1
                if j < PAIRS:
                    named(("k2", j), XH, XL)
                    if j == 0:
                        lru_gate(LRU_T - 1)
                if g >= 0:
                    evacuated(pe, ("k2", g))
                    evacuated(pe, ("q2", g))
                    scores2(g, 0)
                    scores2(g, 1)
                if j < PAIRS:
                    named(("q2", j), XH, XL)
                else:
                    named(("gr", 2), XH, XL)
                if g >= 0:
                    turn2(g, 0)
                    turn2(g, 1)
                    scores2(g, 2)
                    scores2(g, 3)
                if j < PAIRS:
                    named(("v2", j), XH, XL)
                else:
                    named(("gr", 3), XH, XL)
                if g >= 0:
                    px_read(pe, ("vt2", g))
                    values2(g, 0)
                    values2(g, 1)
                    turn2(g, 2)
                    turn2(g, 3)
                if 0 < j < 3:
                    named(("gr", g), XH, XL)
                if g >= 0:
                    values2(g, 2)
                    values2(g, 3)
                if j < PAIRS:
                    x_use(("vt2", j))
                    evacuated(pe, ("v2", j))
                    for b in range(QB):
                        last = pe.transpose(px[:, P * b:P * b + P], v_raw2[:, P * b:P * b + P], ident)
                    last.then_inc(px_full, 1)

            M2H, M2L = model(mx2_hi, mx2_lo)

            def last_pair(k):
                if k >= 4:
                    pe.wait_ge(xlo_done, SPLIT["rec"] + k - 3)
                if k == 3:
                    py_read(pe, ("pv2", PAIRS - 1))
            for m in range(KT):
                named(("out2", m), M2H, M2L, ks=(4, 5, 6, 7, 0, 1, 2, 3), ahead_of=last_pair if m == 0 else None)
            statistic(4)
            ffn(FF2, ("ff",), "down2", "norm4", "act2", act2_hi, act2_lo, 6)


        @block.scalar
        def _(act):
            sent = {}

            def put(ins, s):
                ins.then_inc(s, 1)
                sent[s.name] = sent.get(s.name, 0) + 1
                return sent[s.name]

            def hi(u):
                if u >= len(UNITS):
                    return
                s = u % RING
                act.wait_ge(w_landed[s], 16 * (u // RING + 1))
                if u >= RING:
                    act.wait_ge(tile_done, TILES_AFTER[u - RING])
                put(act.activation(w_hi[:, s], w_raw[:, s], ACT.Copy), hi_done)

            def ahead(name):
                hi(UNIT[name] + RING - 1)

            def done(name):
                act.wait_ge(tile_done, TILE[name] + 1)
                return pg[TILE[name] % 2][:]

            def free(ins, name):
                ins.then_inc(pg_free[TILE[name] % 2], 1)

            def px_ready(name):
                act.wait_ge(px_full, XUSE[name] + 1)

            def py_ready(name):
                act.wait_ge(py_full, YUSE[name] + 1)

            def split_hi(group, k, dst, src):
                act.wait_ge(src_done, SRC[group] + k + 1)
                put(act.activation(dst, src, ACT.Copy), xhi_done)

            def square(n, k, src):
                if k >= 2 and n == 5:
                    act.wait_ge(sq5_read, k - 1)
                elif k >= 2:
                    act.wait_ge(sq_read, (KT - 2) * (n - 1 if n < 5 else n - 2) + max(1, k - 2))
                elif n > 1:
                    act.wait_ge(px_full, XUSE[("stat", n - 1)] + 1)
                put(act.activation(sqr[:, k % 2], src, ACT.Square), sq_done)

            def ln_and_exp():
                act.preload_act_table_set("natural_log_exp_and_others")

            def inverse_root(n, dst, power=-0.5):
                if n > 1:
                    ln_and_exp()
                px_ready(("stat", n))
                act.activation(dst[:], px[:], ACT.Ln, bias=cc(C_EPS), scale=1.0 / D).then_inc(px_free, 1)
                px_read(act, ("stat", n))
                put(act.activation(dst[:], dst[:], ACT.Exp, scale=power), rstd_ready)

            ln_and_exp()
            for k in range(KT):
                act.wait_ge(x_landed[k // 2], 16)
                square(1, k, hid[:, k])
                if k == 5:
                    hi(0)
            act.wait_ge(c_landed, 16)
            inverse_root(1, rstd)
            for u in range(1, RING - 1):
                hi(u)
            for k in range(KT):
                split_hi("norm1", k, x_hi[:, k], nrm[:, k % 2])
            act.wait_ge(p_landed, 16)
            put(act.activation(lane[:, L_DT], pars("log_dt"), ACT.Exp), lane_act)
            px_ready("lam")
            act.activation(lam_t[:, 2:4], px[:, 0:2], ACT.Exp).then_inc(px_free, 1)
            act.wait_ge(lane_dve, 1)
            put(act.activation(lane[:, L_MAG], lane[:, L_Z], ACT.Exp), lane_act)
            put(act.activation(lane[:, L_TANH], lane[:, L_Z], ACT.Tanh, scale=0.5), lane_act)
            put(act.activation(lcf[:, 1], lcf[:, 0], ACT.Exp, scale=-1.0), lane_act)
            ahead(("u", 0))
            act.wait_ge(lane_dve, 2)
            put(act.activation(lane[:, L_S], lane[:, L_R], ACT.Sin, scale=0.5), lane_act)
            put(act.activation(lane[:, L_C], lane[:, L_R], ACT.Sin, scale=0.5, bias=cc(C_HPI)), lane_act)
            for t in range(SSM_T):
                if t > 0:
                    ahead(("u", t))
                a = done(("u", t))
                free(act.activation(hid[:, t], a, ACT.Copy), ("u", t))
            def gate(g):
                ahead(("gate", g))
                free(act.activation(gates[:, g], done(("gate", g)), ACT.Sigmoid), ("gate", g))

            def power(n):
                return lane[:, L_POW + 3 * n]

            def table(t, n):
                w = 64 << n
                if n == 0:
                    if t == 0:
                        act.wait_ge(lane_dve, 3)
                    if t >= 3:
                        act.wait_ge(out_mul, t - 2)
                        act.wait_ge(x_mul, t - 2)
                    put(act.activation(rot[:, t % 3, :, 0:64], powers[:, :, t], ACT.Copy), tab_act)
                if t > 0 or n > 0:
                    act.wait_ge(tab_dve, 3 * t + n)
                src = powers[:, :, t] if n == 0 else rot[:, t % 3, :, 0:w]
                if n > 0:
                    act.wait_ge(tab_act, 4 * t + 1)
                put(act.activation(rot_m[:, :, 0:w], src, ACT.Copy, scale=power(n)[:, t:t + 1]), tab_act)

            for g in range(GATES_FIRST):
                gate(g)
            for n in range(3):
                table(0, n)
            for t in range(LANE_T):
                if t + 1 < LANE_T:
                    for n in range(3):
                        table(t + 1, n)
                for g in GATE_AT[t]:
                    gate(g)
            for g in range(16 - GATES_LAST, 16):
                gate(g)
            act.wait_ge(ya_free, SSM_T)
            act.dma_start(rtab[:], rope).then_inc(r_landed, 16)
            for t in range(SSM_T):
                put(act.activation(y5[:, t], y5[:, t], ACT.Gelu_apprx_tanh), gelu_done)

            def exps(use, dst, w, i, negmax, sums):
                act.wait_ge(maxed, EXPS[use] + 1)
                bank = ps_ready(act, use)
                for c in range(2):
                    kw = {"accum_out": sums[:, i % 2, 2 + c:3 + c]} if sums is not None else {}
                    ins = act.activation(dst[:, c, 0:w], bank[:, c, 0:w], ACT.Exp, bias=negmax[:, i % 2, c:c + 1], **kw)
                    ins.then_inc(ps_free[SUSE[use] % 2] if c else act_c, 1)

            def exps1(h, i):
                if 4 * h + i >= 2:
                    act.wait_ge(combed, 4 * h + i - 1)
                exps(("s", h, i), pr[:, i % 2], P * (i + 1), i, soft, soft)

            def turned(h, i):
                w = P * (i + 1)
                bank = ps_ready(act, ("t", h, i))
                act.activation(pt[:, 0:i + 1, P * i:w], bank[:, 0, 0:w].rearrange("p (j q) -> p j q", q=P), ACT.Copy)\
                    .then_inc(ps_free[SUSE[("t", h, i)] % 2], 1)

            def kq_out(h, name, n, gain):
                ahead((name, h))
                a = done((name, h))
                if h > 0:
                    act.wait_ge(roped, 2 * h - 1 + n)
                act.activation(kq_sq[n], a, ACT.Square)
                free(act.activation(kq_raw[:, n], a, ACT.Copy, scale=par(gain)), (name, h))

            def head_root(use, n, eps, scale, ready):
                px_ready(use)
                act.activation(kq_rs[:, n], px[:], ACT.Ln, bias=cc(eps), scale=scale).then_inc(px_free, 1)
                px_read(act, use)
                put(act.activation(kq_rs[:, n], kq_rs[:, n], ACT.Exp, scale=-0.5), ready)

            def glu(m):
                if m % 2 == 0:
                    ahead(("glu", m // 2))
                a = done(("glu", m))
                if m >= 2:
                    act.wait_ge(src_done, SRC["s"] + m - 1)
                free(act.activation(sqr[:, m % 2], a, ACT.Sigmoid, bias=par("b_glu", m)), ("glu", m))

            ln_and_exp()
            for h in range(HEADS + 2):
                g = h - 1
                attends = 0 <= g < HEADS
                if h < HEADS:
                    kq_out(h, "k", 0, "kg")
                if attends:
                    px_ready(("vt", g))
                    act.activation(vv[:, g % 2], px[:].rearrange("p (j d) -> p j d", d=P), ACT.Copy).then_inc(px_free, 1)
                    exps1(g, 0)
                    exps1(g, 1)
                if h == HEADS:
                    act.wait_ge(tile_done, TILE[("v", HEADS - 1)] + 1)
                    for t in range(SSM_T):
                        act.wait_ge(gelu_done, t + 1)
                        put(act.activation(x_hi[:, t], y5[:, t], ACT.Copy), xhi_done)
                if h == HEADS + 1:
                    glu(2)
                if h >= 2:
                    py_ready(("pv", h - 2))
                    put(act.activation(kq_sq[2], py[:], ACT.Square), o_sq)
                    act.activation(hid[:, h - 2], py[:], ACT.Copy).then_inc(py_free, 1)
                if h < HEADS:
                    kq_out(h, "q", 1, "qg")
                if h == HEADS + 1:
                    glu(3)
                    for m in range(SSM_T):
                        split_hi("s", m, x_hi[:, 4 + m], y5[:, m])
                    ln_and_exp()
                if attends:
                    turned(g, 0)
                if h < HEADS:
                    head_root(("ssq_k", h), 0, C_EPS, 1.0 / 64, rs_k)
                if h >= 2:
                    if h >= 3:
                        act.wait_ge(o_done, h - 2)
                    head_root(("ssq_o", h - 2), 2, C_EPS, 1.0 / P, rs_o)
                if attends:
                    exps1(g, 2)
                    exps1(g, 3)
                if h < HEADS:
                    ahead(("v", h))
                    free(act.activation(v_raw[:], done(("v", h)), ACT.Copy), ("v", h))
                    head_root(("ssq_q", h), 1, C_EPS64, 1.0, rs_q)
                if h == HEADS:
                    glu(0)
                    glu(1)
                if attends:
                    turned(g, 2)

            for n in range(4):
                ahead(("ssm", n))
            act.wait_ge(tile_done, TILE[("ssm", KT - 1)] + 1)
            for h in range(HEADS):
                act.wait_ge(o_done, h + 1)
                put(act.activation(x_hi[:, h], hid[:, h], ACT.Copy), xhi_done)
            for m in range(KT):
                ahead(("attn", m))
                if m == 2:
                    act.wait_ge(xlo_done, SPLIT["o"] + KT)
                    act.dma_start(hid[:], x_dram).then_inc(x2_landed, 16)
                split_hi("mix", m, mix_hi[:, m], mix(m))
            for m in range(KT):
                ahead(("out", m))
                evacuated(act, ("out", m))
                square(2, m, hid[:, m])
                split_hi("norm2", m, x_hi[:, m], nrm[:, m % 2])
            inverse_root(2, rstd)
            order = ffn_order(FF1)
            for kind, c in order:
                a, b = chunks_of(FF1)[c]
                if kind == "up":
                    if c >= 2:
                        act.wait_ge(tile_done, TILE[("down", c - 2, KT - 1)] + 1)
                    for i in range(a, b):
                        for n, (name, col) in enumerate((("fgate", i), ("fval", FF1 + i))):
                            ahead((name, i))
                            evacuated(act, (name, i))
                            if i > 0 and n == 0:
                                act.wait_ge(src_done, SRC["act"] + i)
                            put(act.activation(cnv[:, n], cu[:, n], ACT.Identity, bias=par("cb", col),
                                               scale=par("cw", 88 + col)), cnv_act)
                            if n == 0 and i > a:
                                split_hi("act", i - 1, act_hi[:, c % 2, i - 1 - a], hsrc[:, (i - 1) % 2])
                        act.wait_ge(cnv_done, 2 * i + 1)
                        put(act.activation(cnv[:, 0], cnv[:, 0], ACT.Silu), silu_done)
                    split_hi("act", b - 1, act_hi[:, c % 2, b - 1 - a], hsrc[:, (b - 1) % 2])
                else:
                    for m in range(KT):
                        ahead(("down", c, m))
                        if (kind, c) == order[-1]:
                            evacuated(act, ("down", c, m))
                            square(3, m, hid[:, m])
                            split_hi("norm3", m, x_hi[:, m], nrm[:, m % 2])
            act.dma_start(lru_b[:], lru_w).then_inc(l_landed, 16)
            inverse_root(3, rstd)

            def lru_gate(t):
                px_ready(("rg", t))
                act.activation(ra[:, t], px[:], ACT.Sigmoid, bias=par("b_r", t)).then_inc(px_free, 1)
                py_ready(("ig", t))
                act.activation(ii[:, t], py[:], ACT.Sigmoid, bias=par("b_i", t)).then_inc(py_free, 1)

            for t in range(LRU_T):
                ahead(("xr", t))
                evacuated(act, ("xr", t))
                put(act.activation(xc[:, t], sqr[:, t % 2], ACT.Identity, bias=par("cb2", t),
                                   scale=par("cw2", 12 + t)), xc_act)
                if t > 0:
                    lru_gate(t - 1)

            def turned2(j, i):
                w = P * (i + 1)
                bank = ps_ready(act, ("t2", j, i))
                act.activation(pt2[:, i % 2, :, 0:i + 1, :], bank[:, :, 0:w].rearrange("p c (b q) -> p c b q", q=P), ACT.Copy)\
                    .then_inc(ps_free[SUSE[("t2", j, i)] % 2], 1)

            def exps2(j, i):
                n = 4 * j + i
                if n >= 2:
                    ps_ready(act, ("t2", (n - 2) // 4, (n - 2) % 4))
                exps(("p", j, i), pr2[:, i % 2], P * (i + 1), i, soft2, None)

            for j in range(PAIRS + 1):
                g = j - 1
                if j < PAIRS:
                    ahead(("k2", j))
                if j == 0:
                    lru_gate(LRU_T - 1)
                    for t in range(LRU_T):
                        px_read(act, ("rg", t))
                        put(act.activation(tt[:, t], ra[:, t], ACT.Tanh, scale=lcf[:, 6, t:t + 1]), act_c)
                        put(act.activation(ra[:, t], ra[:, t], ACT.Exp, scale=lcf[:, 7, t:t + 1]), la_done)
                if g >= 0:
                    if g == 0:
                        act.wait_ge(lru_h, LRU_T)
                    exps2(g, 0)
                    exps2(g, 1)
                ahead(("q2", j) if j < PAIRS else ("gr", 2))
                if g >= 0:
                    turned2(g, 0)
                    exps2(g, 2)
                    exps2(g, 3)
                ahead(("v2", j) if j < PAIRS else ("gr", 3))
                if j == 0:
                    for t in range(LRU_T):
                        act.wait_ge(tt_dve, t + 1)
                        put(act.activation(tt[:, t], tt[:, t], ACT.Sqrt), tt_act)
                if g >= 0:
                    turned2(g, 2)
                if 0 < j < 3:
                    ahead(("gr", g))
                for t in GR_AT[j]:
                    evacuated(act, ("gr", t))
                    put(act.activation(sqr[:, t % 2], sqr[:, t % 2], ACT.Gelu_apprx_tanh), gelu2_done)
                for t in GR_AT[j]:
                    split_hi("rec", t, mx2_hi[:, 4 + t], nrm[:, t % 2])
                if g >= 0:
                    py_ready(("pv2", g))
                    put(act.activation(mx2_hi[:, g], py[:], ACT.Copy), pv2_hi)
                if j < PAIRS:
                    px_ready(("vt2", j))
                    act.activation(vv2[:], px[:].rearrange("p (b d) -> p b d", d=P), ACT.Copy).then_inc(px_free, 1)
            for m in range(KT):
                ahead(("out2", m))
                a = done(("out2", m))
                square(4, m, a)
                free(act.activation(acc[:, m], a, ACT.Copy), ("out2", m))
            inverse_root(4, rstd)
            for k in range(KT):
                act.wait_ge(res_done, k + 1)
                if k >= 2:
                    act.wait_ge(xlo_done, SPLIT["norm4"] + k - 1)
                put(act.activation(nrm[:, k % 2], hid[:, k], ACT.Copy, scale=par("mlp_pre", k)), gained)
                square(5, k, hid[:, k])
                act.wait_ge(gained, k + 1)
                put(act.activation(x_hi[:, k], nrm[:, k % 2], ACT.Copy), xhi_done)
            inverse_root(5, rstd_sq, -1.0)
            order = ffn_order(FF2)
            for kind, c in order:
                a, b = chunks_of(FF2)[c]
                if kind == "up":
                    if c >= 2:
                        act.wait_ge(tile_done, TILE[("down2", c - 2, KT - 1)] + 1)
                    for i in range(a, b):
                        ahead(("ff", i))
                        a_ff = done(("ff", i))
                        if i > 0:
                            act.wait_ge(src_done, SRC["act2"] + i)
                        free(act.activation(rel[:], a_ff, ACT.Relu), ("ff", i))
                        split_hi("act2", i, act2_hi[:, c % 2, i - a], nrm[:, i % 2])
                else:
                    for m in range(KT):
                        ahead(("down2", c, m))
                        if c == 0:
                            free(act.activation(acc[:, m], done(("down2", c, m)), ACT.Copy), ("down2", c, m))
                        if (kind, c) == order[-1]:
                            act.wait_ge(acc_done, m + 1)
                            square(6, m, acc[:, m])
            inverse_root(6, rstd)

        @block.vector
        def _(dve):
            sent = {}

            def put(ins, s):
                ins.then_inc(s, 1)
                sent[s.name] = sent.get(s.name, 0) + 1
                dve.wait_ge(s, sent[s.name])

            def link(ins):
                put(ins, dve_c)

            def done(name):
                dve.wait_ge(tile_done, TILE[name] + 1)
                return pg[TILE[name] % 2][:]

            def free(ins, name):
                ins.then_inc(pg_free[TILE[name] % 2], 1)
                evacuated(dve, name)

            def tt_(out_, a, b, op=ALU.mult):
                return dve.tensor_tensor(out_, a, b, op)

            def stt(out_, a, s, b, op0=ALU.mult, op1=ALU.mult):
                return dve.scalar_tensor_tensor(out_, a, s, b, op0, op1)

            def ts(out_, a, s1, op0, s2=None, op1=ALU.bypass):
                return dve.tensor_scalar(out_, a, s1, s2, op0, op1)

            def split_lo(n, dst, src, hi_):
                dve.wait_ge(xhi_done, n + 1)
                put(tt_(dst, src, hi_.bitcast(F32), ALU.subtract), xlo_done)

            def root_ready(n):
                dve.wait_ge(rstd_ready, n)

            def add_squares(n, k):
                if 1 <= k < KT - 1:
                    dve.wait_ge(sq_done, KT * (n - 1) + k + 1)
                    put(tt_(sq_sum[:], sqr[:, 0] if k == 1 else sq_sum[:], sqr[:, k % 2], ALU.add), sq_read)

            def scaled(group, m, gain, last=KT - 1):
                put(ts(nrm[:, m % 2], hid[:, m], par(gain, m), ALU.mult), src_done)
                for k in ([m - 1] if m > 0 else []) + ([m] if m == last else []):
                    split_lo(SPLIT[group] + k, x_lo[:, k], nrm[:, k % 2], x_hi[:, k])

            for k in range(KT):
                add_squares(1, k)
            dve.wait_ge(p_landed, 16)
            lam4 = pars("lam")
            tt_(lam_t[:, 0:1], lam4[:, 0:1], lam4[:, 1:2])
            put(tt_(lam_t[:, 1:2], lam4[:, 2:3], lam4[:, 3:4]), lam_dve)
            root_ready(1)
            for k in range(KT + 1):
                if k < KT:
                    put(stt(nrm[:, k % 2], hid[:, k], par("norm1", k), rstd[:]), src_done)
                if k > 0:
                    split_lo(SPLIT["norm1"] + k - 1, x_lo[:, k - 1], nrm[:, (k - 1) % 2], x_hi[:, k - 1])

            dve.wait_ge(m_landed, 16)
            link(dve.tensor_copy(msk[:], msk_raw))

            def L(i):
                return lane[:, i]

            dve.wait_ge(lane_act, 1)
            tt_(L(L_TH), pars("a_im"), L(L_DT))
            link(ts(lcf[:, 0], pars("lru"), -1.0, ALU.mult))
            link(tt_(lcf[:, 0], lcf[:, 0], pars("lru"), ALU.max))
            put(tt_(L(L_Z), pars("a_re"), L(L_DT)), lane_dve)
            dve.wait_ge(lane_dve, 1)
            link(ts(L(L_N), L(L_TH), 1.0 / TWO_PI, ALU.mult, BIG, ALU.add))
            link(ts(L(L_N), L(L_N), BIG, ALU.subtract))
            link(stt(L(L_R), L(L_N), -PI_1, L(L_TH), ALU.mult, ALU.add))
            link(stt(L(L_R), L(L_N), -PI_2, L(L_R), ALU.mult, ALU.add))
            link(stt(L(L_R), L(L_N), -PI_3, L(L_R), ALU.mult, ALU.add))
            put(ts(L(L_R), L(L_R), 3.1415925, ALU.min, -3.1415925, ALU.max), lane_dve)
            px_read(dve, "lam")
            link(tt_(lam_t[:, 4:5], lam_t[:, 3:4], lam_t[:, 2:3], ALU.subtract))
            link(ts(lam_t[:, 5:6], lam_t[:, 4:5], -LAM_INIT, ALU.add))
            link(ts(lam_t[:, 6:7], par("subln"), 1.0 - LAM_INIT, ALU.mult))
            dve.wait_ge(lane_act, 4)
            link(ts(lcf[:, 2], lcf[:, 1], 2.0, ALU.add))
            link(dve.reciprocal(lcf[:, 2], lcf[:, 2]))
            link(tt_(lcf[:, 2], lcf[:, 2], lcf[:, 1]))
            link(tt_(lcf[:, 3], lcf[:, 2], lcf[:, 2]))
            link(ts(lcf[:, 4], lcf[:, 3], 1.0 / 17, ALU.mult))
            for n in (15, 13, 11, 9, 7, 5, 3):
                link(stt(lcf[:, 4], lcf[:, 4], 1.0 / n, lcf[:, 3], ALU.add, ALU.mult))
            link(stt(lcf[:, 4], lcf[:, 4], 1.0, lcf[:, 2], ALU.add, ALU.mult))
            link(ts(lcf[:, 5], pars("lru"), -1.0, ALU.mult, 0.0, ALU.max))
            link(stt(lcf[:, 5], lcf[:, 4], 2.0, lcf[:, 5], ALU.mult, ALU.add))
            link(ts(lcf[:, 6], lcf[:, 5], 8.0, ALU.mult))
            link(ts(lcf[:, 7], lcf[:, 5], -8.0, ALU.mult))
            dve.wait_ge(lane_act, 6)
            link(tt_(L(L_T1), L(L_S), L(L_C)))
            link(ts(L(L_SIN), L(L_T1), 2.0, ALU.mult))
            link(tt_(L(L_T2), L(L_S), L(L_S)))
            link(ts(L(L_CM1), L(L_T2), -2.0, ALU.mult))
            link(ts(L(L_COS), L(L_CM1), 1.0, ALU.add))
            link(stt(L(L_T1), L(L_MAG), 1.0, L(L_TANH), ALU.add, ALU.mult))
            link(tt_(L(L_T1), L(L_T1), L(L_COS)))
            link(tt_(L(L_NR), L(L_T1), L(L_CM1), ALU.add))
            link(tt_(L(L_NI), L(L_MAG), L(L_SIN)))
            link(tt_(L(L_T1), pars("a_re"), pars("a_re")))
            link(tt_(L(L_T2), pars("a_im"), pars("a_im")))
            link(tt_(L(L_T1), L(L_T1), L(L_T2), ALU.add))
            link(dve.reciprocal(L(L_T3), L(L_T1)))
            link(tt_(L(L_T1), L(L_NR), pars("a_re")))
            link(tt_(L(L_T2), L(L_NI), pars("a_im")))
            link(tt_(L(L_T1), L(L_T1), L(L_T2), ALU.add))
            link(tt_(L(L_CR), L(L_T1), L(L_T3)))
            link(tt_(L(L_T1), L(L_NI), pars("a_re")))
            link(tt_(L(L_T2), L(L_NR), pars("a_im")))
            link(tt_(L(L_T1), L(L_T1), L(L_T2), ALU.subtract))
            link(tt_(L(L_CI), L(L_T1), L(L_T3)))
            dve.wait_ge(s_landed, 32)

            def wide(i):
                return lane[:, i, :].rearrange("p (t o) -> p t o", o=1).broadcast_to([P, LANE_T, 32])

            def c3(a):
                return a.rearrange("p (t c) -> p t c", c=32)

            tmp0, tmp1 = nrm[:, 0], nrm[:, 1]
            tt_(c3(c_out[:, 0]), c3(c_in[:, 0]), wide(L_CR))
            link(tt_(c3(tmp0), c3(c_in[:, 1]), wide(L_CI)))
            tt_(c3(c_out[:, 1]), c3(c_in[:, 0]), wide(L_CI))
            link(tt_(c3(tmp1), c3(c_in[:, 1]), wide(L_CR)))
            link(tt_(c_out[:, 0], c_out[:, 0], tmp0, ALU.subtract))
            link(stt(c_out[:, 1], c_out[:, 1], -1.0, tmp1, ALU.mult, ALU.subtract))
            pc, pn = L_COS, L_SIN
            free_rows = [(L_T1, L_T2), (L_NR, L_NI)]
            dve.memset(powers[:, 0, :, 0:1], 1.0)
            link(dve.memset(powers[:, 1, :, 0:1], 0.0))
            for k in range(8):
                n = 1 << k
                qc, qn = (L_POW + 3 * (k - 5), L_POW + 3 * (k - 5) + 1) if k >= 5 else free_rows[k % 2]
                if n < 64:
                    def pw(i):
                        return lane[:, i, :].rearrange("p (t o) -> p t o", o=1).broadcast_to([P, LANE_T, n])

                    old_c, old_s = powers[:, 0, :, 0:n], powers[:, 1, :, 0:n]
                    new_c, new_s = powers[:, 0, :, n:2 * n], powers[:, 1, :, n:2 * n]
                    t0 = nrm[:, 0, 0:LANE_T * n].rearrange("p (t n) -> p t n", n=n)
                    t1 = nrm[:, 1, 0:LANE_T * n].rearrange("p (t n) -> p t n", n=n)
                    tt_(new_c, old_c, pw(pc))
                    tt_(t0, old_s, pw(pn))
                    tt_(new_s, old_s, pw(pc))
                    tt_(t1, old_c, pw(pn))
                tt_(L(qc), L(pc), L(pc))
                tt_(L(L_T3), L(pn), L(pn))
                link(tt_(L(qn), L(pc), L(pn)))
                if n < 64:
                    tt_(new_c, new_c, t0, ALU.subtract)
                    tt_(new_s, new_s, t1, ALU.add)
                tt_(L(qc), L(qc), L(L_T3), ALU.subtract)
                link(ts(L(qn), L(qn), 2.0, ALU.mult))
                if k >= 5:
                    link(ts(L(qn + 1), L(qn), -1.0, ALU.mult))
                pc, pn = qc, qn
            put(dve.tensor_copy(L(L_T3), L(pc)), lane_dve)

            def table(t, n):
                w = 64 << n
                row = L_POW + 3 * n
                r = rot[:, t % 3]
                old = powers[:, :, t] if n == 0 else r[:, :, 0:w]
                dve.wait_ge(tab_act, 4 * t + n + 2)
                stt(r[:, 0, w:2 * w], old[:, 1], lane[:, row + 2, t:t + 1], rot_m[:, 0, 0:w], ALU.mult, ALU.add)
                put(stt(r[:, 1, w:2 * w], old[:, 0], lane[:, row + 1, t:t + 1], rot_m[:, 1, 0:w], ALU.mult, ALU.add), tab_dve)

            def channels_out(k):
                dve.wait_ge(y_mm, 4 * k + 4)
                put(stt(y5[:, k], hid[:, k], par("ssm_d", k), ps[k % 2][:, 0, :], ALU.mult, ALU.add), ya_free)

            for n in range(3):
                table(0, n)
            for t in range(LANE_T + 1):
                v = vz[:, t % 2]
                if t < LANE_T:
                    co, si = rot[:, t % 3, 0], rot[:, t % 3, 1]
                    dve.wait_ge(px_full, XUSE[("br", t)] + 1)
                    if t >= 2:
                        dve.wait_ge(x_mul, t - 1)
                    tt_(v[:, 0], px[:], co)
                    tt_(v_m[:, 1], px[:], si).then_inc(px_free, 1)
                    dve.wait_ge(py_full, YUSE[("bi", t)] + 1)
                    tt_(v_m[:, 0], py[:], si)
                    tt_(v[:, 1], py[:], co).then_inc(py_free, 1)
                if t + 1 < LANE_T:
                    table(t + 1, 0)
                if t > 0:
                    if t >= 3:
                        dve.wait_ge(y_mm, t - 2)
                    z, x2 = vz[:, (t - 1) % 2], xs[:, (t - 1) % 2]
                    co, si = rot[:, (t - 1) % 3, 0], rot[:, (t - 1) % 3, 1]
                    tt_(x2[:, 0], z[:, 0], co)
                    put(stt(x2[:, 1], z[:, 1], -1.0, si), out_mul)
                if t + 1 < LANE_T:
                    table(t + 1, 1)
                if t < LANE_T:
                    dve.wait_ge(in_add, 2 * t + 2)
                    mag = lane[:, L_MAG, t:t + 1].broadcast_to([P, T])
                    dve.tensor_tensor_scan(v[:, 0], mag, v[:, 0], 0.0, ALU.mult, ALU.add)
                    put(dve.tensor_tensor_scan(v[:, 1], mag, v[:, 1], 0.0, ALU.mult, ALU.add), scanned)
                if t + 1 < LANE_T:
                    table(t + 1, 2)
                if t % 4 == 1 and t > 1:
                    channels_out(t // 4 - 1)
            channels_out(SSM_T - 1)

            def maximum(use, w, i, s):
                bank = ps_ready(dve, use)
                put(dve.tensor_reduce(s[:, i % 2, 0:2], bank[:, :, 0:w], AX.X, ALU.max, negate=True), maxed)

            def combine(h, i):
                w, s = P * (i + 1), soft[:, i % 2]
                ps_read(dve, ("s", h, i))
                link(dve.reciprocal(s[:, 4:6], s[:, 2:4]))
                link(ts(s[:, 5:6], s[:, 5:6], lam_t[:, 5:6], ALU.mult))
                link(ts(pr[:, i % 2, 1, 0:w], pr[:, i % 2, 1, 0:w], s[:, 5:6], ALU.mult))
                n = 4 * h + i
                if n >= 2:
                    ps_ready(dve, ("t", (n - 2) // 4, (n - 2) % 4))
                put(stt(pa[:, i % 2, 0:w], pr[:, i % 2, 0, 0:w], s[:, 4:5], pr[:, i % 2, 1, 0:w], ALU.mult, ALU.add), combed)

            def turned(h, i):
                w = P * (i + 1)
                bank = ps_ready(dve, ("t", h, i))
                dve.tensor_copy(pt[:, 0:i + 1, P * i:w], bank[:, 0, 0:w].rearrange("p (j q) -> p j q", q=P))\
                    .then_inc(ps_free[SUSE[("t", h, i)] % 2], 1)
                ps_read(dve, ("t", h, i))

            def rope_step(h, name, n, ready, dst):
                evacuated(dve, (name, h))
                tt_(rope_a[:, 0], kq_raw[:, n], rtab[:, 0])
                dve.wait_ge(py_full, YUSE[("rot_" + name, h)] + 1)
                tt_(rope_a[:, 1], py[:], rtab[:, 1]).then_inc(py_free, 1)
                py_read(dve, ("rot_" + name, h))
                link(tt_(rope_a[:, 0], rope_a[:, 0], rope_a[:, 1], ALU.add))
                dve.wait_ge(ready, h + 1)
                put(tt_(dst[:, h % 2], rope_a[:, 0], kq_rs[:, n]), roped)

            dve.wait_ge(r_landed, 16)
            for h in range(HEADS + 2):
                g = h - 1
                attends = 0 <= g < HEADS
                if attends:
                    maximum(("s", g, 0), P, 0, soft)
                    maximum(("s", g, 1), 2 * P, 1, soft)
                    combine(g, 0)
                    combine(g, 1)
                if h == HEADS:
                    for t in range(SSM_T):
                        split_lo(SPLIT["g"] + t, x_lo[:, t], y5[:, t], x_hi[:, t])
                if h == HEADS + 1:
                    for m in range(SSM_T):
                        evacuated(dve, ("glu", m))
                        put(tt_(y5[:, m], y5[:, m], sqr[:, m % 2]), src_done)
                    for m in range(SSM_T):
                        split_lo(SPLIT["s"] + m, x_lo[:, 4 + m], y5[:, m], x_hi[:, 4 + m])
                if attends:
                    turned(g, 1)
                if h >= 2:
                    py_read(dve, ("pv", h - 2))
                    dve.wait_ge(rs_o, h - 1)
                    put(stt(hid[:, h - 2], hid[:, h - 2], lam_t[:, 6:7], kq_rs[:, 2]), o_done)
                if attends:
                    maximum(("s", g, 2), 3 * P, 2, soft)
                    maximum(("s", g, 3), 4 * P, 3, soft)
                if h < HEADS:
                    rope_step(h, "k", 0, rs_k, kk)
                if attends:
                    combine(g, 2)
                    combine(g, 3)
                if h < HEADS:
                    rope_step(h, "q", 1, rs_q, qq)
                if attends:
                    turned(g, 3)

            for m in range(KT):
                free(tt_(mix(m), done(("ssm", m)), gates[:, 8 + m]), ("ssm", m))
            for h in range(HEADS):
                split_lo(SPLIT["o"] + h, x_lo[:, h], hid[:, h], x_hi[:, h])
            for m in range(KT + 1):
                if m < KT:
                    free(tt_(nrm[:, m % 2], done(("attn", m)), gates[:, m]), ("attn", m))
                    evacuated(dve, ("attn", m))
                    put(tt_(mix(m), mix(m), nrm[:, m % 2], ALU.add), src_done)
                if m > 0:
                    split_lo(SPLIT["mix"] + m - 1, mix_lo[:, m - 1], mix(m - 1), mix_hi[:, m - 1])
            dve.wait_ge(x2_landed, 16)
            for m in range(KT):
                free(tt_(hid[:, m], hid[:, m], done(("out", m)), ALU.add), ("out", m))
                add_squares(2, m - 1)
                scaled("norm2", m, "norm2")
            root_ready(2)

            order = ffn_order(FF1)
            for kind, c in order:
                a, b = chunks_of(FF1)[c]
                if kind == "up":
                    for i in range(a, b):
                        for n, (name, col) in enumerate((("fgate", i), ("fval", FF1 + i))):
                            free(tt_(cu[:, n], done((name, i)), rstd[:]), (name, i))
                            if n == 0 and i > a:
                                split_lo(SPLIT["act"] + i - 1, act_lo[:, c % 2, i - 1 - a], hsrc[:, (i - 1) % 2],
                                         act_hi[:, c % 2, i - 1 - a])
                            dve.wait_ge(cnv_act, 2 * i + n + 1)
                            link(stt(cnv[:, n, 1:T], cu[:, n, 0:T - 1], par("cw", 44 + col), cnv[:, n, 1:T], ALU.mult, ALU.add))
                            put(stt(cnv[:, n, 2:T], cu[:, n, 0:T - 2], par("cw", col), cnv[:, n, 2:T], ALU.mult, ALU.add),
                                cnv_done)
                        dve.wait_ge(silu_done, i + 1)
                        put(tt_(hsrc[:, i % 2], cnv[:, 0], cnv[:, 1]), src_done)
                    split_lo(SPLIT["act"] + b - 1, act_lo[:, c % 2, b - 1 - a], hsrc[:, (b - 1) % 2],
                             act_hi[:, c % 2, b - 1 - a])
                else:
                    for m in range(KT):
                        if c > 0:
                            evacuated(dve, ("down", c - 1, m))
                        free(tt_(hid[:, m], hid[:, m], done(("down", c, m)), ALU.add), ("down", c, m))
                        if (kind, c) == order[-1]:
                            add_squares(3, m - 1)
                            scaled("norm3", m, "mix_pre")
            root_ready(3)

            for t in range(LRU_T):
                free(tt_(sqr[:, t % 2], done(("xr", t)), rstd[:]), ("xr", t))
                dve.wait_ge(xc_act, t + 1)
                for d in (1, 2, 3):
                    put(stt(xc[:, t, d:T], sqr[:, t % 2, 0:T - d], par("cw2", 4 * (3 - d) + t), xc[:, t, d:T], ALU.mult,
                            ALU.add), xc_done)

            def lru_factor(t):
                dve.wait_ge(la_done, t + 1)
                link(tt_(nrm[:, t % 2], ra[:, t], ra[:, t]))
                put(stt(tt[:, t], nrm[:, t % 2], 1.0, tt[:, t], ALU.add, ALU.mult), tt_dve)
                py_read(dve, ("ig", t))
                link(tt_(ii[:, t], ii[:, t], xc[:, t]))

            def recurrence(t):
                dve.wait_ge(tt_act, t + 1)
                link(tt_(ii[:, t], ii[:, t], tt[:, t]))
                put(dve.tensor_tensor_scan(xc[:, t], ra[:, t], ii[:, t], 0.0, ALU.mult, ALU.add), lru_h)

            free(tt_(kk2[:, 0], done(("k2", 0)), rstd[:]), ("k2", 0))
            lru_factor(0)
            lru_factor(1)
            free(stt(qq2[:, 0], done(("q2", 0)), 0.125, rstd[:]), ("q2", 0))
            lru_factor(2)
            lru_factor(3)
            free(tt_(v_raw2[:], done(("v2", 0)), rstd[:]), ("v2", 0))
            for t in range(3):
                recurrence(t)
            free(tt_(kk2[:, 1], done(("k2", 1)), rstd[:]), ("k2", 1))
            recurrence(3)

            def combine2(j, i):
                w, s = P * (i + 1), soft2[:, i % 2]
                ps_read(dve, ("p", j, i))
                for c in range(2):
                    link(dve.tensor_tensor_reduce(pr2[:, i % 2, c, 0:w], pr2[:, i % 2, c, 0:w], mult[:, T - w:T], 1.0, 0.0,
                                                  ALU.mult, ALU.add, s[:, 2 + c:3 + c]))
                link(dve.reciprocal(s[:, 4:6], s[:, 2:4]))
                ts(pr2[:, i % 2, 0, 0:w], pr2[:, i % 2, 0, 0:w], s[:, 4:5], ALU.mult)
                put(ts(pr2[:, i % 2, 1, 0:w], pr2[:, i % 2, 1, 0:w], s[:, 5:6], ALU.mult), combed)

            def turned2(j, i):
                w = P * (i + 1)
                bank = ps_ready(dve, ("t2", j, i))
                dve.tensor_copy(pt2[:, i % 2, :, 0:i + 1, :], bank[:, :, 0:w].rearrange("p c (b q) -> p c b q", q=P))\
                    .then_inc(ps_free[SUSE[("t2", j, i)] % 2], 1)
                ps_read(dve, ("t2", j, i))

            def gr_out(t):
                free(tt_(sqr[:, t % 2], done(("gr", t)), rstd[:]), ("gr", t))

            for j in range(1, PAIRS + 1):
                g = j - 1
                if 1 < j < PAIRS:
                    free(tt_(kk2[:, j % 2], done(("k2", j)), rstd[:]), ("k2", j))
                if g >= 0:
                    maximum(("p", g, 0), P, 0, soft2)
                    maximum(("p", g, 1), 2 * P, 1, soft2)
                    combine2(g, 0)
                    combine2(g, 1)
                if 0 < j < PAIRS:
                    free(stt(qq2[:, j % 2], done(("q2", j)), 0.125, rstd[:]), ("q2", j))
                if g >= 0:
                    turned2(g, 1)
                    if j == PAIRS:
                        gr_out(2)
                    maximum(("p", g, 2), 3 * P, 2, soft2)
                    maximum(("p", g, 3), 4 * P, 3, soft2)
                    combine2(g, 2)
                    combine2(g, 3)
                if j < PAIRS:
                    free(tt_(v_raw2[:], done(("v2", j)), rstd[:]), ("v2", j))
                if g >= 0:
                    turned2(g, 3)
                for t in GR_AT[j]:
                    if t != 2:
                        gr_out(t)
                for t in GR_AT[j]:
                    dve.wait_ge(gelu2_done, t + 1)
                    put(tt_(nrm[:, t % 2], xc[:, t], sqr[:, t % 2]), src_done)
                for t in GR_AT[j]:
                    split_lo(SPLIT["rec"] + t, mx2_lo[:, 4 + t], nrm[:, t % 2], mx2_hi[:, 4 + t])
                if g >= 0:
                    dve.wait_ge(pv2_hi, g + 1)
                    tt_(mx2_lo[:, g], py[:], mx2_hi[:, g].bitcast(F32), ALU.subtract).then_inc(py_free, 1)
                    py_read(dve, ("pv2", g))

            for m in range(KT):
                add_squares(4, m)
            root_ready(4)
            for m in range(KT):
                link(stt(nrm_t[:], acc[:, m], par("mix_post", m), rstd[:]))
                put(tt_(hid[:, m], hid[:, m], nrm_t[:], ALU.add), res_done)
                if m > 0:
                    split_lo(SPLIT["norm4"] + m - 1, x_lo[:, m - 1], nrm[:, (m - 1) % 2], x_hi[:, m - 1])
            split_lo(SPLIT["norm4"] + KT - 1, x_lo[:, KT - 1], nrm[:, (KT - 1) % 2], x_hi[:, KT - 1])
            order = ffn_order(FF2)
            for kind, c in order:
                a, b = chunks_of(FF2)[c]
                if kind == "up":
                    for i in range(a, b):
                        evacuated(dve, ("ff", i))
                        put(tt_(nrm[:, i % 2], rel[:], rel[:]), src_done)
                        split_lo(SPLIT["act2"] + i, act2_lo[:, c % 2, i - a], nrm[:, i % 2], act2_hi[:, c % 2, i - a])
                elif c > 0:
                    for m in range(KT):
                        evacuated(dve, ("down2", c - 1, m))
                        free(tt_(acc[:, m], acc[:, m], done(("down2", c, m)), ALU.add), ("down2", c, m))
                        if (kind, c) == order[-1]:
                            if m == 0:
                                root_ready(5)
                            put(tt_(acc[:, m], acc[:, m], rstd_sq[:]), acc_done)
                            add_squares(6, m - 1)
            root_ready(6)
            for m in range(KT):
                put(stt(acc[:, m], acc[:, m], par("mlp_post", m), rstd[:]), fin_mul)
                if m % 2 == 0:
                    put(tt_(hid[:, m], hid[:, m], acc[:, m], ALU.add), fin_done)


def _units(i):
    import numpy as np

    def tiles(w, m):
        return w[:, m * P:(m + 1) * P].reshape(-1, P, P).transpose(1, 0, 2)

    w_in, w_up, w_down = i["w_in"][0], i["w_up"][0], i["w_down"][0]
    w_in2, f_in, f_out = i["w_in_2"][0], i["w_ff_in_2"][0], i["w_ff_out_2"][0]

    def piece(name):
        kind, n = name[0], name[1]
        if kind in ("glu", "ssm"):
            w = i["w_glu"][0] if kind == "glu" else i["w_ssm_proj"][0]
            return np.concatenate([tiles(w, 2 * n), tiles(w, 2 * n + 1)], axis=1)
        if kind in ("down", "down2"):
            a, b = chunks_of(FF1 if kind == "down" else FF2)[n]
            w = (w_down if kind == "down" else f_out)[a * P:b * P]
            return tiles(w, name[2])
        w, m = {"q": (w_in, n), "k": (w_in, 8 + n), "v": (w_in, 16 + n), "u": (w_in, 24 + n), "gate": (w_in, 28 + n),
                "attn": (i["w_attn_proj"][0], n), "out": (i["w_out"][0], n), "fgate": (w_up, n),
                "fval": (w_up, FF1 + n), "q2": (w_in2, n), "k2": (w_in2, 4 + n), "v2": (w_in2, 8 + n),
                "xr": (w_in2, 12 + n), "gr": (w_in2, 16 + n), "out2": (i["w_out_2"][0], n), "ff": (f_in, n)}[kind]
        return tiles(w, m)

    out = np.zeros((len(UNITS), P, KT * P), np.float32)
    for n, name in enumerate(UNITS):
        p = piece(name)
        out[n, :, :p.shape[1] * P] = p.reshape(P, -1)
    return out


def _constants():
    import numpy as np

    c = np.zeros((P, N_CONST), np.float32)
    c[:, C_ID:C_ID + P] = np.eye(P)
    c[:, C_ONES:C_ONES + P] = 1
    c[:64, C_BLK:C_BLK + 64] = 1
    c[64:, C_BLK + 64:C_BLK + 128] = 1
    for b in (0, 64):
        for d in range(32):
            c[b + d + 32, C_ROT + b + d] = -1
            c[b + d, C_ROT + b + d + 32] = 1
    q, k = np.arange(P)[:, None], np.arange(T)[None, :]
    dist = q + (T - P) - k
    count = ((dist >= 0) & (dist <= 128)).astype(int) + ((dist >= 0) & (dist % 4 == 0)) + ((dist >= 0) & (dist % 16 == 0))
    c[:, C_MULT:C_MULT + T] = count
    c[:, C_EPS], c[:, C_EPS64], c[:, C_HPI] = EPS, 64 * EPS, np.pi / 2
    m = np.zeros((P, N_MASK), np.float32)
    m[:, M_ID:M_ID + P] = np.eye(P)
    m[:, M_TRI:M_TRI + P] = np.where(np.arange(P)[None, :] <= q, 0, -1e30)
    m[:, M_UNI:M_UNI + T] = np.where(count > 0, 0, -1e30)
    inv = (1.0 / (10000.0 ** (np.arange(0, 64, 2, dtype=np.float32) / 64))).astype(np.float32)
    ang = (np.arange(T, dtype=np.float32)[None, :] * inv[:, None]).astype(np.float32)
    rope = np.stack([np.tile(np.cos(ang.astype(np.float64)), (4, 1)), np.tile(np.sin(ang.astype(np.float64)), (4, 1))], axis=1)
    return c, m, rope.astype(np.float32)


def _parameters(i):
    import numpy as np

    def cols(a):
        return np.asarray(a).reshape(-1, P).T

    def lanes(a):
        return np.asarray(a).reshape(LANE_T, P).T

    lam = np.zeros((P, 4), np.float32)
    for n, name in enumerate(("lambda_q1", "lambda_k1", "lambda_q2", "lambda_k2")):
        lam[:64, n] = i[name][0]
    parts = {
        "norm1": cols(i["norm1_gain"][0]), "norm2": cols(i["norm2_gain"][0]),
        "mix_pre": cols(i["mix_norm_pre_2"][0]), "mix_post": cols(i["mix_norm_post_2"][0]),
        "mlp_pre": cols(i["mlp_norm_pre_2"][0]), "mlp_post": cols(i["mlp_norm_post_2"][0]),
        "qg": cols(np.tile(i["q_norm_gain"][0], 2)), "kg": cols(np.tile(i["k_norm_gain"][0], 2)),
        "subln": cols(i["subln_gain"][0]), "lam": lam,
        "cw": np.concatenate([cols(i["conv_w"][0][j]) for j in range(3)], axis=1), "cb": cols(i["conv_b"][0]),
        "b_glu": cols(i["b_glu"][0]), "ssm_d": cols(i["ssm_d"][0]),
        "a_re": lanes(i["ssm_a_re"][0]), "a_im": lanes(i["ssm_a_im"][0]),
        "log_dt": lanes(np.repeat(i["ssm_log_dt"][0], 64)),
        "cw2": np.concatenate([cols(i["conv_w_2"][0][j]) for j in range(4)], axis=1), "cb2": cols(i["conv_b_2"][0]),
        "b_r": cols(i["b_rgate_2"][0]), "b_i": cols(i["b_igate_2"][0]), "lru": cols(i["lru_lambda_2"][0]),
    }
    out = np.zeros((P, N_PARAM), np.float32)
    for name, (a, w) in PARAMS.items():
        out[:, a:a + w] = parts[name]
    b = np.zeros((P, SSM_T, 2, P), np.float32)
    c = np.zeros((P, 2, LANE_T, 32), np.float32)
    for n, (bn, cn) in enumerate((("ssm_b_re", "ssm_c_re"), ("ssm_b_im", "ssm_c_im"))):
        for g in range(32):
            h = g % 2
            b[16 * (g % 8):16 * (g % 8) + 16, g // 8, n, 64 * h:64 * h + 64] = i[bn][0][g].T
            c[64 * h:64 * h + 64, n, g // 2, 16 * h:16 * h + 16] = i[cn][0][g].T
    lru = np.zeros((P, 2, LRU_T, P), np.float32)
    for n, name in enumerate(("w_rgate_2", "w_igate_2")):
        for k in range(8):
            h = k % 2
            lru[64 * h:64 * h + 64, n, k // 2, 64 * h:64 * h + 64] = i[name][0][k]
    return out, b, c.reshape(P, 2, LANE_T * 32), lru


def kernel(**inputs):
    import concourse.bacc as _bacc
    import numpy as _np
    from concourse.bass_utils import run_bass_kernel_spmd as _run

    i = {n: _np.asarray(a) for n, a in inputs.items()}
    consts, masks, rope = _constants()
    params, ssm_b, ssm_c, lru = _parameters(i)
    arrays = {
        "weights": _units(i), "x": _np.ascontiguousarray(i["x"][0].T.reshape(KT, P, T).transpose(1, 0, 2)),
        "consts": consts, "rope": rope, "masks": masks, "params": params, "ssm_b": ssm_b, "ssm_c": ssm_c, "lru_w": lru,
    }
    nc = _bacc.Bacc("TRN2", target_bir_lowering=False, num_devices=1)
    args = [nc.dram_tensor(n, a.shape, mybir.dt.from_np(a.dtype), kind="ExternalInput").ap() for n, a in arrays.items()]
    args.append(nc.dram_tensor("out", (P, KT, T), F32, kind="ExternalOutput").ap())
    build(nc, *args)
    got = _run(nc, [arrays], core_ids=[0]).results[0]["out"]
    return got.transpose(1, 0, 2).reshape(D, T).T[None]
```
